# Optimizing a Trainium2 kernel written in Bass

```python
import jax, jax.numpy as jnp
from jax import lax
import numpy as np
import math

D_MODEL = 2048
BATCH = 1
SEQ = 256
DEPTH = 1

CHUNK = 64
PLE_DIM = 256
DN_HEADS = 16
DN_HEAD_DIM = 128
DN_WIDTH = DN_HEADS * DN_HEAD_DIM
SHORT_CONV = 4
CONV_CH = D_MODEL
CONV_KERNEL = 31
N_BRANCHES = 2
EPS = 1e-6
IN_SIZES = (3 * DN_WIDTH,
            DN_WIDTH,
            DN_HEADS,
            DN_HEADS,
            2 * CONV_CH,
            CONV_CH,
            N_BRANCHES * D_MODEL)
IN_COLS = sum(IN_SIZES)


def _split_points():
    return np.cumsum(np.array(IN_SIZES))[:-1].tolist()

def rmsnorm(x, g):
    xf = x.astype(jnp.float32)
    y = xf * lax.rsqrt(jnp.mean(xf * xf, axis=-1, keepdims=True) + EPS)
    return (y * g.astype(jnp.float32)).astype(x.dtype)

def layernorm(x, g, b):
    xf = x.astype(jnp.float32)
    mu = jnp.mean(xf, axis=-1, keepdims=True)
    var = jnp.mean(jnp.square(xf - mu), axis=-1, keepdims=True)
    y = (xf - mu) * lax.rsqrt(var + EPS)
    return (y * g.astype(jnp.float32) + b.astype(jnp.float32)).astype(x.dtype)

def l2norm(x):
    return x * lax.rsqrt(jnp.sum(x * x, axis=-1, keepdims=True) + EPS)

def causal_depthwise_conv(x, w):
    K = w.shape[0]
    xp = jnp.pad(x, ((0, 0), (K - 1, 0), (0, 0)))
    return lax.conv_general_dilated(
        xp, w[:, None, :].astype(x.dtype), window_strides=(1,), padding='VALID',
        dimension_numbers=('NWC', 'WIO', 'NWC'), feature_group_count=x.shape[-1])

def gated_delta_chunked(q, k, v, g, beta):
    B, S, H, Dk = q.shape
    nc = S // CHUNK

    def to_chunks(t):
        t = t.reshape((B, nc, CHUNK, H) + t.shape[3:])
        return jnp.moveaxis(t, 3, 1)

    q, k, v = to_chunks(q) * (Dk ** -0.5), to_chunks(k), to_chunks(v)
    g, beta = to_chunks(g), to_chunks(beta)
    gc = jnp.cumsum(g, axis=-1)
    idx = jnp.arange(CHUNK)
    causal = idx[:, None] >= idx[None, :]
    strict = idx[:, None] > idx[None, :]
    decay = jnp.exp(jnp.where(causal, gc[..., :, None] - gc[..., None, :], -jnp.inf))
    kb = k * beta[..., None]
    A = jnp.einsum('bhnid,bhnjd->bhnij', kb, k) * decay * strict
    eye = jnp.eye(CHUNK, dtype=jnp.float32)
    T = lax.linalg.triangular_solve(eye + A, jnp.broadcast_to(eye, A.shape),
                                    left_side=True, lower=True, unit_diagonal=True)
    u = jnp.einsum('bhnij,bhnjd->bhnid', T, v * beta[..., None])
    w = jnp.einsum('bhnij,bhnjd->bhnid', T, kb * jnp.exp(gc)[..., None])
    qk = jnp.einsum('bhnid,bhnjd->bhnij', q, k) * decay
    q_dec = q * jnp.exp(gc)[..., None]
    g_last = gc[..., -1]
    k_end = k * jnp.exp(g_last[..., None] - gc)[..., None]
    xs = tuple(jnp.moveaxis(t, 2, 0) for t in (u, w, qk, q_dec, k_end, g_last))

    def step(Sst, inp):
        u_n, w_n, qk_n, qd_n, ke_n, gl_n = inp
        v_new = u_n - jnp.einsum('bhid,bhde->bhie', w_n, Sst)
        o = jnp.einsum('bhid,bhde->bhie', qd_n, Sst) + jnp.einsum('bhij,bhje->bhie', qk_n, v_new)
        Sst = Sst * jnp.exp(gl_n)[..., None, None] + jnp.einsum('bhid,bhie->bhde', ke_n, v_new)
        return Sst, o

    S0 = jnp.zeros((B, H, Dk, v.shape[-1]), jnp.float32)
    _, o = lax.scan(step, S0, xs)
    return jnp.transpose(o, (1, 0, 3, 2, 4)).reshape(B, S, H, v.shape[-1])

def first_inputs(seed: int = 0) -> dict:
    key = jax.random.key(seed)
    ks = jax.random.split(key, 24)
    f32 = jnp.float32
    nrm = lambda k, shape, s: jax.random.normal(k, shape, f32) * s
    gain = lambda k, shape: 1.0 + 0.05 * jax.random.normal(k, shape, f32)
    dt = jnp.exp(jax.random.uniform(ks[7], (DEPTH, DN_HEADS), f32, np.log(1e-3), np.log(1e-1)))
    return {
        "x": nrm(ks[0], (BATCH, SEQ, D_MODEL), 1.0),
        "p": nrm(ks[1], (DEPTH, BATCH, SEQ, PLE_DIM), 1.0),
        "g_pre": gain(ks[2], (DEPTH, D_MODEL)),
        "w_in": nrm(ks[3], (DEPTH, D_MODEL, IN_COLS), D_MODEL ** -0.5),
        "b_gate": nrm(ks[4], (DEPTH, N_BRANCHES * D_MODEL), 0.02),
        "w_conv_qkv": nrm(ks[5], (DEPTH, SHORT_CONV, 3 * DN_WIDTH), SHORT_CONV ** -0.5),
        "a_log": jnp.log(jax.random.uniform(ks[6], (DEPTH, DN_HEADS), f32, 1.0, 16.0)),
        "dt_bias": dt + jnp.log(-jnp.expm1(-dt)),
        "g_dn_out": gain(ks[8], (DEPTH, DN_HEAD_DIM)),
        "w_dw": nrm(ks[9], (DEPTH, CONV_KERNEL, CONV_CH), CONV_KERNEL ** -0.5),
        "b_dw": nrm(ks[10], (DEPTH, CONV_CH), 0.02),
        "ln_g": gain(ks[11], (DEPTH, CONV_CH)),
        "ln_b": nrm(ks[12], (DEPTH, CONV_CH), 0.02),
        "w_br_a": nrm(ks[13], (DEPTH, DN_WIDTH, D_MODEL), DN_WIDTH ** -0.5),
        "w_br_b": nrm(ks[14], (DEPTH, CONV_CH, D_MODEL), CONV_CH ** -0.5),
        "w_out": nrm(ks[15], (DEPTH, D_MODEL, D_MODEL), D_MODEL ** -0.5),
        "g_post": gain(ks[16], (DEPTH, D_MODEL)),
        "w_ple_gate": nrm(ks[17], (DEPTH, D_MODEL, D_MODEL), D_MODEL ** -0.5),
        "w_ple_proj": nrm(ks[18], (DEPTH, PLE_DIM, D_MODEL), PLE_DIM ** -0.5),
        "g_ple": gain(ks[19], (DEPTH, D_MODEL)),
    }

def first_block(x, p, g_pre, w_in, b_gate, w_conv_qkv, a_log, dt_bias, g_dn_out, w_dw, b_dw,
              ln_g, ln_b, w_br_a, w_br_b, w_out, g_post, w_ple_gate, w_ple_proj, g_ple):
    B, S, _ = x.shape
    f32 = jnp.float32
    for i in range(DEPTH):
        h = rmsnorm(x, g_pre[i])
        proj = h @ w_in[i]
        qkv, z_a, b_raw, a_raw, glu_in, z_b, gate_logits = jnp.split(proj, _split_points(), axis=-1)

        qkv = jax.nn.silu(causal_depthwise_conv(qkv, w_conv_qkv[i]))
        q, k, v = jnp.split(qkv, 3, axis=-1)
        heads = lambda t: t.reshape(B, S, DN_HEADS, DN_HEAD_DIM).astype(f32)
        q, k, v = l2norm(heads(q)), l2norm(heads(k)), heads(v)
        beta = jax.nn.sigmoid(b_raw.astype(f32))
        g_log = -jnp.exp(a_log[i].astype(f32)) * jax.nn.softplus(a_raw.astype(f32) + dt_bias[i].astype(f32))
        o_a = gated_delta_chunked(q, k, v, g_log, beta)
        o_a = rmsnorm(o_a, g_dn_out[i]).reshape(B, S, DN_WIDTH).astype(x.dtype) * jax.nn.silu(z_a)
        y_a = o_a @ w_br_a[i]

        u = jax.nn.glu(glu_in, axis=-1)
        u = causal_depthwise_conv(u, w_dw[i]) + b_dw[i]
        u = jax.nn.silu(layernorm(u, ln_g[i], ln_b[i])) * jax.nn.silu(z_b)
        y_b = u @ w_br_b[i]

        gate_a, gate_b = jnp.split(jax.nn.sigmoid(gate_logits + b_gate[i]), N_BRANCHES, axis=-1)
        mixed = (gate_a * y_a + gate_b * y_b) @ w_out[i]
        x = x + rmsnorm(mixed, g_post[i])

        e = p[i] @ w_ple_proj[i]
        x = x + rmsnorm(jax.nn.sigmoid(x @ w_ple_gate[i]) * e, g_ple[i])
    return x


N_HEADS = 16
QK_NOPE_DIM = 128
ROPE_DIM = 64
V_HEAD_DIM = 128
Q_LORA_RANK = 512
KV_LORA_RANK = 512
MLA_WIDTH = N_HEADS * V_HEAD_DIM
CONV_WIDTH = D_MODEL
CONV_K = 3
ROPE_THETA = 10000.0
RMS_EPS = 1e-6
BLOCK_Q = 128

IN_SPLIT = [
    Q_LORA_RANK,
    KV_LORA_RANK,
    ROPE_DIM,
    MLA_WIDTH,
    CONV_WIDTH,
    CONV_WIDTH,
    CONV_WIDTH,
    CONV_WIDTH,
    D_MODEL,
    D_MODEL,
]
IN_TOTAL = sum(IN_SPLIT)


def _rmsnorm(x, g):
    xf = x.astype(jnp.float32)
    r = lax.rsqrt(jnp.mean(xf * xf, axis=-1, keepdims=True) + RMS_EPS)
    return (xf * r * g.astype(jnp.float32)).astype(x.dtype)

def _rope_tables(positions):
    inv_freq = ROPE_THETA ** (-jnp.arange(0, ROPE_DIM, 2, dtype=jnp.float32) / ROPE_DIM)
    ang = positions.astype(jnp.float32)[..., None] * inv_freq
    return jnp.cos(ang), jnp.sin(ang)

def _apply_rope(x, cos, sin):
    xf = x.astype(jnp.float32)
    x1, x2 = jnp.split(xf, 2, axis=-1)
    out = jnp.concatenate([x1 * cos - x2 * sin, x1 * sin + x2 * cos], axis=-1)
    return out.astype(x.dtype)

def _causal_mla_attention(q_nope, q_rope, k_nope, k_rope, v):
    b, s, h, _ = q_nope.shape
    nb = s // BLOCK_Q
    scale = 1.0 / math.sqrt(QK_NOPE_DIM + ROPE_DIM)
    qn_blocks = q_nope.reshape(b, nb, BLOCK_Q, h, QK_NOPE_DIM).transpose(1, 0, 2, 3, 4)
    qr_blocks = q_rope.reshape(b, nb, BLOCK_Q, h, ROPE_DIM).transpose(1, 0, 2, 3, 4)
    key_pos = jnp.arange(s, dtype=jnp.int32)

    def one_block(args):
        qn, qr, blk = args
        sc = (jnp.einsum('bqhd,bkhd->bhqk', qn, k_nope)
              + jnp.einsum('bqhr,bkr->bhqk', qr, k_rope)).astype(jnp.float32) * scale
        q_pos = blk * BLOCK_Q + jnp.arange(BLOCK_Q, dtype=jnp.int32)
        mask = key_pos[None, :] <= q_pos[:, None]
        sc = jnp.where(mask[None, None], sc, -jnp.inf)
        p = jax.nn.softmax(sc, axis=-1).astype(v.dtype)
        return jnp.einsum('bhqk,bkhd->bqhd', p, v)

    out = lax.map(one_block, (qn_blocks, qr_blocks, jnp.arange(nb, dtype=jnp.int32)))
    return out.transpose(1, 0, 2, 3, 4).reshape(b, s, h, V_HEAD_DIM)

def second_inputs(seed: int = 0) -> dict:
    key = jax.random.key(seed)
    ks = jax.random.split(key, 16)
    f32 = jnp.float32

    def w(k, shape, fan_in):
        return jax.random.normal(k, shape, f32) * (fan_in ** -0.5)

    def gain(k, n):
        return 1.0 + 0.02 * jax.random.normal(k, (n,), f32)

    x = jax.random.normal(ks[0], (BATCH, SEQ, D_MODEL), f32)
    start = jax.random.randint(ks[1], (BATCH, 1), 0, 1024, dtype=jnp.int32)
    positions = start + jnp.arange(SEQ, dtype=jnp.int32)[None, :]
    return {
        "x": x,
        "positions": positions,
        "pre_norm_g": gain(ks[2], D_MODEL),
        "w_in": w(ks[3], (D_MODEL, IN_TOTAL), D_MODEL),
        "q_a_norm_g": gain(ks[4], Q_LORA_RANK),
        "w_q_b": w(ks[5], (Q_LORA_RANK, N_HEADS * (QK_NOPE_DIM + ROPE_DIM)), Q_LORA_RANK),
        "kv_a_norm_g": gain(ks[6], KV_LORA_RANK),
        "w_kv_b": w(ks[7], (KV_LORA_RANK, N_HEADS * (QK_NOPE_DIM + V_HEAD_DIM)), KV_LORA_RANK),
        "conv_w": w(ks[8], (CONV_K, CONV_WIDTH), CONV_K),
        "w_o_mla": w(ks[9], (MLA_WIDTH, D_MODEL), MLA_WIDTH),
        "w_o_conv": w(ks[10], (CONV_WIDTH, D_MODEL), CONV_WIDTH),
        "w_out": w(ks[11], (D_MODEL, D_MODEL), D_MODEL),
        "post_norm_g": gain(ks[12], D_MODEL),
    }

def second_block(x, positions, pre_norm_g, w_in, q_a_norm_g, w_q_b, kv_a_norm_g, w_kv_b,
              conv_w, w_o_mla, w_o_conv, w_out, post_norm_g):
    b, s, _ = x.shape
    cos, sin = _rope_tables(positions)
    for _layer in range(DEPTH):
        h = _rmsnorm(x, pre_norm_g)
        proj = jnp.einsum('bsd,de->bse', h, w_in)
        cuts = [int(c) for c in np.cumsum(IN_SPLIT)[:-1]]
        (q_a, c_kv, k_rope, z_mla, c_in, b_gate, c_gate, z_conv,
         g_mla, g_conv) = jnp.split(proj, cuts, axis=-1)

        q = jnp.einsum('bsr,re->bse', _rmsnorm(q_a, q_a_norm_g), w_q_b)
        q = q.reshape(b, s, N_HEADS, QK_NOPE_DIM + ROPE_DIM)
        q_nope, q_rope = q[..., :QK_NOPE_DIM], q[..., QK_NOPE_DIM:]
        kv = jnp.einsum('bsr,re->bse', _rmsnorm(c_kv, kv_a_norm_g), w_kv_b)
        kv = kv.reshape(b, s, N_HEADS, QK_NOPE_DIM + V_HEAD_DIM)
        k_nope, v = kv[..., :QK_NOPE_DIM], kv[..., QK_NOPE_DIM:]
        q_rope = _apply_rope(q_rope, cos[:, :, None, :], sin[:, :, None, :])
        k_rope = _apply_rope(k_rope, cos, sin)
        attn = _causal_mla_attention(q_nope, q_rope, k_nope, k_rope, v)
        attn = attn.reshape(b, s, MLA_WIDTH) * jax.nn.silu(z_mla)
        y_mla = jnp.einsum('bse,ed->bsd', attn, w_o_mla)

        u = c_gate * c_in
        u_pad = jnp.pad(u, ((0, 0), (CONV_K - 1, 0), (0, 0)))
        conv = sum(conv_w[k] * u_pad[:, k:k + s] for k in range(CONV_K))
        y_conv = jnp.einsum('bse,ed->bsd', b_gate * conv * jax.nn.silu(z_conv), w_o_conv)

        merged = jax.nn.sigmoid(g_mla) * y_mla + jax.nn.sigmoid(g_conv) * y_conv
        out = jnp.einsum('bsd,de->bse', merged, w_out)
        x = x + _rmsnorm(out, post_norm_g)
    return x


def setup_inputs(seed=0):
    out = dict(first_inputs(seed))
    for name, value in second_inputs(seed + 1).items():
        if name != "x":
            out[name + "_2"] = value
    return out


def reference(
    x, p, g_pre, w_in, b_gate, w_conv_qkv, a_log, dt_bias, g_dn_out, w_dw, b_dw, ln_g, ln_b,
    w_br_a, w_br_b, w_out, g_post, w_ple_gate, w_ple_proj, g_ple, positions_2, pre_norm_g_2,
    w_in_2, q_a_norm_g_2, w_q_b_2, kv_a_norm_g_2, w_kv_b_2, conv_w_2, w_o_mla_2, w_o_conv_2,
    w_out_2, post_norm_g_2,
):
    x = first_block(
        x, p, g_pre, w_in, b_gate, w_conv_qkv, a_log, dt_bias, g_dn_out, w_dw, b_dw, ln_g, ln_b,
        w_br_a, w_br_b, w_out, g_post, w_ple_gate, w_ple_proj, g_ple,
    )
    return second_block(
        x, positions_2, pre_norm_g_2, w_in_2, q_a_norm_g_2, w_q_b_2, kv_a_norm_g_2, w_kv_b_2,
        conv_w_2, w_o_mla_2, w_o_conv_2, w_out_2, post_norm_g_2,
    )


_drawn_inputs = setup_inputs


def setup_inputs(seed=0):
    import zlib

    import numpy as np

    out = dict(_drawn_inputs(seed))
    spreads = {}
    factors = {'b_gate': 8.0,
     'b_dw': 2.892,
     'ln_b': 6.536,
     'pre_norm_g_2': 2.822,
     'q_a_norm_g_2': 8.0,
     'kv_a_norm_g_2': 8.0,
     'post_norm_g_2': 5.432}
    for name, (base, spread) in spreads.items():
        noise = np.random.default_rng([zlib.crc32(name.encode()), seed]).standard_normal(out[name].shape)
        drawn = base * np.exp(spread * noise) if base else spread * noise
        out[name] = __import__('jax').numpy.asarray(drawn.astype(out[name].dtype))
    for name, factor in factors.items():
        out[name] = (out[name] * factor).astype(out[name].dtype)
    return out
```

```python
from contextlib import ExitStack

import concourse.bass as bass
from concourse import mybir

ALU = mybir.AluOpType
ACT = mybir.ActivationFunctionType
AX = mybir.AxisListType
F32 = mybir.dt.float32
F32R = mybir.dt.float32r
I32 = mybir.dt.int32

P = 128
TOK = 256
TT = TOK // P
D = 2048
KT = D // P
NB = 512
NJ = D // NB
CT = NB // P
CHUNK_KT = 4
CHUNK = CHUNK_KT * NB
HALF = CHUNK // 2
RAW = 4
HL = 4
LEAD = 3
LO_CREDIT = 2 * RAW
EPS = 1e-6
OWN_BYTES = 50 * 1024

HEADS, DK = 16, 128
SEQ_CHUNK = 64
GH = 4
TAPS = 31
LEVELS = 5
NCH = TOK // SEQ_CHUNK
SCAN = 2 * (NCH - 1)
SHORT = 4
PLE = 256
C_QKV = 0
C_Z = 3 * D
C_BA = C_Z + D
C_GLU = C_BA + 2 * HEADS
C_ZB = C_GLU + 2 * D
C_GATE = C_ZB + D

LORA = 512
NOPE, ROPE, VD = 128, 64, 128
QH = NOPE + ROPE
KVH = NOPE + VD
TAPS2 = 3
SCORES = 3 * P
C2_QA = 0
C2_KV = LORA
C2_KR = 2 * LORA
C2_ZM = C2_KR + ROPE
C2_CIN = C2_ZM + D
C2_BG = C2_CIN + D
C2_CG = C2_BG + D
C2_ZC = C2_CG + D
C2_GM = C2_ZC + D
C2_GC = C2_GM + D
ROPE_THETA = 10000.0
TWO_PI = 6.283185307179586
TWO_PI_1, TWO_PI_2, TWO_PI_3 = 6.28125, 0.001934051513671875, 1.255665914356996e-06
PI_BELOW = 3.1415925
ATT_SCALE = (NOPE + ROPE) ** -0.5

R_DW, R_BDW, R_LNG, R_LNB, R_GPRE, R_GPRE2, R_CW2, R_SC = 0, 31, 32, 33, 34, 35, 36, 39
N_ROWS = R_SC + 3 * SHORT
SQ_X, SQ_LN, SQ_MIX, SQ_PLE, SQ_X2, SQ_OUT = range(1, 7)
RSTD_X, RSTD_LN, RSTD_MIX, RSTD_PLE, RSTD_X2, RSTD_QA, RSTD_KV, RSTD_OUT = range(1, 9)
OP_HT, OP_X1, OP_H2, OP_LAT = 0, NJ, 2 * NJ, 3 * NJ
OP_M, OP_ATTN, OP_Y = 0, NJ, 2 * NJ
ROWS_X = 2 * TT
ROWS_PLE = ROWS_X + TT * NJ
TANH_ZB, TANH_Z, TANH_PLE, TANH_ZC, TANH_ZM = 0, NJ, 2 * NJ, 3 * NJ, 4 * NJ
MASK_IDENT, MASK_TRI, MASK_LVL, MASK_CAUSAL = range(1, 5)
PREP_ANGLE, PREP_PC, PREP_BA, PREP_GLOG, PREP_KEND = range(1, 6)
TABLE_SIN, TABLE_SOFTPLUS, TABLE_EXP = range(1, 4)
R2_QA, R2_KV, R2_DN, N_ROWS2 = 0, 4, 8, 9

OWN = ((8, 9, 10, (11, 14), 15, 16), (16, 18, 19, (20, 22), 23, 24), (24, 25, 26, (27, 29), 30, 31))
OWN_BANKS = (2, 2, 0)


class Phase:

    def __init__(self, k0, h0, b0, iters, halves, blocks):
        self.k0, self.h0, self.b0, self.iters = k0, h0, b0, iters
        self.kn, self.hn, self.bn = len(halves), sum(n for n, _ in halves), blocks


def plan():
    full = (2, HALF)
    order = [
        ("BA", 1, [(1, KT * 2 * HEADS)], 0),
        ("GLU0", 1, [full] * 8, 2),
        ("GLU", 3, [full] * 16, 4),
        ("GT3", 1, [full] * 8, 2),
        ("ZB", 2, [full] * 8, 2),
        ("QKVZ", 4, [full] * 16, 4),
        ("YB", 1, [full] * 16, 4),
        ("YA", 2, [full] * 8, 2),
        ("MIX", 2, [full] * 8, 2),
        ("PLEP", 1, [full] * 2, 4),
        ("PLEG", 2, [full] * 8, 2),
        ("QA", 1, [full] * 4, 1),
        ("KR", 1, [(1, KT * ROPE)], 0),
        ("KVA", 1, [full] * 4, 1),
        ("FC", 4, [full] * 20, 8),
        ("FZ", 2, [full] * 8, 2),
        ("FG", 4, [full] * 8, 2),
        ("YM", 2, [full] * 8, 2),
        ("YC", 2, [full] * 8, 2),
        ("OUT", 1, [full] * 16, 4),
    ]
    phases, halves, k, b = {}, [], 0, 0
    for name, iters, chunks, blocks in order:
        phases[name] = Phase(k, len(halves), b, iters, chunks, blocks)
        for _ in range(iters):
            for n, size in chunks:
                halves += [(k, x, size) for x in range(n)]
                k += 1
            b += blocks
    return phases, halves


class Chain:

    def __init__(self, eng, sem):
        self.eng, self.sem, self.n = eng, sem, 0

    def inc(self, ins):
        ins.then_inc(self.sem, 1)
        self.n += 1

    def wait(self, lag=0):
        if self.n > lag:
            self.eng.wait_ge(self.sem, self.n - lag)

    def link(self, ins):
        self.inc(ins)
        self.wait()

    def step(self):
        self.eng.sem_inc(self.sem, 1)
        self.n += 1
        self.wait()

    def restart(self):
        if self.n:
            self.step()
            self.eng.sem_clear(self.sem)
        self.n = 0


def build_layer(nc, t, out):
    PH, HALVES = plan()
    ctx = ExitStack()
    sems = {}

    def sem(name):
        if name not in sems:
            sems[name] = ctx.enter_context(nc.semaphore(name))
        return sems[name]

    def sb(name, shape, dt=F32, stack=ctx):
        return stack.enter_context(nc.sbuf_tensor(name, shape, dt))

    def dram(name, shape, dt=F32):
        return nc.dram_tensor(name, shape, dt, kind="Internal").ap()

    def kp(w):
        return w.rearrange("(kt p) n -> p kt n", p=P)

    w_in, w_in2 = kp(t["w_in"][0]), kp(t["w_in_2"])
    w_br_a, w_br_b, w_out = kp(t["w_br_a"][0]), kp(t["w_br_b"][0]), kp(t["w_out"][0])
    w_ple_gate, w_ple_proj = kp(t["w_ple_gate"][0]), kp(t["w_ple_proj"][0])
    w_q_b, w_kv_b = kp(t["w_q_b_2"]), kp(t["w_kv_b_2"])
    w_o_mla, w_o_conv, w_out2 = kp(t["w_o_mla_2"]), kp(t["w_o_conv_2"]), kp(t["w_out_2"])
    tok = lambda a: a.rearrange("(t p) n -> p t n", p=P)

    gate_dram = dram("gate_spill", (2, NJ, P, TT * NB))
    uT_dram = dram("conv_branch_spill", (2, NJ, P, CT * TOK), F32R)
    oT_dram = dram("delta_branch_spill", (2, NJ, P, CT * TOK), F32R)
    cT_dram = dram("short_conv_spill", (2, NJ, P, CT * TOK), F32R)
    o_dram = dram("attention_spill", (NJ, P, TT * NB))
    x2_dram = dram("residual_spill", (TOK, D))

    with ctx:
        raw = sb("raw", [P, RAW, CHUNK])
        w_hi = sb("w_hi", [P, HL, HALF], F32R)
        w_lo = sb("w_lo", [P, HL, HALF], F32R)
        r1h, r1l = sb("r1h", [P, KT, TOK], F32R), sb("r1l", [P, KT, TOK], F32R)
        ident = sb("ident", [P, P])
        tri_incl = sb("tri_incl", [P, P])
        strict_lo = sb("strict_lo", [P, P])
        same = sb("same", [P, P])
        half_ones = sb("half_ones", [P, 2, P])
        lvl = sb("lvl", [P, 5, P])
        m1u = sb("m1u", [P, P])
        ones_mean = sb("ones_mean", [P, P])
        pc = sb("pc", [P, KT, N_ROWS])
        pc2 = sb("pc2", [P, N_ROWS2])
        lnh = sb("lnh", [P, KT, 2])
        neg_half = sb("neg_half", [P, 1])
        beta = sb("beta", [P, TT, HEADS])
        hbeta = sb("hbeta", [P, TT, HEADS])
        glog = sb("glog", [P, TT, HEADS])
        egc = sb("egc", [P, TT, HEADS])
        kend = sb("kend", [P, TT, HEADS])
        egl = sb("egl", [P, TT, 2, HEADS])
        cos_t, sin_t = sb("cos_t", [P, TT, ROPE // 2]), sb("sin_t", [P, TT, ROPE // 2])
        stat = sb("stat", [P, 64])
        arena_at = nc.sbuf_base

        with ExitStack() as st:
            s1 = lambda n, shape, dt=F32: sb(n, shape, dt, st)
            upad = s1("upad", [P, CT, TAPS - 1 + TOK])
            ycur = s1("ycur", [P, CT, TOK])
            sg = s1("sg", [P, TT, NB])
            u = s1("u", [P, TT, NB])
            gtA, gtB = s1("gtA", [P, TT, NB]), s1("gtB", [P, TT, NB])
            bgt = s1("bgt", [P, 2, NB])
            th0 = s1("th0", [P, TT, NB])
            sz0 = s1("sz0", [P, TT, NB])
            pcw = s1("pcw", [P, CT, TAPS + 1])
            uz = s1("uz", [P, TAPS - 1 + TOK])
            pcz = s1("pcz", [P, TAPS + 1])
            bat = s1("bat", [P, TT, 2 * HEADS])
            ba_tmp = s1("ba_tmp", [P, 6, TT, HEADS])
            ba_const = s1("ba_const", [P, 2, HEADS])
            rope_f = s1("rope_f", [P, 6, TT, ROPE // 2])
            pos_i = s1("pos_i", [P, TT], I32)
            pos_f = s1("pos_f", [P, TT])
            inv_f = s1("inv_f", [P, ROPE // 2])
            own_end = delta_at = arena_at + OWN_BYTES
            s1("pad_to_delta", [P, (own_end - nc.sbuf_base) // 4])
            with ExitStack() as st2:
                xt = sb("xt", [P, TT, D], F32, st2)
                crow = sb("crow", [N_ROWS, D], F32, st2)
                crow2 = sb("crow2", [N_ROWS2, P], F32, st2)
            y = s1("y", [P, KT, TOK])
            szT = s1("szT", [P, KT, TOK])
            lnsq = s1("lnsq", [P, CT, TOK])
            lnt = s1("lnt", [P, CT, TOK])
            luh, lul = s1("luh", [P, CT, TOK], F32R), s1("lul", [P, CT, TOK], F32R)
            var = s1("var", [P, TT])
            rows = s1("rows", [P, TOK])
            rdiag = s1("rdiag", [P, TT, P])

        with ExitStack() as st:
            s1 = lambda n, shape, dt=F32: sb(n, shape, dt, st)
            praw = s1("praw", [P, TT, NB])
            cpad = s1("cpad", [P, GH, SHORT - 1 + TOK])
            cy = s1("cy", [P, GH, TOK])
            cth = s1("cth", [P, TT, NB])
            qtok, qd = s1("qtok", [P, TT, GH, DK]), s1("qd", [P, TT, GH, DK])
            ktok, kb = s1("ktok", [P, TT, GH, DK]), s1("kb", [P, TT, GH, DK])
            kbe, ke = s1("kbe", [P, TT, GH, DK]), s1("ke", [P, TT, GH, DK])
            vb = s1("vb", [P, TT, GH, DK])
            sz = s1("sz", [P, TT, GH, DK])
            wq4 = s1("wq4", [P, 3, GH, SHORT])
            dcol = s1("dcol", [P, 12, TT, GH])
            degl = s1("degl", [P, TT, 2, GH])
            assert nc.sbuf_base <= own_end, (nc.sbuf_base, own_end)
            s1("pad_to_delta2", [P, max(1, (own_end - nc.sbuf_base) // 4)])
            kT, kbT = s1("kT", [P, TT, GH, P]), s1("kbT", [P, TT, GH, P])
            qT, qdT = s1("qT", [P, TT, GH, P]), s1("qdT", [P, TT, GH, P])
            decT = s1("decT", [P, TT, GH, P])
            xs = s1("xs", [P, TT, GH, P])
            bf = s1("bf", [P, TT, GH, P])
            qkT = s1("qkT", [P, TT, GH, P])
            uinv = s1("uinv", [P, TT, GH, P])
            state = s1("state", [P, GH, DK])
            oh, ol = s1("oh", [P, GH, TOK], F32R), s1("ol", [P, GH, TOK], F32R)
            gm, tinv, us, wT, otok = xs, kb, qd, kbT, qT
        with ExitStack() as st:
            gy = sb("gy", [P, TT, D], F32, st)
            assert nc.sbuf_base <= arena_at + 4 * 4 * 1024 + 64

        tail_at = delta_at + 2 * KT * TOK * 4
        with ExitStack() as st:
            s1 = lambda n, shape, dt=F32: sb(n, shape, dt, st)
            mix = s1("mix", [P, TT, D])
            e = s1("e", [P, TT, D])
            xres = s1("xres", [P, 2, TT, NB])
            pth = s1("pth", [P, TT, NB])
            pTh, pTl = s1("pTh", [P, PLE // P, TOK], F32R), s1("pTl", [P, PLE // P, TOK], F32R)
            s1("pad_d", [P, max(1, (own_end - nc.sbuf_base) // 4)])
            r2h, r2l = s1("r2h", [P, KT, TOK], F32R), s1("r2l", [P, KT, TOK], F32R)
            gpost, gple = s1("gpost", [P, D]), s1("gple", [P, D])
        ptok = pth[:, 0].rearrange("p (t n) -> p t n", t=TT)
        with ExitStack() as st:
            s1 = lambda n, shape, dt=F32: sb(n, shape, dt, st)
            qst = s1("qst", [P, TT, GH * QH])
            kvst = s1("kvst", [P, TT, 2, NB])
            qr = s1("qr", [P, TT, GH, ROPE])
            qTn, qrT = s1("qTn", [P, GH, TOK]), s1("qrT", [P, GH // 2, TOK])
            kTn = s1("kTn", [P, GH, TOK])
            sc = s1("sc", [P, GH, SCORES])
            pT = s1("pT", [P, GH, SCORES])
            ost = s1("ost", [P, TT, GH, VD])
            c3 = s1("c3", [P, CT, TOK])
            krT = s1("krT", [P, TOK])
            amask = s1("amask", [P, SCORES])
            mx, nmx, den, rec = [s1(n, [P, TT, GH]) for n in ("mx", "nmx", "den", "rec")]
            assert nc.sbuf_base <= own_end
            s1("pad_f", [P, (tail_at - nc.sbuf_base) // 4])
            cg = s1("cg", [P, TT, NB])
            u2pad = s1("u2pad", [P, CT, TAPS2 - 1 + TOK])
            zs = s1("zs", [P, TT, NB])
            rtmp = s1("rtmp", [P, 2, TT, GH, ROPE // 2])
            wc2 = s1("wc2", [P, CT, TAPS2])
            assert nc.sbuf_base <= tail_at + 2 * D * 4
        qa_t, kva_t = kvst[:, :, 0], kvst[:, :, 1]
        with ExitStack() as st:
            s1 = lambda n, shape, dt=F32: sb(n, shape, dt, st)
            thm, thc = s1("thm", [P, TT, D]), s1("thc", [P, TT, D])
            oin = s1("oin", [P, 2, TT, NB])
            thz = s1("thz", [P, TT, NB])
            assert nc.sbuf_base <= own_end
        outst, x2r, gpost2 = thm, thc, gpost
        gth = [qtok, ktok]
        mtmp = kbe[:].rearrange("p t h d -> p t (h d)")

        acc = ctx.enter_context(nc.psum_tensor("acc", [P, 2, TT, NB], F32))
        X = ctx.enter_context(nc.psum_tensor("aux", [P, 4, NB], F32))

        landed = [sem(f"raw_landed{i}") for i in range(RAW)]
        hi_ready, lo_ready, w_used = sem("hi_ready"), sem("lo_ready"), sem("w_used")
        acc_free = [sem("acc0_free"), sem("acc1_free")]

        def used(ph, hl, i=0):
            return HL + ph.h0 + hl + 1 + i * ph.hn

        def freed(ph, bl, i=0):
            return 2 * ((ph.b0 + bl) // 2) + 2 + i * ph.bn

        block = ctx.enter_context(nc.Block())

        @block.sync
        def _(sp):
            def load(ph, cl, src, i=0, shape=None):
                k = ph.k0 + cl
                if k >= RAW:
                    last = max(h for h, (c, _, _) in enumerate(HALVES) if c == k - RAW)
                    sp.wait_ge(lo_ready, LO_CREDIT + last + 1 + i * ph.hn)
                elif not isinstance(i, int):
                    sp.wait_ge(lo_ready, LO_CREDIT + 2 * (k - RAW) + 1 + i * ph.hn)
                a, b = shape or (CHUNK_KT, NB)
                dst = raw[:, k % RAW, 0:a * b].rearrange("p (a b) -> p a b", a=a)
                sp.dma_start(dst, src).then_inc(landed[k % RAW], 16)

            def load_block(ph, bl, w, col, i=0, cl=None):
                cl = 4 * bl if cl is None else cl
                for c in range(KT // CHUNK_KT):
                    load(ph, cl + c, w[:, CHUNK_KT * c:CHUNK_KT * (c + 1), bass.ds(col, NB)], i)

            sp.dma_start(xt[:], tok(t["x"][0])).then_inc(sem("x_landed"), 16)
            sp.dma_start(crow[R_DW:R_DW + TAPS, :], t["w_dw"][0]).then_inc(sem("rows_landed"), 16)
            for r, name in ((R_BDW, "b_dw"), (R_LNG, "ln_g"), (R_LNB, "ln_b"), (R_GPRE, "g_pre")):
                sp.dma_start(crow[r:r + 1, :], t[name]).then_inc(sem("rows_landed"), 16)
            sp.dma_start(crow[R_GPRE2:R_GPRE2 + 1, :], t["pre_norm_g_2"].rearrange("(a n) -> a n", a=1)).then_inc(sem("rows_landed"), 16)
            sp.dma_start(crow[R_CW2:R_CW2 + TAPS2, :], t["conv_w_2"]).then_inc(sem("rows_landed"), 16)
            for n in range(3):
                sp.dma_start(crow[R_SC + SHORT * n:R_SC + SHORT * (n + 1), :],
                             t["w_conv_qkv"][0][:, n * D:(n + 1) * D]).then_inc(sem("rows_landed"), 16)
            for r, name in ((R2_QA, "q_a_norm_g_2"), (R2_KV, "kv_a_norm_g_2")):
                sp.dma_start(crow2[r:r + 4, :], t[name].rearrange("(a n) -> a n", n=P)).then_inc(sem("rows_landed"), 16)
            sp.dma_start(crow2[R2_DN:R2_DN + 1, :], t["g_dn_out"]).then_inc(sem("rows_landed"), 16)

            load(PH["BA"], 0, w_in[:, :, C_BA:C_BA + 2 * HEADS], shape=(KT, 2 * HEADS))
            load_block(PH["GLU0"], 0, w_in, C_GLU + D)
            load_block(PH["GLU0"], 1, w_in, C_GLU)
            with sp.Fori(0, PH["GLU"].iters) as i:
                ph = PH["GLU"]
                load_block(ph, 0, w_in, i * NB + C_GATE, i)
                load_block(ph, 1, w_in, i * NB + (C_GATE + D), i)
                load_block(ph, 2, w_in, i * NB + (C_GLU + D + NB), i)
                load_block(ph, 3, w_in, i * NB + (C_GLU + NB), i)
            load_block(PH["GT3"], 0, w_in, C_GATE + 3 * NB)
            load_block(PH["GT3"], 1, w_in, C_GATE + D + 3 * NB)
            with sp.Fori(0, 2) as i:
                load_block(PH["ZB"], 0, w_in, i * (2 * NB) + C_ZB, i)
                load_block(PH["ZB"], 1, w_in, i * (2 * NB) + (C_ZB + NB), i)
            with sp.Fori(0, NJ) as i:
                for n in range(4):
                    load_block(PH["QKVZ"], n, w_in, i * NB + n * D, i)
            for j in range(NJ):
                load_block(PH["YB"], j, w_br_b, j * NB)
            for name, w in (("YA", w_br_a), ("MIX", w_out)):
                with sp.Fori(0, 2) as i:
                    load_block(PH[name], 0, w, i * (2 * NB), i)
                    load_block(PH[name], 1, w, i * (2 * NB) + NB, i)
            for c in range(2):
                load(PH["PLEP"], c, w_ple_proj[:, :, c * 2 * NB:(c + 1) * 2 * NB], shape=(2, 2 * NB))
            with sp.Fori(0, 2) as i:
                load_block(PH["PLEG"], 0, w_ple_gate, i * (2 * NB), i)
                load_block(PH["PLEG"], 1, w_ple_gate, i * (2 * NB) + NB, i)
            load_block(PH["QA"], 0, w_in2, C2_QA)
            load(PH["KR"], 0, w_in2[:, :, C2_KR:C2_KR + ROPE], shape=(KT, ROPE))
            load_block(PH["KVA"], 0, w_in2, C2_KV)
            with sp.Fori(0, NJ) as i:
                ph = PH["FC"]
                load(ph, 0, w_q_b[:, :, bass.ds(i * (GH * QH), NB)], i)
                load(ph, 1, w_q_b[:, :, bass.ds(i * (GH * QH) + (GH * QH - NB), NB)], i)
                load(ph, 2, w_kv_b[:, :, bass.ds(i * (GH * KVH), NB)], i)
                load(ph, 3, w_kv_b[:, :, bass.ds(i * (GH * KVH) + NB, NB)], i)
                for n, col in enumerate((C2_CG, C2_CIN, C2_ZC, C2_BG)):
                    load_block(ph, None, w_in2, i * NB + col, i, cl=4 + 4 * n)
            with sp.Fori(0, 2) as i:
                load_block(PH["FZ"], 0, w_in2, i * (2 * NB) + C2_ZM, i)
                load_block(PH["FZ"], 1, w_in2, i * (2 * NB) + (C2_ZM + NB), i)
            with sp.Fori(0, NJ) as i:
                load_block(PH["FG"], 0, w_in2, i * NB + C2_GM, i)
                load_block(PH["FG"], 1, w_in2, i * NB + C2_GC, i)
            for name, w in (("YM", w_o_mla), ("YC", w_o_conv)):
                with sp.Fori(0, 2) as i:
                    load_block(PH[name], 0, w, i * (2 * NB), i)
                    load_block(PH[name], 1, w, i * (2 * NB) + NB, i)
            for j in range(NJ):
                load_block(PH["OUT"], j, w_out2, j * NB)
            for j in range(NJ):
                sp.wait_ge(sem("out_ready"), j + 1)
                sp.dma_start(tok(out[0])[:, :, j * NB:(j + 1) * NB], outst[:, :, j * NB:(j + 1) * NB]).then_inc(sem("out_done"), 16)
            sp.wait_ge(sem("out_done"), 16 * NJ)

        @block.gpsimd
        def _(pool):
            c = Chain(pool, sem("pool_order"))
            g = nc.gpsimd
            c.link(g.memset(ident[:], 0.0))
            c.link(g.affine_select(out=ident[:], in_=ident[:], compare_op=ALU.not_equal, fill=1.0, base=0,
                                   pattern=[[-1, P]], channel_multiplier=1))
            pool.sem_inc(sem("mask_ready"), 1)
            c.link(g.memset(neg_half[:], -0.5))
            for m in (same, tri_incl, strict_lo):
                c.link(g.memset(m[:], 1.0))
                v = m[:].rearrange("p (b s) -> p b s", s=SEQ_CHUNK)
                c.link(g.affine_select(out=v, in_=v, compare_op=ALU.is_ge, fill=0.0, base=0,
                                       pattern=[[-SEQ_CHUNK, P // SEQ_CHUNK], [0, SEQ_CHUNK]], channel_multiplier=1))
                c.link(g.affine_select(out=v, in_=v, compare_op=ALU.is_ge, fill=0.0, base=SEQ_CHUNK - 1,
                                       pattern=[[SEQ_CHUNK, P // SEQ_CHUNK], [0, SEQ_CHUNK]], channel_multiplier=-1))
            c.link(g.affine_select(out=tri_incl[:], in_=tri_incl[:], compare_op=ALU.is_ge, fill=0.0, base=0,
                                   pattern=[[1, P]], channel_multiplier=-1))
            c.link(g.affine_select(out=strict_lo[:], in_=strict_lo[:], compare_op=ALU.is_ge, fill=0.0, base=-1,
                                   pattern=[[-1, P]], channel_multiplier=1))
            c.link(g.memset(half_ones[:], 0.0))
            for n in range(2):
                c.link(g.memset(half_ones[n * SEQ_CHUNK:(n + 1) * SEQ_CHUNK, n, :], 1.0))
            c.link(g.memset(ones_mean[:], 1.0 / D))
            pool.sem_inc(sem("mask_ready"), 1)
            c.link(g.memset(lvl[:], 0.0))
            c.link(g.memset(m1u[:], 0.0))
            for l in range(5):
                s = 4 << l
                v = lvl[:, l, :].rearrange("p (b s) -> p b s", s=s)
                c.link(g.memset(v[:, :, 0:s // 2], 1.0))
                c.link(g.affine_select(out=v, in_=v, compare_op=ALU.is_ge, fill=0.0, base=-s // 2,
                                       pattern=[[-s, P // s], [0, s]], channel_multiplier=1))
                c.link(g.affine_select(out=v, in_=v, compare_op=ALU.is_ge, fill=0.0, base=s - 1,
                                       pattern=[[s, P // s], [0, s]], channel_multiplier=-1))
            v = m1u[:].rearrange("p (b s) -> p b s", s=2)
            c.link(g.affine_select(out=v[:, :, 1], in_=v[:, :, 1], compare_op=ALU.not_equal, fill=1.0, base=0,
                                   pattern=[[-2, P // 2]], channel_multiplier=1))
            pool.sem_inc(sem("mask_ready"), 1)

            pool.dma_start(ba_const[:, 0, :], t["a_log"][0].partition_broadcast(P)).then_inc(sem("small_landed"), 16)
            pool.dma_start(ba_const[:, 1, :], t["dt_bias"][0].partition_broadcast(P)).then_inc(sem("small_landed"), 16)
            pool.dma_start(inv_f[:], t["inv_freq"][0].partition_broadcast(P)).then_inc(sem("small_landed"), 16)
            with nc.allow_non_contiguous_dma(reason="256 positions"):
                pool.dma_start(pos_i[:], t["positions_2"][0].rearrange("(t p) -> p t", p=P)).then_inc(sem("small_landed"), 16)

            def rsqrt(dst, src, scale, ready, value, post=None):
                pool.wait_ge(ready, value)
                n = src.shape[-1]
                c.link(g.tensor_scalar(dst, src, scale, EPS, ALU.mult, ALU.add))
                c.link(g.tensor_tensor(dst, dst, neg_half[:, 0:1].to_broadcast([P, n]), ALU.pow))
                if post is not None:
                    c.link(g.tensor_scalar(dst, dst, post, None, ALU.mult))
                pool.sem_inc(sem("rstd_ready"), 1)

            rsqrt(stat[:, 2:4], stat[:, 0:2], 1.0 / D, sem("square_ready"), SQ_X)

            def bias(i):
                pool.dma_start(bgt[:, 0, :], t["b_gate"][0, bass.ds(i * NB, NB)].partition_broadcast(P)).then_inc(sem("bias_landed"), 16)
                pool.dma_start(bgt[:, 1, :], t["b_gate"][0, bass.ds(i * NB + D, NB)].partition_broadcast(P)).then_inc(sem("bias_landed"), 16)

            def gates_out(i):
                for kind, tile in ((0, gtA), (1, gtB)):
                    pool.wait_ge(sem(f"gate{kind}_ready"), i + 1)
                    pool.dma_start(gate_dram[kind, bass.ds(i, 1)].rearrange("a p n -> p (a n)"),
                                   tile[:].rearrange("p t n -> p (t n)")).then_inc(sem("gate_out"), 16)

            bias(0)
            c.restart()
            with pool.Fori(0, PH["GLU"].iters) as i:
                gates_out(i)
                pool.wait_ge(sem("gate_out"), 32 * i + 32)
                bias(i + 1)
            gates_out(3)

            q4 = lambda q: y[:, CT * q:CT * (q + 1)]
            row4 = rows[:].unsqueeze(1).to_broadcast([P, CT, TOK])
            pool.wait_ge(sem("rows_ready"), 1)
            pool.wait_ge(sem("conv_done"), NJ + 3)
            for q in range(NJ):
                g.tensor_tensor(q4(q), q4(q), row4, ALU.subtract).then_inc(sem("ln_centered"), 1)
            rsqrt(var[:], var[:], 1.0, sem("square_ready"), SQ_LN)
            def ln_out(q):
                pool.wait_ge(sem("ln_silu"), q + 1)
                g.tensor_tensor(lnt[:], lnt[:], szT[:, CT * q:CT * (q + 1)], ALU.mult).then_inc(sem("ln_out"), 1)
                pool.wait_ge(sem("ln_lo"), q + 1)
                for n, tile in ((0, luh), (1, lul)):
                    pool.dma_start(uT_dram[n, q], tile[:].rearrange("p a b -> p (a b)")).then_inc(sem("uT_out"), 16)
            pool.wait_ge(sem("rows_ready"), 2)
            pool.wait_ge(sem("ln_centered"), NJ)
            for q in range(NJ):
                g.tensor_tensor(q4(q), q4(q), row4, ALU.mult).then_inc(sem("ln_norm"), 1)
            for q in range(NJ):
                ln_out(q)

            def inverse_norm(i, dst, src, n, post):
                pool.wait_ge(sem("qk_square"), i * 2 + (n + 1))
                c.step()
                c.link(g.tensor_scalar(dcol[:, dst], dcol[:, src], 0.25, EPS, ALU.mult, ALU.add))
                c.link(g.tensor_tensor(dcol[:, dst], dcol[:, dst], neg_half[:, 0:1].to_broadcast([P, TT, GH]), ALU.pow))
                c.link(g.tensor_scalar(dcol[:, dst], dcol[:, dst], post, None, ALU.mult))

            def columns_q(i):
                heads = bass.ds(i * GH, GH)
                inverse_norm(i, 0, 8, 0, 0.5 * DK ** -0.5)
                c.link(g.tensor_copy(dcol[:, 1], egc[:, :, heads]))
                c.link(g.tensor_copy(dcol[:, 3], beta[:, :, heads]))
                c.link(g.tensor_tensor(dcol[:, 4], dcol[:, 3], egc[:, :, heads], ALU.mult))
                c.link(g.tensor_copy(dcol[:, 5], kend[:, :, heads]))
                c.link(g.tensor_copy(dcol[:, 6], hbeta[:, :, heads]))
                c.link(g.tensor_copy(dcol[:, 7], glog[:, :, heads]))

            def columns_k(i, first):
                heads = bass.ds(i * GH, GH)
                inverse_norm(i, 2, 9, 1, 0.5)
                if not first:
                    pool.wait_ge(sem("scan_ready"), i * SCAN)
                    c.step()
                c.link(g.tensor_copy(degl[:], egl[:, :, :, heads]))
                pool.sem_inc(sem("cols_ready"), 1)

            def delta_norm(d):
                pool.wait_ge(sem("o_square"), d + 1)
                c.step()
                c.link(g.tensor_scalar(dcol[:, 10], dcol[:, 11], 1.0 / DK, EPS, ALU.mult, ALU.add))
                c.link(g.tensor_tensor(dcol[:, 10], dcol[:, 10], neg_half[:, 0:1].to_broadcast([P, TT, GH]), ALU.pow))
                pool.sem_inc(sem("o_rstd"), 1)

            def delta_out(d):
                pool.wait_ge(sem("oT_lo"), 2 * (d + 1))
                for n, tile in ((0, oh), (1, ol)):
                    pool.dma_start(oT_dram[n, bass.ds(d, 1)].rearrange("a p n -> p (a n)"),
                                   tile[:].rearrange("p a b -> p (a b)")).then_inc(sem("oT_out"), 16)
                pool.wait_ge(sem("oT_out"), 32 * (d + 1))

            columns_q(0)
            columns_k(0, True)
            c.restart()
            with pool.Fori(1, NJ) as i:
                columns_q(i)
                delta_norm(i - 1)
                columns_k(i, False)
                delta_out(i - 1)
                c.restart()

            def reload(src, dst, ph, bl, i, out_sem, out_value):
                for q in range(NJ):
                    pool.wait_ge(w_used, used(ph, 8 * bl + 2 * q + 1, i))
                    pool.wait_ge(out_sem, out_value)
                    for n, r in enumerate(dst):
                        pool.dma_start(r[:, CT * q:CT * (q + 1), :].rearrange("p a b -> p (a b)"), src[n, q]).then_inc(sem(f"operand_landed{q}"), 16)

            reload(uT_dram, (r1h, r1l), PH["QKVZ"], 3, 3, sem("uT_out"), 32 * NJ)

            def load_gate(kind, j, n):
                src = gate_dram[kind, bass.ds(j, 1)].rearrange("a p n -> p (a n)")
                pool.dma_start(gth[n][:].rearrange("p t h d -> p (t h d)"), src).then_inc(sem(f"tile_landed{n}"), 16)

            pool.wait_ge(sem("gate_out"), 16 * 2 * NJ)
            pool.wait_ge(sem("qT_tr"), 2 * NJ)
            load_gate(1, 0, 0)
            pool.wait_ge(sem("k_scaled"), NJ)
            load_gate(1, 1, 1)
            for j in range(2, NJ):
                pool.wait_ge(sem("gy_ready"), j - 1)
                load_gate(1, j, j % 2)
            delta_norm(3)
            delta_out(3)
            pool.wait_ge(sem("gy_ready"), NJ - 1)
            load_gate(0, 0, 0)
            reload(oT_dram, (r1h, r1l), PH["YB"], 3, 0, sem("oT_out"), 32 * NJ)
            pool.wait_ge(sem("gy_ready"), NJ)
            load_gate(0, 1, 1)
            for j in range(2, NJ):
                pool.wait_ge(sem("m_ready"), OP_M + j - 1)
                load_gate(0, j, j % 2)
            pool.wait_ge(sem("oT_out"), 32 * NJ)
            pool.dma_start(ptok, tok(t["p"][0, 0])).then_inc(sem("p_landed"), 16)
            pool.dma_start(gpost[:], t["g_post"][0].partition_broadcast(P)).then_inc(sem("gains_landed"), 16)
            pool.dma_start(gple[:], t["g_ple"][0].partition_broadcast(P)).then_inc(sem("gains_landed"), 16)
            pool.wait_ge(sem("m_tr"), NJ)
            for j in range(NJ):
                if j >= 2:
                    pool.wait_ge(sem("op_ready"), j - 1)
                pool.dma_start(xres[:, j % 2], tok(t["x"][0])[:, :, j * NB:(j + 1) * NB]).then_inc(sem(f"tile_landed{j % 2}"), 16)
                if j == 1:
                    rsqrt(stat[:, 6:8], stat[:, 4:6], 1.0 / D, sem("square_ready"), SQ_MIX)
            rsqrt(stat[:, 10:12], stat[:, 8:10], 0.25 / D, sem("square_ready"), SQ_PLE, post=0.5)
            rsqrt(stat[:, 14:16], stat[:, 12:14], 1.0 / D, sem("square_ready"), SQ_X2)
            pool.dma_start(tok(x2_dram), mix[:]).then_inc(sem("x2_out"), 16)

            c.link(g.memset(amask[:], 0.0))
            for at in (0, 2 * P):
                m = amask[:, at:at + P]
                c.link(g.affine_select(out=m, in_=m, compare_op=ALU.is_ge, fill=-1e30, base=0, pattern=[[-1, P]], channel_multiplier=1))
            pool.sem_inc(sem("mask_ready"), 1)
            rsqrt(stat[:, 48:50], stat[:, 44:46], 1.0 / LORA, acc_free[0], freed(PH["QA"], 0))
            rsqrt(stat[:, 50:52], stat[:, 46:48], 1.0 / LORA, acc_free[1], freed(PH["KVA"], 0))
            pool.sem_inc(sem("ost_free"), 1)
            pool.sem_inc(sem("ct_free"), 1)
            c.restart()
            with pool.Fori(0, NJ) as i:
                pool.wait_ge(sem("ost_ready"), i + 1)
                c.step()
                pool.dma_start(o_dram[bass.ds(i, 1)].rearrange("a p n -> p (a n)"), ost[:].rearrange("p t h d -> p (t h d)")).then_inc(sem("o_out"), 16)
                pool.wait_ge(sem("o_out"), i * 16 + 16)
                pool.sem_inc(sem("ost_free"), 1)
                pool.wait_ge(sem("c_lo"), i + 1)
                c.step()
                for n, r in enumerate((r1h, r1l)):
                    pool.dma_start(cT_dram[n, bass.ds(i, 1)].rearrange("a p n -> p (a n)"),
                                   r[:, 2 * CT:3 * CT].rearrange("p a b -> p (a b)")).then_inc(sem("cT_out"), 16)
                pool.wait_ge(sem("cT_out"), i * 32 + 32)
                pool.sem_inc(sem("ct_free"), 1)
                c.restart()
            for j in range(NJ):
                if j >= 2:
                    pool.wait_ge(sem("m_tr"), OP_ATTN + j - 1)
                pool.dma_start(oin[:, j % 2].rearrange("p t n -> p (t n)"), o_dram[j]).then_inc(sem(f"tile_landed{j % 2}"), 16)
            pool.dma_start(gpost2[:], t["post_norm_g_2"].partition_broadcast(P)).then_inc(sem("gains_landed"), 16)
            reload(cT_dram, (r2h, r2l), PH["FG"], 1, 3, sem("cT_out"), 32 * NJ)
            pool.wait_ge(sem("m_ready"), OP_Y + NJ)
            pool.dma_start(x2r[:], tok(x2_dram)).then_inc(sem("x2_landed"), 16)
            rsqrt(stat[:, 62:64], stat[:, 60:62], 1.0 / D, sem("square_ready"), SQ_OUT)

        @block.scalar
        def _(act):
            c = Chain(act, sem("act_order"))
            A = nc.scalar.activation

            def split(h, i=0, hn=0, kn=0):
                if h >= len(HALVES):
                    return
                k, x, n = HALVES[h]
                act.wait_ge(landed[k % RAW], 16 * (k // RAW + 1) + i * (16 * kn // RAW))
                act.wait_ge(w_used, h + 1 + i * hn)
                nc.scalar.copy(w_hi[:, h % HL, 0:n], raw[:, k % RAW, x * HALF:x * HALF + n]).then_inc(hi_ready, 1)

            def ahead(ph, hl, i=0):
                split(ph.h0 + hl + LEAD, i, ph.hn, ph.kn)

            def sig(ins, name, value):
                ins.then_inc(sem(name), 1)
                act.wait_ge(sem(name), value)

            def sig_free(ins, s, value):
                ins.then_inc(acc_free[s], 1)

            for h in range(LEAD):
                split(h)

            act.wait_ge(sem("x_landed"), 16)
            for n in range(TT):
                sig(A(sz0[:].rearrange("p t n -> p (t n)"), xt[:, n, 0:D // 2], ACT.Square, accum_out=stat[:, 40 + n:41 + n]), "row_sq", 2 * n + 1)
                sig(A(sz0[:].rearrange("p t n -> p (t n)"), xt[:, n, D // 2:D], ACT.Square, accum_out=stat[:, 42 + n:43 + n]), "row_sq", 2 * n + 2)
            act.wait_ge(sem("prep_ready"), PREP_ANGLE)
            c.inc(A(sin_t[:], rope_f[:, 2], ACT.Sin))
            c.link(A(rope_f[:, 3], rope_f[:, 2], ACT.Sin, scale=0.5))
            act.sem_inc(sem("table_ready"), 1)

            act.wait_ge(sem("rstd_ready"), RSTD_X)
            for n in range(TT):
                sig(A(xt[:, n], xt[:, n], ACT.Copy, scale=stat[:, 2 + n:3 + n]), "xn_ready", n + 1)

            def stationary_hi(dst, kt, bank, scale_col, tr_sem, tr_value, hi_sem, hi_value):
                act.wait_ge(tr_sem, tr_value)
                c.inc(A(dst[:, kt], X[:, bank, 0:TOK], ACT.Copy, scale=scale_col[0]))
                sig(A(dst[:, kt + 1], X[:, bank, TOK:2 * TOK], ACT.Copy, scale=scale_col[1]), hi_sem, hi_value)

            act.wait_ge(sem("prep_ready"), PREP_PC)
            for m in range(KT // 2):
                stationary_hi(r1h, 2 * m, m % 4, [pc[:, 2 * m + q, R_GPRE:R_GPRE + 1] for q in range(2)],
                              sem("xT_tr"), m + 1, "op_hi", 2 * OP_HT + m + 1)

            ahead(PH["BA"], 0)
            act.wait_ge(sem("prep_ready"), PREP_BA)
            c.inc(A(ba_tmp[:, 0], bat[:, :, 0:HEADS], ACT.Tanh, scale=0.5))
            c.link(A(ba_tmp[:, 3], ba_tmp[:, 2], ACT.Exp))
            c.inc(A(ba_const[:, 0, :], ba_const[:, 0, :], ACT.Exp))
            c.link(A(ba_tmp[:, 4], ba_tmp[:, 3], ACT.Ln, bias=1.0))
            act.sem_inc(sem("table_ready"), 1)
            act.wait_ge(sem("gc_done"), 1)
            n16 = TT * HEADS
            c.inc(A(egc[:].rearrange("p t h -> p (t h)"), X[:, 3, 64:64 + n16], ACT.Exp))
            c.link(A(egl[:].rearrange("p t c h -> p (t c h)"), X[:, 3, 128:128 + 2 * n16], ACT.Exp))
            act.sem_inc(sem("table_ready"), 1)
            act.wait_ge(sem("prep_ready"), PREP_KEND)
            c.link(A(kend[:], kend[:], ACT.Exp))
            act.sem_inc(sem("table_ready"), 1)

            def half_tanh(dst, s, done, name=None):
                act.wait_ge(w_used, done)
                for n in range(TT):
                    ins = A(dst[:, n], acc[:, s, n], ACT.Tanh, scale=0.5)
                    if name is None:
                        ins.then_inc(acc_free[s], 1)
                    elif n == TT - 1:
                        ins.then_inc(sem(name), 1)

            def upad_copy(value):
                act.wait_ge(sem("uT_tr"), value)
                c.inc(nc.scalar.copy(upad[:, 0:2, TAPS - 1:], X[:, 0].rearrange("p (a b) -> p a b", a=2)))
                sig(nc.scalar.copy(upad[:, 2:4, TAPS - 1:], X[:, 1].rearrange("p (a b) -> p a b", a=2)), "upad_ready", value)

            def gate_tanh(kind, tile, ph, bl, i, value):
                act.wait_ge(acc_free[kind], freed(ph, bl, i))
                sig(A(tile[:], tile[:], ACT.Tanh, scale=0.5), f"gate{kind}_ready", value)

            ph = PH["GLU0"]
            for hl in range(ph.hn):
                ahead(ph, hl)
                if hl == 8:
                    half_tanh(sg, 0, used(ph, 7))
            ph = PH["GLU"]
            c.restart()
            with act.Fori(0, ph.iters) as i:
                for hl in range(ph.hn):
                    ahead(ph, hl, i)
                    if hl == 3:
                        act.wait_ge(sem("conv_done"), i + 1)
                        upad_copy(i + 1)
                    if hl == 9:
                        gate_tanh(0, gtA, ph, 0, i, i + 1)
                    if hl == 17:
                        gate_tanh(1, gtB, ph, 1, i, i + 1)
                    if hl == 24:
                        act.wait_ge(acc_free[1], freed(ph, -1, i))
                        half_tanh(sg, 0, used(ph, 23, i))
                c.restart()
            ph = PH["GT3"]
            for hl in range(ph.hn):
                ahead(ph, hl)
                if hl == 3:
                    act.wait_ge(sem("conv_done"), NJ)
                    upad_copy(NJ)
                if hl == 9:
                    gate_tanh(0, gtA, ph, 0, 0, NJ)
            gate_tanh(1, gtB, ph, 1, 0, NJ)

            ph = PH["ZB"]
            c.restart()

            def z_block(i, bl):
                act.wait_ge(acc_free[1 - bl], freed(ph, bl - 1, i))
                half_tanh(th0, bl, used(ph, 8 * bl + 7, i), "tanh_ready")

            def szT_copy(i, bl):
                act.wait_ge(sem("zT_tr"), i * 2 + (bl + 1))
                for q in range(2):
                    dst = szT[:, bass.ds(i * (2 * CT) + (bl * CT + 2 * q), 2)]
                    sig(A(dst, X[:, 2 + q].rearrange("p (a b) -> p a b", a=2), ACT.Copy, scale=0.25),
                        "szT_ready", i * 4 + (2 * bl + q + 1))

            with act.Fori(0, ph.iters) as i:
                for hl in range(ph.hn):
                    ahead(ph, hl, i)
                    if hl == 8:
                        z_block(i, 0)
                    if hl == 11:
                        szT_copy(i, 0)
                z_block(i, 1)
                szT_copy(i, 1)
                c.restart()

            def own(ph, hl, i, first):
                for n, (evac, _, pad, (_, conv_end), silu, back) in enumerate(OWN):
                    if hl == back + 1 and n < 2:
                        dst = (qtok, ktok)[n]
                        act.wait_ge(sem("tok_tr"), i * 3 + (n + 1))
                        if not first:
                            act.wait_ge(sem(("qT_tr", "kT_tr")[n]), i * 2)
                        c.inc(nc.scalar.copy(dst[:, 0].rearrange("p h d -> p (h d)"), X[:, 2]))
                        sig(nc.scalar.copy(dst[:, 1].rearrange("p h d -> p (h d)"), X[:, 3]), "tok_ready", i * 2 + (n + 1))
                        sig(A(cy[:].rearrange("p h n -> p (h n)"), dst[:].rearrange("p t h d -> p (t h d)"), ACT.Square),
                            "qk_sq", i * 2 + (n + 1))
                for n, (evac, _, pad, (_, conv_end), silu, back) in enumerate(OWN):
                    if hl == evac:
                        if n or not first:
                            act.wait_ge(sem("ch_tr"), i * 3 + n)
                        act.wait_ge(w_used, used(ph, 8 * n + 7, i))
                        for x in range(TT):
                            nc.scalar.copy(praw[:, x], acc[:, n % 2, x]).then_inc(acc_free[n % 2], 1)
                    if hl == pad:
                        act.wait_ge(sem("ch_tr"), i * 3 + (n + 1))
                        act.wait_ge(sem("conv4_done"), i * 3 + (n + 1))
                        b = OWN_BANKS[n]
                        c.inc(nc.scalar.copy(cpad[:, 0:2, SHORT - 1:], X[:, b].rearrange("p (a b) -> p a b", a=2)))
                        sig(nc.scalar.copy(cpad[:, 2:4, SHORT - 1:], X[:, b + 1].rearrange("p (a b) -> p a b", a=2)),
                            "cpad_ready", i * 3 + (n + 1))
                    if hl == silu:
                        act.wait_ge(sem("conv4_done"), i * 3 + (n + 2))
                        if n or not first:
                            act.wait_ge(sem("tok_tr"), i * 3 + n)
                        sig(A(cth[:].rearrange("p t n -> p (t n)"), cy[:].rearrange("p h n -> p (h n)"), ACT.Tanh, scale=0.5),
                            "cth_ready", i * 3 + (n + 1))

            def values(i):
                act.wait_ge(sem("tok_tr"), i * 3 + 3)
                act.wait_ge(sem("cols_ready"), i + 1)
                for x in range(TT):
                    for h in range(GH):
                        ins = A(vb[:, x, h], X[:, 2 + x, h * DK:(h + 1) * DK], ACT.Copy, scale=dcol[:, 6, x, h:h + 1])
                        if (x, h) != (TT - 1, GH - 1):
                            c.inc(ins)
                sig(ins, "vb_ready", i + 1)

            def z_tanh(ph, i):
                half_tanh(cth, 1, used(ph, 31, i), "tanh_ready")

            def bank_copies(dst, banks, tr, dv, name, per=2, at=0):
                for x in range(TT):
                    act.wait_ge(sem(tr), dv(per, at + x + 1))
                    sig(nc.scalar.copy(dst[:, x].rearrange("p h d -> p (h d)"), X[:, banks[x]]), name, dv(per, at + x + 1))

            def delta(hl, dv):
                if hl == 1:
                    bank_copies(kT, (0, 1), "kT_tr", dv, "kT_ready")
                if hl == 2:
                    for x in range(TT):
                        act.wait_ge(sem("decay_done"), dv(2, x + 1))
                        sig(A(decT[:, x].rearrange("p h i -> p (h i)"), X[:, x], ACT.Exp), "decT_ready", dv(2, x + 1))
                if hl == 4:
                    bank_copies(qT, (0, 1), "qT_tr", dv, "qT_ready")
                if hl == 5:
                    bank_copies(tinv, (2, 3), "tinv_tr", dv, "tinv_ready")
                if hl == 16:
                    bank_copies(us, (0, 1), "uw_done", dv, "uw_ready", 4)
                    bank_copies(wT, (2, 3), "uw_done", dv, "uw_ready", 4, 2)
                if hl in (18, 20, 22, 24):
                    n = (hl - 18) // 2
                    x, rows = n // 2, slice(n % 2 * SEQ_CHUNK, (n % 2 + 1) * SEQ_CHUNK)
                    act.wait_ge(sem("o_done"), dv(4, n + 1))
                    sig(nc.scalar.copy(otok[rows, x].rearrange("p h d -> p (h d)"), X[rows, 1]), "o_ready", dv(4, n + 1))
                if hl == 25:
                    sig(A(xs[:].rearrange("p t h d -> p (t h d)"), otok[:].rearrange("p t h d -> p (t h d)"), ACT.Square), "o_sq", dv(2, 1))
                if hl == 27:
                    act.wait_ge(sem("o_rstd"), dv(1, 1))
                    for x in range(TT):
                        for h in range(GH):
                            ins = A(otok[:, x, h], otok[:, x, h], ACT.Copy, scale=dcol[:, 10, x, h:h + 1])
                            if (x, h) != (TT - 1, GH - 1):
                                c.inc(ins)
                    sig(ins, "o_sq", dv(2, 2))
                if hl == 30:
                    act.wait_ge(sem("oT_tr"), dv(1, 1))
                    for q in range(2):
                        sig(A(oh[:, 2 * q:2 * q + 2], X[:, q].rearrange("p (a b) -> p a b", a=2), ACT.Copy, scale=pc2[:, R2_DN:R2_DN + 1]),
                            "oT_hi", dv(2, q + 1))

            ph = PH["QKVZ"]

            def ln_values(q):
                act.wait_ge(sem("ln_norm"), q + 1)
                if q:
                    act.wait_ge(sem("ln_lo"), q)
                for a in range(CT):
                    kt = CT * q + a
                    c.inc(A(lnt[:, a], y[:, kt], ACT.Tanh, scale=lnh[:, kt, 0:1], bias=lnh[:, kt, 1:2]))
                for a in range(CT):
                    kt = CT * q + a
                    ins = A(lnsq[:, a], y[:, kt], ACT.Identity, scale=pc[:, kt, R_LNG:R_LNG + 1], bias=pc[:, kt, R_LNB:R_LNB + 1])
                    if a < CT - 1:
                        c.inc(ins)
                    else:
                        sig(ins, "ln_value", q + 1)

            for hl in range(ph.hn):
                ahead(ph, hl)
                own(ph, hl, 0, True)
                if hl == 2:
                    act.wait_ge(sem("mean_done"), 1)
                    sig(nc.scalar.copy(rows[:], X[:, 0, 0:TOK]), "rows_ready", 1)
                if hl == 11:
                    act.wait_ge(sem("rstd_rows"), 1)
                    act.wait_ge(sem("ln_centered"), NJ)
                    sig(nc.scalar.copy(rows[:], X[:, 1, 0:TOK]), "rows_ready", 2)
                if 4 <= hl < 4 + NJ:
                    q = hl - 4
                    act.wait_ge(sem("ln_centered"), q + 1)
                    if q:
                        act.wait_ge(sem("ln_sq_used"), q)
                    sig(A(lnsq[:].rearrange("p a b -> p (a b)"), y[:, CT * q:CT * (q + 1)].rearrange("p a b -> p (a b)"), ACT.Square), "ln_sq", q + 1)
                if hl in (14, 18, 22, 26):
                    ln_values((hl - 14) // 4)
                if hl in (16, 20, 24, 28):
                    q = (hl - 16) // 4
                    act.wait_ge(sem("ln_out"), q + 1)
                    if q:
                        act.wait_ge(sem("uT_out"), 32 * q)
                    sig(nc.scalar.copy(luh[:].rearrange("p a b -> p (a b)"), lnt[:].rearrange("p a b -> p (a b)")), "ln_hi", q + 1)
            values(0)
            z_tanh(ph, 0)
            act.wait_ge(sem("uT_out"), 32 * NJ)
            c.restart()
            with act.Fori(1, NJ) as i:
                dv = lambda per, n: i * per + (n - per)
                for hl in range(ph.hn):
                    ahead(ph, hl, i)
                    delta(hl, dv)
                    own(ph, hl, i, False)
                values(i)
                z_tanh(ph, i)
                c.restart()

            dv = lambda per, n: (NJ - 1) * per + n
            ph = PH["YB"]
            for hl in range(ph.hn):
                ahead(ph, hl)
                delta(hl, dv)

            def transposed_hi(banks, dst, tr, tr_value, name, value, scale):
                act.wait_ge(sem(tr), tr_value)
                for q in range(2):
                    sig(A(dst(q), X[:, banks[q]].rearrange("p (a b) -> p a b", a=2), ACT.Copy, scale=scale), name, value - 1 + q)

            def merged_hi(dst, i, bl, base):
                transposed_hi((0, 1), lambda q: dst[:, bass.ds(i * (2 * CT) + (CT * bl + 2 * q), 2)],
                              "m_tr", i * 2 + (base + bl + 1), "m_hi", i * 4 + (2 * (base + bl) + 2), 0.5)

            ph = PH["YA"]
            c.restart()
            with act.Fori(0, ph.iters) as i:
                for hl in range(ph.hn):
                    ahead(ph, hl, i)
                    if hl == 10:
                        merged_hi(r2h, i, 0, OP_M)
                merged_hi(r2h, i, 1, OP_M)

            def evac_square(dst, ssq, scratch, ph, bl, i):
                s = (ph.b0 + bl) % 2
                act.wait_ge(w_used, used(ph, 8 * bl + 7, i))
                for x in range(TT):
                    c.link(nc.scalar.copy(dst(x), acc[:, s, x]))
                for x in range(TT):
                    A(scratch(x), dst(x), ACT.Square, accum_out=ssq(x)).then_inc(acc_free[s], 1)
                act.wait_ge(acc_free[s], freed(ph, bl, i))

            act.wait_ge(sem("p_tr"), 1)
            sig(nc.scalar.copy(pTh[:].rearrange("p a b -> p (a b)"), X[:, 2]), "p_hi", 1)
            ph = PH["MIX"]

            def mix_block(i, bl):
                evac_square(lambda x: mix[:, x, bass.ds(i * (2 * NB) + bl * NB, NB)],
                            lambda x: stat[:, bass.ds(i * 2 + (16 + NJ * x + bl), 1)],
                            lambda x: e[:, x, 0:NB], ph, bl, i)

            with act.Fori(0, ph.iters) as i:
                for hl in range(ph.hn):
                    ahead(ph, hl, i)
                    if hl == 8:
                        mix_block(i, 0)
                mix_block(i, 1)
                c.restart()

            ph = PH["PLEP"]
            for hl in range(ph.hn):
                ahead(ph, hl)
                if hl % 2:
                    act.wait_ge(w_used, used(ph, hl))
                    for s in range(2):
                        for x in range(TT):
                            nc.scalar.copy(e[:, x, (hl - 1 + s) * NB:(hl + s) * NB], acc[:, s, x]).then_inc(acc_free[s], 1)

            def stationary_block(dst, j, base, scale=lambda kt: 1.0):
                act.wait_ge(sem("op_tr"), base - OP_X1 + j + 1)
                bank0 = 2 * (j % 2)
                for q in range(2):
                    for a in range(2):
                        kt = CT * j + 2 * q + a
                        ins = A(dst[:, kt], X[:, bank0 + q, a * TOK:(a + 1) * TOK], ACT.Copy, scale=scale(kt))
                        if a == 0:
                            c.inc(ins)
                    sig(ins, "op_hi", 2 * (base + j) + q + 1)

            for j in range(NJ):
                stationary_block(r1h, j, OP_X1)

            ph = PH["PLEG"]
            c.restart()

            def ple_gate(i, bl):
                if bl == 1:
                    act.wait_ge(sem("row_sq"), i * 4 + (ROWS_X + 2))
                act.wait_ge(sem("p_hi"), 1)
                half_tanh(pth, bl, used(ph, 8 * bl + 7, i), "tanh_ready")

            def ple_squares(i, bl):
                act.wait_ge(sem("ple_gated"), i * 2 + (bl + 1))
                for x in range(TT):
                    sig(A(pth[:, x], e[:, x, bass.ds(i * (2 * NB) + bl * NB, NB)], ACT.Square,
                          accum_out=stat[:, bass.ds(i * 2 + (24 + NJ * x + bl), 1)]), "row_sq", i * 4 + (ROWS_X + 2 * bl + x + 1))

            with act.Fori(0, ph.iters) as i:
                for hl in range(ph.hn):
                    ahead(ph, hl, i)
                    if hl == 8:
                        ple_gate(i, 0)
                    if hl == 9:
                        ple_squares(i, 0)
                ple_gate(i, 1)
                ple_squares(i, 1)

            for j in range(NJ):
                act.wait_ge(sem("x2_ready"), j + 1)
                for x in range(TT):
                    sig(A(pth[:, x], mix[:, x, j * NB:(j + 1) * NB], ACT.Square,
                          accum_out=stat[:, 32 + NJ * x + j:33 + NJ * x + j]), "row_sq", ROWS_PLE + 2 * j + x + 1)
            for j in range(NJ):
                stationary_block(r2h, j, OP_H2, lambda kt: pc[:, kt, R_GPRE2:R_GPRE2 + 1])

            def latent(ph, tile, at):
                evac_square(lambda x: tile[:, x], lambda x: stat[:, at + x:at + x + 1],
                            lambda x: ost[:, x].rearrange("p h d -> p (h d)"), ph, 0, 0)

            for hl in range(PH["QA"].hn):
                ahead(PH["QA"], hl)
            ahead(PH["KR"], 0)
            act.wait_ge(sem("x2_out"), 16)
            latent(PH["QA"], qa_t, 44)
            gain = lambda kt: pc2[:, kt:kt + 1]
            for hl in range(PH["KVA"].hn):
                ahead(PH["KVA"], hl)
                if hl == 4:
                    stationary_block(r1h, 0, OP_LAT, gain)
            latent(PH["KVA"], kva_t, 46)
            stationary_block(r1h, 1, OP_LAT, gain)

            ph = PH["FC"]
            c.restart()

            def heads_evac(dst, bl, i, n=NB):
                act.wait_ge(w_used, used(ph, 2 * bl + 1, i))
                for x in range(TT):
                    nc.scalar.copy(dst(x), acc[:, bl % 2, x, 0:n]).then_inc(acc_free[bl % 2], 1)

            def tile_copies(dst, tr, name, i):
                act.wait_ge(sem(tr), i + 1)
                for q in range(2):
                    sig(nc.scalar.copy(dst[:, 2 * q:2 * q + 2].rearrange("p h n -> p (h n)"), X[:, q]), name, i * 2 + (q + 1))

            with act.Fori(0, ph.iters) as i:
                for hl in range(ph.hn):
                    ahead(ph, hl, i)
                    if hl == 2:
                        heads_evac(lambda x: qst[:, x, 0:NB], 0, i)
                    if hl == 4:
                        heads_evac(lambda x: qst[:, x, NB:GH * QH], 1, i, GH * QH - NB)
                    if hl == 6:
                        heads_evac(lambda x: kvst[:, x, 0], 2, i)
                        tile_copies(qTn, "qn_tr", "qTn_ready", i)
                    if hl == 8:
                        heads_evac(lambda x: kvst[:, x, 1], 3, i)
                    if hl == 10:
                        tile_copies(kTn, "kn_tr", "kTn_ready", i)
                    if hl == 14:
                        act.wait_ge(sem("smax_ready"), i + 1)
                        for h in range(GH):
                            for x, at in ((0, slice(0, P)), (1, slice(P, SCORES))):
                                ins = A(sc[:, h, at], sc[:, h, at], ACT.Exp, scale=ATT_SCALE, bias=nmx[:, x, h:h + 1], accum_out=den[:, x, h:h + 1])
                                if (h, x) != (GH - 1, 1):
                                    c.inc(ins)
                        sig(ins, "exp_ready", i + 1)
                    if hl == 16:
                        act.wait_ge(w_used, used(ph, 15, i))
                        for x in range(TT):
                            nc.scalar.copy(cg[:, x], acc[:, 0, x]).then_inc(acc_free[0], 1)
                    if hl == 17:
                        act.wait_ge(sem("pT_tr"), i + 1)
                        sig(nc.scalar.copy(pT[:, 0:2], X[:, 0:2, 0:SCORES]), "pT_ready0", i + 1)
                    if hl == 26:
                        act.wait_ge(sem("u2_tr"), i + 1)
                        c.inc(nc.scalar.copy(u2pad[:, 0:2, TAPS2 - 1:], X[:, 0].rearrange("p (a b) -> p a b", a=2)))
                        sig(nc.scalar.copy(u2pad[:, 2:4, TAPS2 - 1:], X[:, 1].rearrange("p (a b) -> p a b", a=2)), "u2_ready", i + 1)
                    if hl == 32:
                        half_tanh(zs, 0, used(ph, 31, i), "tanh_ready")
                act.wait_ge(sem("c_ready"), i + 1)
                act.wait_ge(sem("ct_free"), i + 1)
                sig(nc.scalar.copy(r1h[:, 2 * CT:3 * CT].rearrange("p a b -> p (a b)"), c3[:].rearrange("p a b -> p (a b)")), "c_hi", i + 1)
                c.restart()

            ph = PH["FZ"]

            def z_tanh2(i, bl):
                act.wait_ge(acc_free[1 - bl], freed(ph, bl - 1, i))
                act.wait_ge(sem("ct_free"), NJ + 1)
                half_tanh(thz, bl, used(ph, 8 * bl + 7, i), "tanh_ready")

            with act.Fori(0, ph.iters) as i:
                for hl in range(ph.hn):
                    ahead(ph, hl, i)
                    if hl == 8:
                        z_tanh2(i, 0)
                    if hl == 11:
                        merged_hi(r1h, i, 0, OP_ATTN)
                z_tanh2(i, 1)
                merged_hi(r1h, i, 1, OP_ATTN)

            ph = PH["FG"]
            with act.Fori(0, ph.iters) as i:
                for hl in range(ph.hn):
                    ahead(ph, hl, i)
                    if hl == 8:
                        half_tanh(thm[:, :, bass.ds(i * NB, NB)], 0, used(ph, 7, i))
                half_tanh(thc[:, :, bass.ds(i * NB, NB)], 1, used(ph, 15, i))

            ph = PH["YM"]
            with act.Fori(0, ph.iters) as i:
                for hl in range(ph.hn):
                    ahead(ph, hl, i)
            ph = PH["YC"]
            with act.Fori(0, ph.iters) as i:
                for hl in range(ph.hn):
                    ahead(ph, hl, i)
                    if hl == 10:
                        merged_hi(r1h, i, 0, OP_Y)
                merged_hi(r1h, i, 1, OP_Y)

            ph = PH["OUT"]

            def out_block(j):
                evac_square(lambda x: outst[:, x, j * NB:(j + 1) * NB], lambda x: stat[:, 52 + NJ * x + j:53 + NJ * x + j],
                            lambda x: thz[:, x], ph, j, 0)

            for hl in range(ph.hn):
                ahead(ph, hl)
                if hl and hl % 8 == 0:
                    out_block(hl // 8 - 1)
            out_block(NJ - 1)

        @block.vector
        def _(dve):
            c = Chain(dve, sem("dve_order"))
            V = nc.vector
            TC2 = TT * GH

            def sig(ins, name, value):
                ins.then_inc(sem(name), 1)
                dve.wait_ge(sem(name), value)

            def split(h, i=0, hn=0):
                if h >= len(HALVES):
                    return
                k, x, n = HALVES[h]
                dve.wait_ge(hi_ready, h + 1 + i * hn)
                V.tensor_tensor(w_lo[:, h % HL, 0:n], raw[:, k % RAW, x * HALF:x * HALF + n],
                                w_hi[:, h % HL, 0:n].bitcast(F32), ALU.subtract).then_inc(lo_ready, 1)

            def ahead(ph, hl, i=0):
                split(ph.h0 + hl + LEAD, i, ph.hn)

            def over(ap, n):
                return ap.unsqueeze(2).to_broadcast([P, ap.shape[1], n])

            def rep(ap, n):
                return ap.unsqueeze(1).to_broadcast([P, n, ap.shape[1]])

            th = lambda tile: tile[:].rearrange("p t h d -> p (t h) d")
            col = lambda k: dcol[:, k].rearrange("p t h -> p (t h)")
            flat = lambda tile: tile[:].rearrange("p a b -> p (a b)")
            banks = lambda b: X[:, b:b + 2].rearrange("p b (h d) -> p (b h) d", h=GH)

            def gated(dst, tanh, s, done, free):
                dve.wait_ge(w_used, done)
                for x in range(TT):
                    V.scalar_tensor_tensor(dst(x), tanh(x), 1.0, acc[:, s, x], ALU.add, ALU.mult).then_inc(acc_free[s], 1)
                dve.wait_ge(acc_free[s], free)

            dve.sem_inc(lo_ready, LO_CREDIT)
            for h in range(LEAD):
                split(h)

            c.inc(V.memset(upad[:, :, 0:TAPS - 1], 0.0))
            c.link(V.memset(uz[:, 0:TAPS - 1], 0.0))
            dve.sem_inc(sem("conv_done"), 1)

            dve.wait_ge(sem("row_sq"), ROWS_X)
            sig(V.tensor_tensor(stat[:, 0:2], stat[:, 40:42], stat[:, 42:44], ALU.add), "square_ready", SQ_X)

            dve.wait_ge(sem("small_landed"), 64)
            c.link(V.tensor_copy(pos_f[:], pos_i[:]))
            f = lambda k: rope_f[:, k].rearrange("p t n -> p (t n)")
            for x in range(TT):
                c.link(V.tensor_scalar(rope_f[:, 0, x], inv_f[:], pos_f[:, x:x + 1], None, ALU.mult))
            MAGIC = 1.5 * 2.0 ** 23
            c.link(V.tensor_scalar(f(1), f(0), 1.0 / TWO_PI, MAGIC, ALU.mult, ALU.add))
            c.link(V.tensor_scalar(f(1), f(1), -MAGIC, None, ALU.add))
            c.link(V.scalar_tensor_tensor(f(2), f(1), -TWO_PI_1, f(0), ALU.mult, ALU.add))
            c.link(V.scalar_tensor_tensor(f(2), f(1), -TWO_PI_2, f(2), ALU.mult, ALU.add))
            c.link(V.scalar_tensor_tensor(f(2), f(1), -TWO_PI_3, f(2), ALU.mult, ALU.add))
            c.link(V.tensor_scalar(f(2), f(2), PI_BELOW, -PI_BELOW, ALU.min, ALU.max))
            dve.sem_inc(sem("prep_ready"), 1)

            dve.wait_ge(sem("rows_tr"), 1)
            for b in range(2):
                c.inc(V.tensor_copy(pc[:, 8 * b:8 * (b + 1), :], X[:, b, 0:8 * N_ROWS].rearrange("p (k r) -> p k r", k=8)))
            c.link(V.tensor_copy(pc2[:], X[:, 2, 0:N_ROWS2]))
            c.inc(V.tensor_scalar(pc[:, :, R_DW:R_DW + TAPS], pc[:, :, R_DW:R_DW + TAPS], 0.5, None, ALU.mult))
            c.inc(V.tensor_scalar(lnh[:], pc[:, :, R_LNG:R_LNG + 2], 0.5, None, ALU.mult))
            c.link(V.tensor_scalar(pc2[:, R2_DN:R2_DN + 1], pc2[:, R2_DN:R2_DN + 1], 0.5, None, ALU.mult))
            dve.sem_inc(sem("prep_ready"), 1)

            def stationary_lo(hi, lo, kt, src, gain, ready, value):
                dve.wait_ge(sem(ready), value)
                for a in range(2):
                    ins = V.scalar_tensor_tensor(lo[:, kt + a], src[:, a * TOK:(a + 1) * TOK], gain(kt + a),
                                                 hi[:, kt + a].bitcast(F32), ALU.mult, ALU.subtract)
                    if a == 0:
                        c.inc(ins)
                return ins

            for m in range(KT // 2):
                sig(stationary_lo(r1h, r1l, 2 * m, X[:, m % 4], lambda kt: pc[:, kt, R_GPRE:R_GPRE + 1], "op_hi", 2 * OP_HT + m + 1), "op_lo", 2 * OP_HT + m + 1)

            dve.wait_ge(sem("table_ready"), TABLE_SIN)
            ct = cos_t[:].rearrange("p t n -> p (t n)")
            c.link(V.tensor_tensor(ct, f(3), f(3), ALU.mult))
            c.link(V.tensor_scalar(ct, ct, -2.0, 1.0, ALU.mult, ALU.add))

            ph = PH["BA"]
            ahead(ph, 0)
            dve.wait_ge(w_used, used(ph, 0))
            ba = X[:, 3, 0:TT * 2 * HEADS].rearrange("p (t n) -> p t n", t=TT)
            a_in = bat[:, :, HEADS:2 * HEADS]
            c.inc(V.tensor_copy(bat[:, :, 0:HEADS], ba[:, :, 0:HEADS]))
            c.link(V.tensor_tensor(a_in, ba[:, :, HEADS:2 * HEADS], rep(ba_const[:, 1, :], TT), ALU.add))
            c.link(V.tensor_scalar(ba_tmp[:, 1], a_in, -1.0, None, ALU.mult))
            c.inc(V.tensor_tensor(ba_tmp[:, 2], ba_tmp[:, 1], a_in, ALU.min))
            c.link(V.tensor_scalar(ba_tmp[:, 5], a_in, 0.0, None, ALU.max))
            dve.sem_inc(sem("prep_ready"), 1)
            dve.wait_ge(sem("table_ready"), TABLE_SOFTPLUS)
            c.link(V.tensor_scalar(beta[:], ba_tmp[:, 0], 0.5, 0.5, ALU.mult, ALU.add))
            c.inc(V.tensor_scalar(hbeta[:], beta[:], 0.5, None, ALU.mult))
            c.link(V.tensor_tensor(ba_tmp[:, 5], ba_tmp[:, 5], ba_tmp[:, 4], ALU.add))
            c.link(V.scalar_tensor_tensor(glog[:], ba_tmp[:, 5], -1.0, rep(ba_const[:, 0, :], TT), ALU.mult, ALU.mult))
            dve.sem_inc(sem("prep_ready"), 1)
            dve.wait_ge(sem("table_ready"), TABLE_EXP)
            n16 = TT * HEADS
            kf = kend[:].rearrange("p t h -> p (t h)")
            c.link(V.tensor_copy(kf, X[:, 3, 96:96 + n16]))
            c.link(V.tensor_tensor(kf, kf, X[:, 3, 64:64 + n16], ALU.subtract))
            dve.sem_inc(sem("prep_ready"), 1)

            def glu(ph, bl, i, sg_free, value):
                dve.wait_ge(acc_free[0], sg_free)
                if value is not None:
                    dve.wait_ge(sem("uT_tr"), value)
                gated(lambda x: u[:, x], lambda x: sg[:, x], 1, used(ph, 8 * bl + 7, i), freed(ph, bl, i))

            def gate_bias(kind, ph, bl, i, value):
                dve.wait_ge(sem("bias_landed"), 32 * value)
                dve.wait_ge(w_used, used(ph, 8 * bl + 7, i))
                for x in range(TT):
                    V.tensor_tensor((gtA, gtB)[kind][:, x], acc[:, kind, x], bgt[:, kind, :], ALU.add).then_inc(acc_free[kind], 1)

            def tap(k, cur, src, w, out):
                c.wait(tap.apart - 1)
                win = src[..., k:k + TOK]
                if k == 0:
                    ins = V.tensor_scalar(cur, win, w[:, 0:1], w[:, TAPS:TAPS + 1], ALU.mult, ALU.add)
                else:
                    ins = V.scalar_tensor_tensor(out if k == TAPS - 1 else cur, win, w[:, k:k + 1], cur, ALU.mult, ALU.add)
                c.inc(ins)

            def conv_steps(steps, slot, first, last):
                n, m = len(steps), last - first + 1
                if first <= slot <= last:
                    for k, a, i in steps[n * (slot - first) // m:n * (slot - first + 1) // m]:
                        tap(k, ycur[:, a], upad[:, a], pcw[:, a, :], y[:, bass.ds(i * CT + a, 1)].rearrange("p a n -> p (a n)"))

            ph = PH["GLU0"]
            for hl in range(ph.hn):
                ahead(ph, hl)
            glu(ph, 1, 0, freed(ph, 0), None)
            ph = PH["GLU"]
            c.restart()
            with dve.Fori(0, ph.iters) as i:
                steps = [(k, a, i) for k in range(TAPS) for a in range(CT)]
                tap.apart = CT
                for hl in range(ph.hn):
                    ahead(ph, hl, i)
                    if hl == 0:
                        c.link(V.tensor_copy(pcw[:], pc[:, bass.ds(i * CT, CT), 0:TAPS + 1]))
                    if hl == 3:
                        dve.wait_ge(sem("upad_ready"), i + 1)
                    if hl == 8:
                        gate_bias(0, ph, 0, i, i + 1)
                    if hl == 16:
                        gate_bias(1, ph, 1, i, i + 1)
                    conv_steps(steps, hl, 3, 31)
                c.wait()
                dve.sem_inc(sem("conv_done"), 1)
                glu(ph, 3, i, freed(ph, 2, i), i + 1)
                c.restart()
            ph = PH["GT3"]
            LAST = NJ - 1
            steps = [(k, a, LAST) for k in range(TAPS) for a in range(2)]
            for hl in range(ph.hn):
                ahead(ph, hl)
                if hl == 0:
                    c.link(V.tensor_copy(pcw[:], pc[:, LAST * CT:, 0:TAPS + 1]))
                if hl == 3:
                    dve.wait_ge(sem("upad_ready"), NJ)
                if hl == 8:
                    gate_bias(0, ph, 0, 0, NJ)
                tap.apart = 2
                conv_steps(steps, hl, 3, 15)
            c.wait()
            dve.sem_inc(sem("conv_done"), 1)

            gate_bias(1, ph, 1, 0, NJ)

            ph = PH["ZB"]
            c.restart()

            def z_gate(i, bl):
                dve.wait_ge(sem("tanh_ready"), i * 2 + (TANH_ZB + bl + 1))
                gated(lambda x: sz0[:, x], lambda x: th0[:, x], bl, used(ph, 8 * bl + 7, i), freed(ph, bl, i))

            with dve.Fori(0, ph.iters) as i:
                c.inc(V.tensor_copy(uz[:, TAPS - 1:], upad[:, bass.ds(i + 2, 1), TAPS - 1:].rearrange("p a n -> p (a n)")))
                c.link(V.tensor_copy(pcz[:], pc[:, bass.ds(i + (KT - 2), 1), 0:TAPS + 1].rearrange("p a n -> p (a n)")))
                tap.apart = 1
                for hl in range(ph.hn):
                    ahead(ph, hl, i)
                    if hl == 9:
                        z_gate(i, 0)
                    for k in range(TAPS * hl // 16, TAPS * (hl + 1) // 16):
                        tap(k, ycur[:, 0], uz[:], pcz[:], y[:, bass.ds(i + (KT - 2), 1)].rearrange("p a n -> p (a n)"))
                c.wait()
                dve.sem_inc(sem("conv_done"), 1)
                z_gate(i, 1)
                c.restart()

            ph = PH["QKVZ"]

            def own(ph, hl, i):
                if hl == 0:
                    for n in range(3):
                        c.link(V.tensor_copy(wq4[:, n], pc[:, bass.ds(i * GH, GH), R_SC + SHORT * n:R_SC + SHORT * (n + 1)]))
                for n, (_, _, _, (conv, conv_end), silu, back) in enumerate(OWN):
                    if hl == conv:
                        dve.wait_ge(sem("cpad_ready"), i * 3 + (n + 1))
                    if conv <= hl <= conv_end:
                        steps, m = [(k, h) for k in range(SHORT) for h in range(GH)], conv_end - conv + 1
                        for k, h in steps[16 * (hl - conv) // m:16 * (hl - conv + 1) // m]:
                            c.wait(GH - 1)
                            win, w = cpad[:, h, k:k + TOK], wq4[:, n, h, k:k + 1]
                            if k == 0:
                                c.inc(V.tensor_scalar(cy[:, h], win, w, None, ALU.mult))
                            else:
                                c.inc(V.scalar_tensor_tensor(cy[:, h], win, w, cy[:, h], ALU.mult, ALU.add))
                    if hl == conv_end:
                        c.wait()
                        dve.sem_inc(sem("conv4_done"), 1)
                    if hl == silu:
                        dve.wait_ge(sem("cth_ready"), i * 3 + (n + 1))
                        sig(V.scalar_tensor_tensor(flat(cth), flat(cth), 1.0, flat(cy), ALU.add, ALU.mult), "s_ready", i * 3 + (n + 1))
                    if hl == back + 2 and n < 2:
                        dve.wait_ge(sem("qk_sq"), i * 2 + (n + 1))
                        sig(V.tensor_reduce(col(8 + n), cy[:].rearrange("p a n -> p (a n)").rearrange("p (m d) -> p m d", d=DK), AX.X, ALU.add),
                            "qk_square", i * 2 + (n + 1))
                if hl == 31:
                    dve.wait_ge(sem("cols_ready"), i + 1)
                    c.link(V.tensor_tensor(th(ktok), th(ktok), over(col(2), DK), ALU.mult))
                    c.link(V.tensor_tensor(th(kb), th(ktok), over(col(3), DK), ALU.mult))
                    dve.sem_inc(sem("kb_ready"), 1)

            def z_silu(ph, i):
                dve.wait_ge(sem("tanh_ready"), i + (TANH_Z + 1))
                gated(lambda x: sz[:, x].rearrange("p h d -> p (h d)"), lambda x: cth[:, x], 1, used(ph, 31, i), freed(ph, 3, i))

            def delta(hl, dv):
                if hl == 0:
                    sig(V.tensor_tensor(th(gm), rep(tri_incl[:], TC2), over(col(7), P), ALU.mult), "gm_ready", dv(1, 1))
                if hl == 2:
                    c.link(V.tensor_tensor(th(qtok), th(qtok), over(col(0), DK), ALU.mult))
                    sig(V.tensor_tensor(th(qd), th(qtok), over(col(1), DK), ALU.mult), "q_scaled", dv(1, 1))
                if hl == 8:
                    c.inc(V.tensor_tensor(th(kbe), th(ktok), over(col(4), DK), ALU.mult))
                if hl == 10:
                    sig(V.tensor_tensor(th(ke), th(ktok), over(col(5), DK), ALU.mult), "k_scaled", dv(1, 1))
                    c.wait()
                if hl == 1:
                    dve.wait_ge(sem("kbT_tr"), dv(1, 1))
                    sig(V.tensor_copy(th(kbT), banks(2)), "kbT_ready", dv(1, 1))
                if hl == 3:
                    dve.wait_ge(sem("B_done"), dv(1, 1))
                    dve.wait_ge(sem("decT_ready"), dv(2, 2))
                    sig(V.tensor_tensor(th(bf), banks(2), th(decT), ALU.mult), "bf_ready", dv(1, 1))
                    c.inc(V.tensor_tensor(th(decT), th(decT), rep(tri_incl[:], TC2), ALU.mult))
                    c.link(V.tensor_tensor(th(xs), th(bf), rep(m1u[:], TC2), ALU.mult))
                    sig(V.tensor_tensor(th(uinv), rep(ident[:], TC2), th(xs), ALU.subtract), "uinv_ready", dv(1, 1))
                if hl == 4:
                    dve.wait_ge(sem("qdT_tr"), dv(1, 1))
                    sig(V.tensor_copy(th(qdT), banks(2)), "qdT_ready", dv(1, 1))
                if hl == 5:
                    dve.wait_ge(sem("qk_done"), dv(1, 1))
                    sig(V.tensor_tensor(th(qkT), banks(0), th(decT), ALU.mult), "qkT_ready", dv(1, 1))
                for l in range(LEVELS):
                    if hl == 6 + 2 * l:
                        dve.wait_ge(sem("lx_done"), dv(LEVELS, l + 1))
                        sig(V.tensor_tensor(th(xs), banks(0), rep(lvl[:, l, :], TC2), ALU.mult), "xs_ready", dv(LEVELS, l + 1))
                    if hl == 7 + 2 * l:
                        dve.wait_ge(sem("ly_done"), dv(LEVELS, l + 1))
                        s = 4 << l
                        late = lambda ap: ap.rearrange("p t h (b s) -> p (t h b) s", s=s)[:, :, s // 2:]
                        early = lambda ap: ap.rearrange("p t h (b s) -> p (t h b) s", s=s)[:, :, 0:s // 2]
                        bank4 = lambda b: X[:, b:b + 2].rearrange("p t (h d) -> p t h d", h=GH)
                        ins = V.tensor_tensor(late(uinv[:]), late(uinv[:]), late(bank4(0)), ALU.subtract)
                        if l < LEVELS - 1:
                            c.inc(ins)
                            ins = V.tensor_tensor(early(tinv[:]), early(tinv[:]), early(bank4(2)), ALU.subtract)
                        sig(ins, "inv_ready", dv(LEVELS, l + 1))
                        c.wait()
                for n in range(NCH):
                    x, rows = n // 2, slice(n % 2 * SEQ_CHUNK, (n % 2 + 1) * SEQ_CHUNK)
                    if hl == 17 + 2 * n and n:
                        dve.wait_ge(sem("scan_done"), dv(SCAN, 2 * n))
                        v = us[rows, x].rearrange("p h d -> p (h d)")
                        sig(V.tensor_tensor(v, v, X[rows, 0], ALU.subtract), "scan_ready", dv(SCAN, 2 * n))
                    if hl == 18 + 2 * n and n < NCH - 1:
                        dve.wait_ge(sem("scan_done"), dv(SCAN, 2 * n + 1))
                        if n == 0:
                            sig(V.tensor_copy(state[:].rearrange("p h d -> p (h d)"), X[:, 0]), "scan_ready", dv(SCAN, 1))
                        else:
                            for h in range(GH):
                                ins = V.scalar_tensor_tensor(state[:, h], state[:, h], degl[:, x, n % 2, h:h + 1],
                                                             X[:, 0, h * DK:(h + 1) * DK], ALU.mult, ALU.add)
                                if h < GH - 1:
                                    c.inc(ins)
                            sig(ins, "scan_ready", dv(SCAN, 2 * n + 1))
                            c.wait()
                if hl == 25:
                    dve.wait_ge(sem("o_sq"), dv(2, 1))
                    sig(V.tensor_reduce(col(11), th(xs), AX.X, ALU.add), "o_square", dv(1, 1))
                if hl == 28:
                    dve.wait_ge(sem("o_sq"), dv(2, 2))
                    sig(V.tensor_tensor(th(otok), th(otok), th(sz), ALU.mult), "o_gated", dv(1, 1))
                if hl == 30:
                    for q in range(2):
                        dve.wait_ge(sem("oT_hi"), dv(2, q + 1))
                        sig(V.scalar_tensor_tensor(ol[:, 2 * q:2 * q + 2], X[:, q].rearrange("p (a b) -> p a b", a=2), pc2[:, R2_DN:R2_DN + 1],
                                                   oh[:, 2 * q:2 * q + 2].bitcast(F32), ALU.mult, ALU.subtract), "oT_lo", dv(2, q + 1))

            dve.wait_ge(sem("gate_out"), 32 * NJ)
            c.link(V.memset(cpad[:, :, 0:SHORT - 1], 0.0))
            dve.sem_inc(sem("conv4_done"), 1)
            q4 = lambda tile, q: tile[:, CT * q:CT * (q + 1)]
            for hl in range(ph.hn):
                ahead(ph, hl)
                own(ph, hl, 0)
                if hl == 8:
                    dve.wait_ge(sem("ln_sq_used"), NJ)
                    sig(V.tensor_copy(var[:], X[:, 0:TT, 0]), "square_ready", SQ_LN)
                if hl == 9:
                    dve.wait_ge(sem("rstd_ready"), RSTD_LN)
                    for x in range(TT):
                        c.inc(V.tensor_scalar(rdiag[:, x], ident[:], var[:, x:x + 1], float(D), ALU.mult, ALU.mult))
                    c.wait()
                    dve.sem_inc(sem("rdiag_ready"), 1)
                if hl in (15, 19, 23, 27):
                    q = (hl - 15) // 4
                    dve.wait_ge(sem("ln_value"), q + 1)
                    sig(V.scalar_tensor_tensor(lnt[:], lnt[:], 1.0, lnsq[:], ALU.add, ALU.mult), "ln_silu", q + 1)
                if hl in (17, 21, 25, 29):
                    q = (hl - 17) // 4
                    dve.wait_ge(sem("ln_hi"), q + 1)
                    sig(V.tensor_tensor(lul[:], lnt[:], luh[:].bitcast(F32), ALU.subtract), "ln_lo", q + 1)
            z_silu(ph, 0)
            c.restart()
            with dve.Fori(1, NJ) as i:
                dv = lambda per, n: i * per + (n - per)
                for hl in range(ph.hn):
                    ahead(ph, hl, i)
                    delta(hl, dv)
                    own(ph, hl, i)
                z_silu(ph, i)
                c.restart()

            ph = PH["YB"]
            dv = lambda per, n: (NJ - 1) * per + n

            def branch_b(j):
                dve.wait_ge(sem(f"tile_landed{j % 2}"), 16 * (j // 2 + 1))
                gated(lambda x: gy[:, x, j * NB:(j + 1) * NB], lambda x: gth[j % 2][:, x].rearrange("p h d -> p (h d)"),
                      j % 2, used(ph, 8 * j + 7), freed(ph, j))
                dve.sem_inc(sem("gy_ready"), 1)

            for hl in range(ph.hn):
                ahead(ph, hl)
                delta(hl, dv)
                if hl and hl % 8 == 0:
                    branch_b(hl // 8 - 1)
            branch_b(NJ - 1)

            def merge(i, bl):
                dve.wait_ge(sem(f"tile_landed{bl}"), i * 16 + 48)
                gated(lambda x: mtmp[:, x], lambda x: gth[bl][:, x].rearrange("p h d -> p (h d)"), bl,
                      used(ph, 8 * bl + 7, i), freed(ph, bl, i))
                sig(V.tensor_tensor(mtmp, mtmp, gy[:, :, bass.ds(i * (2 * NB) + bl * NB, NB)], ALU.add), "m_ready", i * 2 + (OP_M + bl + 1))

            def merged_lo(hi, lo, i, bl, base):
                for q in range(2):
                    dve.wait_ge(sem("m_hi"), i * 4 + (2 * (base + bl) + q + 1))
                    kt = bass.ds(i * (2 * CT) + (CT * bl + 2 * q), 2)
                    sig(V.scalar_tensor_tensor(lo[:, kt], X[:, q].rearrange("p (a b) -> p a b", a=2), 0.5,
                                               hi[:, kt].bitcast(F32), ALU.mult, ALU.subtract), "m_lo", i * 4 + (2 * (base + bl) + q + 1))

            ph = PH["YA"]
            c.restart()
            with dve.Fori(0, ph.iters) as i:
                for hl in range(ph.hn):
                    ahead(ph, hl, i)
                    if hl == 8:
                        merge(i, 0)
                    if hl == 10:
                        merged_lo(r2h, r2l, i, 0, OP_M)
                merge(i, 1)
                merged_lo(r2h, r2l, i, 1, OP_M)

            dve.wait_ge(sem("p_hi"), 1)
            sig(V.tensor_tensor(flat(pTl), X[:, 2], flat(pTh).bitcast(F32), ALU.subtract), "p_lo", 1)
            ph = PH["MIX"]
            with dve.Fori(0, ph.iters) as i:
                for hl in range(ph.hn):
                    ahead(ph, hl, i)
            squares = lambda k: stat[:, k:k + TT * NJ].rearrange("p (t j) -> p t j", t=TT)
            dve.wait_ge(acc_free[1], freed(ph, 3))
            sig(V.tensor_reduce(stat[:, 4:6], squares(16), AX.X, ALU.add), "square_ready", SQ_MIX)

            ph = PH["PLEP"]
            for hl in range(ph.hn):
                ahead(ph, hl)
            dve.wait_ge(sem("rstd_ready"), RSTD_MIX)
            dve.wait_ge(sem("gains_landed"), 32)

            def lo_block(hi, lo, j, gain, base):
                for q in range(2):
                    sig(stationary_lo(hi, lo, CT * j + 2 * q, X[:, 2 * (j % 2) + q], gain, "op_hi", 2 * (base + j) + q + 1),
                        "op_lo", 2 * (base + j) + q + 1)

            for j in range(NJ):
                js = slice(j * NB, (j + 1) * NB)
                for x in range(TT):
                    c.inc(V.scalar_tensor_tensor(mix[:, x, js], mix[:, x, js], stat[:, 6 + x:7 + x], gpost[:, js], ALU.mult, ALU.mult))
                c.wait()
                dve.wait_ge(sem(f"tile_landed{j % 2}"), 64 + 16 * (j // 2 + 1))
                sig(V.tensor_tensor(mix[:, :, js], mix[:, :, js], xres[:, j % 2], ALU.add), "op_ready", j + 1)
                if j:
                    lo_block(r1h, r1l, j - 1, lambda kt: 1.0, OP_X1)
            lo_block(r1h, r1l, NJ - 1, lambda kt: 1.0, OP_X1)

            ph = PH["PLEG"]
            c.restart()

            def ple(i, bl):
                dve.wait_ge(sem("tanh_ready"), i * 2 + (TANH_PLE + bl + 1))
                at = bass.ds(i * (2 * NB) + bl * NB, NB)
                for x in range(TT):
                    ins = V.scalar_tensor_tensor(e[:, x, at], pth[:, x], 1.0, e[:, x, at], ALU.add, ALU.mult)
                    ins.then_inc(acc_free[bl], 1)
                dve.wait_ge(acc_free[bl], freed(ph, bl, i))
                dve.sem_inc(sem("ple_gated"), 1)

            with dve.Fori(0, ph.iters) as i:
                for hl in range(ph.hn):
                    ahead(ph, hl, i)
                    if hl == 9:
                        ple(i, 0)
                ple(i, 1)
            dve.wait_ge(sem("row_sq"), ROWS_PLE)
            sig(V.tensor_reduce(stat[:, 8:10], squares(24), AX.X, ALU.add), "square_ready", SQ_PLE)
            dve.wait_ge(sem("rstd_ready"), RSTD_PLE)
            for j in range(NJ):
                js = slice(j * NB, (j + 1) * NB)
                for x in range(TT):
                    c.inc(V.scalar_tensor_tensor(e[:, x, js], e[:, x, js], stat[:, 10 + x:11 + x], gple[:, js], ALU.mult, ALU.mult))
                c.wait()
                sig(V.tensor_tensor(mix[:, :, js], mix[:, :, js], e[:, :, js], ALU.add), "x2_ready", j + 1)
            dve.wait_ge(sem("row_sq"), ROWS_PLE + 2 * NJ)
            sig(V.tensor_reduce(stat[:, 12:14], squares(32), AX.X, ALU.add), "square_ready", SQ_X2)
            dve.wait_ge(sem("rstd_ready"), RSTD_X2)
            for j in range(NJ):
                js = slice(j * NB, (j + 1) * NB)
                c.inc(V.tensor_scalar(e[:, 0, js], mix[:, 0, js], stat[:, 14:15], None, ALU.mult))
                sig(V.tensor_scalar(e[:, 1, js], mix[:, 1, js], stat[:, 15:16], None, ALU.mult), "op_ready", OP_H2 - OP_X1 + j + 1)
                if j:
                    lo_block(r2h, r2l, j - 1, lambda kt: pc[:, kt, R_GPRE2:R_GPRE2 + 1], OP_H2)
            lo_block(r2h, r2l, NJ - 1, lambda kt: pc[:, kt, R_GPRE2:R_GPRE2 + 1], OP_H2)

            def rope(x1, x2, dst, cos, sin, t1, t2):
                c.inc(V.tensor_tensor(t1, x1, cos, ALU.mult))
                c.link(V.tensor_tensor(t2, x2, sin, ALU.mult))
                c.link(V.tensor_tensor(dst[..., 0:ROPE // 2], t1, t2, ALU.subtract))
                c.inc(V.tensor_tensor(t1, x1, sin, ALU.mult))
                c.link(V.tensor_tensor(t2, x2, cos, ALU.mult))
                c.link(V.tensor_tensor(dst[..., ROPE // 2:], t1, t2, ALU.add))

            def scaled(tile, at, rstd_value, value):
                dve.wait_ge(sem("rstd_ready"), rstd_value)
                c.inc(V.tensor_scalar(tile[:, 0], tile[:, 0], stat[:, at:at + 1], None, ALU.mult))
                sig(V.tensor_scalar(tile[:, 1], tile[:, 1], stat[:, at + 1:at + 2], None, ALU.mult), "op_ready", OP_LAT - OP_X1 + value)

            gain = lambda kt: pc2[:, kt:kt + 1]
            for hl in range(PH["QA"].hn):
                ahead(PH["QA"], hl)
            ahead(PH["KR"], 0)
            for hl in range(PH["KVA"].hn):
                ahead(PH["KVA"], hl)
                if hl == 1:
                    dve.wait_ge(sem("x2_out"), 16)
                    dve.wait_ge(w_used, used(PH["KR"], 0))
                    k = X[:, 3, 0:TT * ROPE].rearrange("p (t n) -> p t n", t=TT)
                    rope(k[:, :, 0:ROPE // 2], k[:, :, ROPE // 2:], qr[:, :, 0], cos_t[:], sin_t[:], rtmp[:, 0, :, 0], rtmp[:, 1, :, 0])
                    sig(V.tensor_copy(qr[:, :, 1], qr[:, :, 0]), "kr_ready", 1)
                if hl == 2:
                    scaled(qa_t, 48, RSTD_QA, 1)
                if hl == 3:
                    dve.wait_ge(sem("kr_tr"), 1)
                    sig(V.tensor_copy(krT[:], X[:, 3, 0:TOK]), "krT_ready", 1)
                if hl == 4:
                    lo_block(r1h, r1l, 0, gain, OP_LAT)
            scaled(kva_t, 50, RSTD_KV, 2)
            lo_block(r1h, r1l, 1, gain, OP_LAT)
            c.link(V.memset(u2pad[:, :, 0:TAPS2 - 1], 0.0))
            dve.wait_ge(sem("mask_ready"), MASK_CAUSAL)

            ph = PH["FC"]
            c.restart()
            with dve.Fori(0, ph.iters) as i:
                for hl in range(ph.hn):
                    ahead(ph, hl, i)
                    if hl == 0:
                        c.link(V.tensor_copy(wc2[:], pc[:, bass.ds(i * CT, CT), R_CW2:R_CW2 + TAPS2]))
                    if hl == 5:
                        dve.wait_ge(acc_free[1], freed(ph, 1, i))
                        for x in range(TT):
                            q = qst[:, x].rearrange("p (h d) -> p h d", h=GH)
                            rope(q[:, :, NOPE:NOPE + ROPE // 2], q[:, :, NOPE + ROPE // 2:], qr[:, x], rep(cos_t[:, x], GH), rep(sin_t[:, x], GH),
                                 rtmp[:, 0, x], rtmp[:, 1, x])
                        dve.sem_inc(sem("qr_ready"), 1)
                    if hl == 8:
                        dve.wait_ge(sem("qr_tr"), i + 1)
                        sig(V.tensor_copy(qrT[:].rearrange("p a n -> p (a n)"), X[:, 2]), "qrT_ready", i + 1)
                    if hl == 12:
                        dve.wait_ge(sem("sc_done"), i + 1)
                        c.link(V.tensor_tensor(sc[:], X[:, 0:GH, 0:SCORES], rep(amask[:], GH), ALU.add))
                    if hl == 13:
                        c.inc(V.tensor_reduce(mx[:, 0], sc[:, :, 0:P], AX.X, ALU.max))
                        c.link(V.tensor_reduce(mx[:, 1], sc[:, :, P:SCORES], AX.X, ALU.max))
                        sig(V.tensor_scalar(nmx[:], mx[:], -ATT_SCALE, None, ALU.mult), "smax_ready", i + 1)
                    if hl == 17:
                        dve.wait_ge(sem("pT_tr"), i + 1)
                        c.link(V.reciprocal(rec[:], den[:]))
                        sig(V.tensor_copy(pT[:, 2:4], X[:, 2:4, 0:SCORES]), "pT_ready1", i + 1)
                    if hl == 19:
                        dve.wait_ge(sem("pv_done"), i + 1)
                        dve.wait_ge(sem("ost_free"), i + 1)
                        sig(V.tensor_tensor(th(ost), banks(0), over(rec[:].rearrange("p t h -> p (t h)"), VD), ALU.mult), "ost_ready", i + 1)
                    if hl == 24:
                        dve.wait_ge(acc_free[0], freed(ph, 4, i))
                        dve.wait_ge(w_used, used(ph, 23, i))
                        for x in range(TT):
                            V.tensor_tensor(cg[:, x], cg[:, x], acc[:, 1, x], ALU.mult).then_inc(acc_free[1], 1)
                    if hl in (27, 28):
                        dve.wait_ge(sem("u2_ready"), i + 1)
                        steps = [(k, a) for k in range(TAPS2) for a in range(CT)]
                        for k, a in steps[6 * (hl - 27):6 * (hl - 26)]:
                            c.wait(CT - 1)
                            win, w = u2pad[:, a, k:k + TOK], wc2[:, a, k:k + 1]
                            if k == 0:
                                c.inc(V.tensor_scalar(c3[:, a], win, w, None, ALU.mult))
                            else:
                                c.inc(V.scalar_tensor_tensor(c3[:, a], win, w, c3[:, a], ALU.mult, ALU.add))
                    if hl == 33:
                        dve.wait_ge(sem("tanh_ready"), i + (TANH_ZC + 1))
                        gated(lambda x: zs[:, x], lambda x: zs[:, x], 0, used(ph, 31, i), freed(ph, 6, i))
                dve.wait_ge(w_used, used(ph, 39, i))
                for x in range(TT):
                    V.tensor_tensor(zs[:, x], zs[:, x], acc[:, 1, x], ALU.mult).then_inc(acc_free[1], 1)
                dve.wait_ge(sem("bz_tr"), i + 1)
                c.wait()
                for q in range(2):
                    cq = c3[:, 2 * q:2 * q + 2].rearrange("p a b -> p (a b)")
                    c.link(V.scalar_tensor_tensor(cq, X[:, 2 + q], 0.5, cq, ALU.mult, ALU.mult))
                dve.sem_inc(sem("c_ready"), 1)
                dve.wait_ge(sem("c_hi"), i + 1)
                sig(V.tensor_tensor(r1l[:, 2 * CT:3 * CT], c3[:], r1h[:, 2 * CT:3 * CT].bitcast(F32), ALU.subtract), "c_lo", i + 1)
                c.restart()

            ph = PH["FZ"]

            def attn_gate(i, bl):
                dve.wait_ge(sem("tanh_ready"), i * 2 + (TANH_ZM + bl + 1))
                dve.wait_ge(sem(f"tile_landed{bl}"), i * 16 + 112)
                gated(lambda x: thz[:, x], lambda x: thz[:, x], bl, used(ph, 8 * bl + 7, i), freed(ph, bl, i))
                sig(V.tensor_tensor(oin[:, bl], oin[:, bl], thz[:], ALU.mult), "m_ready", i * 2 + (OP_ATTN + bl + 1))

            with dve.Fori(0, ph.iters) as i:
                for hl in range(ph.hn):
                    ahead(ph, hl, i)
                    if hl == 9:
                        attn_gate(i, 0)
                    if hl == 11:
                        merged_lo(r1h, r1l, i, 0, OP_ATTN)
                attn_gate(i, 1)
                merged_lo(r1h, r1l, i, 1, OP_ATTN)

            ph = PH["FG"]
            with dve.Fori(0, ph.iters) as i:
                for hl in range(ph.hn):
                    ahead(ph, hl, i)
            ph = PH["YM"]

            def gated_attn(i, bl):
                at = thm[:, :, bass.ds(i * (2 * NB) + bl * NB, NB)]
                gated(lambda x: at[:, x], lambda x: at[:, x], bl, used(ph, 8 * bl + 7, i), freed(ph, bl, i))

            with dve.Fori(0, ph.iters) as i:
                for hl in range(ph.hn):
                    ahead(ph, hl, i)
                    if hl == 8:
                        gated_attn(i, 0)
                gated_attn(i, 1)
            ph = PH["YC"]

            def merge2(i, bl):
                at = bass.ds(i * (2 * NB) + bl * NB, NB)
                gated(lambda x: thz[:, x], lambda x: thc[:, x, at], bl, used(ph, 8 * bl + 7, i), freed(ph, bl, i))
                sig(V.tensor_tensor(thz[:], thz[:], thm[:, :, at], ALU.add), "m_ready", i * 2 + (OP_Y + bl + 1))

            with dve.Fori(0, ph.iters) as i:
                for hl in range(ph.hn):
                    ahead(ph, hl, i)
                    if hl == 8:
                        merge2(i, 0)
                    if hl == 10:
                        merged_lo(r1h, r1l, i, 0, OP_Y)
                merge2(i, 1)
                merged_lo(r1h, r1l, i, 1, OP_Y)

            ph = PH["OUT"]
            for hl in range(ph.hn):
                ahead(ph, hl)
            dve.wait_ge(acc_free[1], freed(ph, NJ - 1))
            sig(V.tensor_reduce(stat[:, 60:62], squares(52), AX.X, ALU.add), "square_ready", SQ_OUT)
            dve.wait_ge(sem("rstd_ready"), RSTD_OUT)
            dve.wait_ge(sem("gains_landed"), 48)
            dve.wait_ge(sem("x2_landed"), 16)
            for j in range(NJ):
                js = slice(j * NB, (j + 1) * NB)
                for x in range(TT):
                    c.inc(V.scalar_tensor_tensor(outst[:, x, js], outst[:, x, js], stat[:, 62 + x:63 + x], gpost2[:, js], ALU.mult, ALU.mult))
                c.wait()
                sig(V.tensor_tensor(outst[:, :, js], outst[:, :, js], x2r[:, :, js], ALU.add), "out_ready", j + 1)

        @block.tensor
        def _(pe):
            T = nc.tensor
            r1, r2 = (r1h, r1l), (r2h, r2l)

            def gemm(ph, hl, i, ops, kt0, bl, start, stop, n=NB, off=0, kts=2):
                h, b = ph.h0 + hl, ph.b0 + bl
                s = b % 2
                pe.wait_ge(lo_ready, LO_CREDIT + h + 1 + i * ph.hn)
                if start and b >= 2:
                    pe.wait_ge(acc_free[s], 2 * (b // 2) + i * ph.bn)
                for k in range(kts):
                    at = slice(k * NB + off, k * NB + off + n)
                    for x in range(TT):
                        xs_ = slice(x * P, (x + 1) * P)
                        for m, (a, w) in enumerate(((ops[0], w_hi), (ops[0], w_lo), (ops[1], w_hi))):
                            ins = T.matmul(acc[:, s, x, 0:n], a[:, kt0 + k, xs_], w[:, h % HL, at],
                                           start=start and k == 0 and m == 0, stop=stop and k == kts - 1 and m == 2)
                ins.then_inc(w_used, 1)

            def model_half(ph, hl, i, ops, hl0=0, bl0=0):
                bl, q = divmod(hl - hl0, 8)
                gemm(ph, hl, i, ops, 2 * q, bl0 + bl, q == 0, q == 7)

            def narrow(ph, ops, n, bank):
                pe.wait_ge(lo_ready, LO_CREDIT + ph.h0 + 1)
                for x in range(TT):
                    for kt in range(KT):
                        for m, (a, w) in enumerate(((ops[0], w_hi), (ops[0], w_lo), (ops[1], w_hi))):
                            ins = T.matmul(X[:, bank, x * n:(x + 1) * n], a[:, kt, x * P:(x + 1) * P],
                                           w[:, ph.h0 % HL, kt * n:(kt + 1) * n],
                                           start=kt == 0 and m == 0, stop=kt == KT - 1 and m == 2)
                ins.then_inc(w_used, 1)

            def channels_first(src, bank):
                for a in range(CT):
                    for x in range(TT):
                        ins = T.transpose(X[:, bank + a // 2, (a % 2) * TOK + x * P:(a % 2) * TOK + (x + 1) * P],
                                          src(x, a), ident[:])
                return ins

            def cols(tile):
                return lambda x, a: tile[:, x, a * P:(a + 1) * P]

            pe.sem_inc(w_used, HL)
            pe.wait_ge(sem("mask_ready"), MASK_IDENT)
            pe.wait_ge(sem("rows_landed"), 16 * 13)
            for kt in range(KT):
                T.transpose(X[:, kt // 8, kt % 8 * N_ROWS:(kt % 8 + 1) * N_ROWS], crow[:, kt * P:(kt + 1) * P], ident[0:N_ROWS, 0:N_ROWS])
            T.transpose(X[:, 2, 0:N_ROWS2], crow2[:], ident[0:N_ROWS2, 0:N_ROWS2]).then_inc(sem("rows_tr"), 1)

            pe.wait_ge(sem("xn_ready"), TT)
            pe.wait_ge(sem("prep_ready"), PREP_PC)
            for m in range(KT // 2):
                if m >= 4:
                    pe.wait_ge(sem("op_lo"), 2 * OP_HT + m - 3)
                for a in range(2):
                    for x in range(TT):
                        ins = T.transpose(X[:, m % 4, a * TOK + x * P:a * TOK + (x + 1) * P], xt[:, x, (2 * m + a) * P:(2 * m + a + 1) * P], ident[:])
                ins.then_inc(sem("xT_tr"), 1)
            pe.wait_ge(sem("op_lo"), 2 * (OP_HT + NJ))

            narrow(PH["BA"], r1, 2 * HEADS, 3)

            def log_decays():
                pe.wait_ge(sem("mask_ready"), MASK_TRI)
                pe.wait_ge(sem("prep_ready"), PREP_GLOG)
                for x in range(TT):
                    T.matmul(X[:, 3, 64 + x * HEADS:64 + (x + 1) * HEADS], tri_incl[:], glog[:, x], start=True, stop=True)
                    T.matmul(X[:, 3, 96 + x * HEADS:96 + (x + 1) * HEADS], same[:], glog[:, x], start=True, stop=True)
                    for n in range(2):
                        at = 128 + (2 * x + n) * HEADS
                        ins = T.matmul(X[:, 3, at:at + HEADS], half_ones[:, n, :], glog[:, x], start=True, stop=True)
                ins.then_inc(sem("gc_done"), 1)

            def u_transposed(ph, i):
                pe.wait_ge(acc_free[1], freed(ph, -1, i))
                channels_first(cols(u), 0).then_inc(sem("uT_tr"), 1)

            ph = PH["GLU0"]
            for hl in range(ph.hn):
                model_half(ph, hl, 0, r1)
                if hl == 1:
                    log_decays()
            ph = PH["GLU"]
            with pe.Fori(0, ph.iters) as i:
                for hl in range(ph.hn):
                    model_half(ph, hl, i, r1)
                    if hl == 2:
                        u_transposed(ph, i)
            ph = PH["GT3"]
            for hl in range(ph.hn):
                model_half(ph, hl, 0, r1)
                if hl == 2:
                    u_transposed(ph, 0)

            ph = PH["ZB"]
            with pe.Fori(0, ph.iters) as i:
                for hl in range(ph.hn):
                    model_half(ph, hl, i, r1)
                    if hl in (9, 15):
                        bl = hl // 15
                        pe.wait_ge(acc_free[bl], freed(ph, bl, i))
                        channels_first(cols(sz0), 2).then_inc(sem("zT_tr"), 1)

            ph = PH["QKVZ"]

            def own(ph, hl, i):
                for n, (_, to_channels, _, _, _, back) in enumerate(OWN):
                    if hl == to_channels:
                        pe.wait_ge(acc_free[n % 2], freed(ph, n, i))
                        if n == 1:
                            pe.wait_ge(sem("tok_ready"), i * 2 + 1)
                        channels_first(cols(praw), OWN_BANKS[n]).then_inc(sem("ch_tr"), 1)
                    if hl == back:
                        pe.wait_ge(sem("s_ready"), i * 3 + (n + 1))
                        pf = cth[:].rearrange("p a b -> p (a b)")
                        for x in range(TT):
                            for h in range(GH):
                                ins = T.transpose(X[:, 2 + x, h * DK:(h + 1) * DK], pf[:, h * TOK + x * P:h * TOK + (x + 1) * P], ident[:])
                        ins.then_inc(sem("tok_tr"), 1)

            PAIRS = [(x, h) for x in range(TT) for h in range(GH)]

            def per_head(bank, lhsT, rhs):
                for x, h in PAIRS:
                    ins = T.matmul(X[:, bank + x, h * P:(h + 1) * P], lhsT[:, x, h], rhs[:, x, h], start=True, stop=True)
                return ins

            def per_head_tr(bank, src, name=None):
                for x, h in PAIRS:
                    ins = T.transpose(X[:, bank + x, h * P:(h + 1) * P], src[:, x, h], ident[:])
                    if name is not None and h == GH - 1:
                        ins.then_inc(sem(name), 1)
                return ins

            def delta(hl, dv, i=None):
                if hl == 0:
                    pe.wait_ge(sem("kb_ready"), dv(1, 1))
                    per_head_tr(0, ktok, "kT_tr")
                    pe.wait_ge(sem("vb_ready"), dv(1, 1))
                    per_head_tr(2, kb).then_inc(sem("kbT_tr"), 1)
                if hl == 1:
                    pe.wait_ge(sem("kT_ready"), dv(2, 2))
                    pe.wait_ge(sem("gm_ready"), dv(1, 1))
                    for x in range(TT):
                        T.matmul(X[:, x], strict_lo[:], gm[:, x].rearrange("p h i -> p (h i)"), start=True, stop=True).then_inc(sem("decay_done"), 1)
                if hl == 2:
                    pe.wait_ge(sem("kbT_ready"), dv(1, 1))
                    per_head(2, kT, kbT).then_inc(sem("B_done"), 1)
                if hl == 3:
                    pe.wait_ge(sem("decT_ready"), dv(2, 2))
                    pe.wait_ge(sem("q_scaled"), dv(1, 1))
                    per_head_tr(0, qtok, "qT_tr")
                    pe.wait_ge(sem("bf_ready"), dv(1, 1))
                    per_head_tr(2, qd).then_inc(sem("qdT_tr"), 1)
                if hl == 4:
                    pe.wait_ge(sem("qT_ready"), dv(2, 2))
                    per_head(0, kT, qT).then_inc(sem("qk_done"), 1)
                    pe.wait_ge(sem("uinv_ready"), dv(1, 1))
                    pe.wait_ge(sem("qdT_ready"), dv(1, 1))
                    per_head_tr(2, uinv, "tinv_tr")
                for l in range(LEVELS):
                    if hl == 5 + 2 * l:
                        if l == 0:
                            pe.wait_ge(sem("qkT_ready"), dv(1, 1))
                            pe.wait_ge(sem("tinv_ready"), dv(2, 2))
                        else:
                            pe.wait_ge(sem("inv_ready"), dv(LEVELS, l))
                        per_head(0, bf, tinv).then_inc(sem("lx_done"), 1)
                    if hl == 6 + 2 * l:
                        pe.wait_ge(sem("xs_ready"), dv(LEVELS, l + 1))
                        ins = per_head(0, xs, uinv)
                        if l < LEVELS - 1:
                            if hl == 10 and i is not None:
                                pe.wait_ge(sem("cpad_ready"), i * 3 + 1)
                            ins = per_head(2, uinv, xs)
                        ins.then_inc(sem("ly_done"), 1)
                if hl == 15:
                    pe.wait_ge(sem("inv_ready"), dv(LEVELS, LEVELS))
                    pe.wait_ge(sem("k_scaled"), dv(1, 1))
                    for x, h in PAIRS:
                        ins = T.matmul(X[:, x, h * P:(h + 1) * P], uinv[:, x, h], vb[:, x, h], start=True, stop=True)
                        if h == GH - 1:
                            ins.then_inc(sem("uw_done"), 1)
                    for x, h in PAIRS:
                        ins = T.matmul(X[:, 2 + x, h * P:(h + 1) * P], kbe[:, x, h], uinv[:, x, h], start=True, stop=True)
                        if h == GH - 1:
                            ins.then_inc(sem("uw_done"), 1)
                for n in range(NCH):
                    x, rows = n // 2, slice(n % 2 * SEQ_CHUNK, (n % 2 + 1) * SEQ_CHUNK)
                    hs = [slice(h * DK, (h + 1) * DK) for h in range(GH)]
                    if hl == 16 + 2 * n and n:
                        pe.wait_ge(sem("scan_ready"), dv(SCAN, 2 * n - 1))
                        for h in range(GH):
                            ins = T.matmul(X[:, 0, hs[h]], wT[:, x, h], state[:, h], start=True, stop=True)
                        ins.then_inc(sem("scan_done"), 1)
                    if hl == 17 + 2 * n:
                        if n == 0:
                            pe.wait_ge(sem("uw_ready"), dv(4, 4))
                        else:
                            pe.wait_ge(sem("scan_ready"), dv(SCAN, 2 * n))
                            pe.wait_ge(sem("o_ready"), dv(NCH, n))
                        for h in range(GH):
                            if n:
                                T.matmul(X[:, 1, hs[h]], qdT[:, x, h], state[:, h], start=True, stop=False)
                            ins = T.matmul(X[:, 1, hs[h]], qkT[:, x, h], us[:, x, h], start=n == 0, stop=True)
                        ins.then_inc(sem("o_done"), 1)
                        if n < NCH - 1:
                            for h in range(GH):
                                ins = T.matmul(X[:, 0, hs[h]], ke[rows, x, h], us[rows, x, h], start=True, stop=True)
                            ins.then_inc(sem("scan_done"), 1)
                if hl == 29:
                    pe.wait_ge(sem("o_gated"), dv(1, 1))
                    channels_first(lambda x, a: otok[:, x, a], 0).then_inc(sem("oT_tr"), 1)

            for hl in range(ph.hn):
                model_half(ph, hl, 0, r1)
                if hl == 1:
                    pe.wait_ge(sem("conv_done"), NJ + 3)
                    for kt in range(KT):
                        ins = T.matmul(X[:, 0, 0:TOK], ones_mean[:], y[:, kt], start=kt == 0, stop=kt == KT - 1)
                    ins.then_inc(sem("mean_done"), 1)
                if 4 <= hl < 4 + NJ:
                    q = hl - 4
                    pe.wait_ge(sem("ln_sq"), q + 1)
                    for x in range(TT):
                        for a in range(CT):
                            ins = T.matmul(X[:, x, 0:1], lnsq[:, a, x * P:(x + 1) * P], ones_mean[:, 0:1],
                                           start=q == 0 and a == 0, stop=q == NJ - 1 and a == CT - 1)
                    ins.then_inc(sem("ln_sq_used"), 1)
                if hl == 10:
                    pe.wait_ge(sem("rdiag_ready"), 1)
                    for x in range(TT):
                        ins = T.matmul(X[:, 1, x * P:(x + 1) * P], ones_mean[:], rdiag[:, x], start=True, stop=True)
                    ins.then_inc(sem("rstd_rows"), 1)
                own(ph, hl, 0)
            with pe.Fori(1, NJ) as i:
                dv = lambda per, n: i * per + (n - per)
                for hl in range(ph.hn):
                    model_half(ph, hl, i, r1)
                    if hl == 9:
                        pe.wait_ge(sem("inv_ready"), dv(LEVELS, 2))
                    if hl == 16:
                        pe.wait_ge(sem("uw_ready"), dv(4, 4))
                    if hl == 25:
                        pe.wait_ge(sem("o_ready"), dv(NCH, NCH))
                    own(ph, hl, i)
                    delta(hl, dv, i)

            ph = PH["YB"]
            dv = lambda per, n: (NJ - 1) * per + n
            for hl in range(ph.hn):
                if hl < 8:
                    pe.wait_ge(sem(f"operand_landed{hl // 2}"), 32)
                model_half(ph, hl, 0, r1)
                delta(hl, dv)
            ph = PH["YA"]
            with pe.Fori(0, ph.iters) as i:
                for hl in range(ph.hn):
                    if hl < 8:
                        pe.wait_ge(sem(f"operand_landed{hl // 2}"), 64)
                    model_half(ph, hl, i, r1)
                    if hl in (9, 15):
                        pe.wait_ge(sem("m_ready"), i * 2 + (OP_M + hl // 15 + 1))
                        channels_first(cols(mtmp), 0).then_inc(sem("m_tr"), 1)

            pe.wait_ge(sem("p_landed"), 16)
            for a in range(PLE // P):
                for x in range(TT):
                    ins = T.transpose(X[:, 2, a * TOK + x * P:a * TOK + (x + 1) * P], ptok[:, x, a * P:(a + 1) * P], ident[:])
            ins.then_inc(sem("p_tr"), 1)
            pe.wait_ge(sem("m_lo"), 2 * (OP_M + NJ))
            ph = PH["MIX"]
            with pe.Fori(0, ph.iters) as i:
                for hl in range(ph.hn):
                    model_half(ph, hl, i, r2)
            ph = PH["PLEP"]
            pe.wait_ge(sem("p_lo"), 1)
            for hl in range(ph.hn):
                n, kt = divmod(hl, 2)
                pe.wait_ge(lo_ready, LO_CREDIT + ph.h0 + hl + 1)
                for s in range(2):
                    if kt == 0:
                        pe.wait_ge(acc_free[s], 2 * ((ph.b0 + 2 * n + s) // 2))
                    for x in range(TT):
                        for m, (a, w) in enumerate(((pTh, w_hi), (pTh, w_lo), (pTl, w_hi))):
                            ins = T.matmul(acc[:, s, x], a[:, kt, x * P:(x + 1) * P], w[:, (ph.h0 + hl) % HL, s * NB:(s + 1) * NB],
                                           start=kt == 0 and m == 0, stop=kt == 1 and m == 2)
                ins.then_inc(w_used, 1)

            def operand(tile, base):
                for j in range(NJ):
                    pe.wait_ge(sem("op_ready"), base - OP_X1 + j + 1)
                    if j >= 2:
                        pe.wait_ge(sem("op_lo"), 2 * (base + j - 1))
                    channels_first(lambda x, a: tile[:, x, j * NB + a * P:j * NB + (a + 1) * P], 2 * (j % 2)).then_inc(sem("op_tr"), 1)
                pe.wait_ge(sem("op_lo"), 2 * (base + NJ))

            operand(mix, OP_X1)
            ph = PH["PLEG"]
            with pe.Fori(0, ph.iters) as i:
                for hl in range(ph.hn):
                    model_half(ph, hl, i, r1)
            operand(e, OP_H2)

            ph = PH["QA"]
            for hl in range(ph.hn):
                model_half(ph, hl, 0, r2)
            narrow(PH["KR"], r2, ROPE, 3)
            ph = PH["KVA"]
            for hl in range(ph.hn):
                model_half(ph, hl, 0, r2)
                if hl == 2:
                    pe.wait_ge(sem("kr_ready"), 1)
                    for x in range(TT):
                        ins = T.transpose(X[:, 3, x * P:(x + 1) * P], qr[:, x, 0:2].rearrange("p a n -> p (a n)"), ident[:])
                    ins.then_inc(sem("kr_tr"), 1)
                if hl == 3:
                    pe.wait_ge(sem("op_ready"), OP_LAT - OP_X1 + 1)
                    channels_first(cols(qa_t), 0).then_inc(sem("op_tr"), 1)
            pe.wait_ge(sem("op_ready"), OP_LAT - OP_X1 + 2)
            pe.wait_ge(sem("krT_ready"), 1)
            channels_first(cols(kva_t), 2).then_inc(sem("op_tr"), 1)
            pe.wait_ge(sem("op_lo"), 2 * OP_LAT + 4)

            ph = PH["FC"]
            V0 = [slice(h % 2 * KVH + NOPE, (h % 2 + 1) * KVH) for h in range(GH)]
            with pe.Fori(0, ph.iters) as i:
                for hl in range(ph.hn):
                    if hl < 8:
                        bl, q = divmod(hl, 2)
                        wide = bl != 1
                        gemm(ph, hl, i, r1, (0 if bl < 2 else CT) + 2 * q, bl, q == 0, q == 1,
                             n=NB if wide else GH * QH - NB, off=0 if wide else 2 * NB - GH * QH)
                    else:
                        model_half(ph, hl, i, r2, 8, 4)
                    if hl == 5:
                        pe.wait_ge(acc_free[0], freed(ph, 0, i))
                        pe.wait_ge(acc_free[1], freed(ph, 1, i))
                        for h in range(GH):
                            for x in range(TT):
                                ins = T.transpose(X[:, h // 2, h % 2 * TOK + x * P:h % 2 * TOK + (x + 1) * P], qst[:, x, h * QH:h * QH + NOPE], ident[:])
                        ins.then_inc(sem("qn_tr"), 1)
                    if hl == 7:
                        pe.wait_ge(sem("qr_ready"), i + 1)
                        for a in range(GH // 2):
                            for x in range(TT):
                                ins = T.transpose(X[:, 2, a * TOK + x * P:a * TOK + (x + 1) * P], qr[:, x, 2 * a:2 * a + 2].rearrange("p a n -> p (a n)"), ident[:])
                        ins.then_inc(sem("qr_tr"), 1)
                    if hl == 9:
                        pe.wait_ge(acc_free[0], freed(ph, 2, i))
                        pe.wait_ge(acc_free[1], freed(ph, 3, i))
                        pe.wait_ge(sem("qTn_ready"), i * 2 + 2)
                        for h in range(GH):
                            for x in range(TT):
                                ins = T.transpose(X[:, h // 2, h % 2 * TOK + x * P:h % 2 * TOK + (x + 1) * P],
                                                  kvst[:, x, h // 2, h % 2 * KVH:h % 2 * KVH + NOPE], ident[:])
                        ins.then_inc(sem("kn_tr"), 1)
                    if hl == 11:
                        pe.wait_ge(sem("kTn_ready"), i * 2 + 2)
                        pe.wait_ge(sem("qrT_ready"), i + 1)
                        for h in range(GH):
                            half = slice(h % 2 * ROPE, (h % 2 + 1) * ROPE)
                            for x, keys, at in ((0, P, slice(0, P)), (1, TOK, slice(P, SCORES))):
                                T.matmul(X[:, h, at], qTn[:, h, x * P:(x + 1) * P], kTn[:, h, 0:keys], start=True, stop=False)
                                ins = T.matmul(X[:, h, at], qrT[half, h // 2, x * P:(x + 1) * P], krT[half, 0:keys], start=False, stop=True)
                        ins.then_inc(sem("sc_done"), 1)
                    if hl == 16:
                        pe.wait_ge(sem("exp_ready"), i + 1)
                        for h in range(GH):
                            for n in range(3):
                                ins = T.transpose(X[:, h, n * P:(n + 1) * P], sc[:, h, n * P:(n + 1) * P], ident[:])
                        ins.then_inc(sem("pT_tr"), 1)
                    if hl == 18:
                        pe.wait_ge(sem("pT_ready0"), i + 1)
                        pe.wait_ge(sem("pT_ready1"), i + 1)
                        for h in range(GH):
                            o = slice(h * VD, (h + 1) * VD)
                            T.matmul(X[:, 0, o], pT[:, h, 0:P], kvst[:, 0, h // 2, V0[h]], start=True, stop=True)
                            T.matmul(X[:, 1, o], pT[:, h, P:2 * P], kvst[:, 0, h // 2, V0[h]], start=True, stop=False)
                            ins = T.matmul(X[:, 1, o], pT[:, h, 2 * P:3 * P], kvst[:, 1, h // 2, V0[h]], start=False, stop=True)
                        ins.then_inc(sem("pv_done"), 1)
                    if hl == 25:
                        pe.wait_ge(acc_free[1], freed(ph, 5, i))
                        channels_first(cols(cg), 0).then_inc(sem("u2_tr"), 1)
                    if hl == 39:
                        pe.wait_ge(acc_free[1], freed(ph, 7, i))
                        channels_first(cols(zs), 2).then_inc(sem("bz_tr"), 1)

            ph = PH["FZ"]
            with pe.Fori(0, ph.iters) as i:
                for hl in range(ph.hn):
                    model_half(ph, hl, i, r2)
                    if hl in (10, 15):
                        bl = hl // 15
                        pe.wait_ge(sem("m_ready"), i * 2 + (OP_ATTN + bl + 1))
                        channels_first(cols(oin[:, bl]), 0).then_inc(sem("m_tr"), 1)
            ph = PH["FG"]
            with pe.Fori(0, ph.iters) as i:
                for hl in range(ph.hn):
                    model_half(ph, hl, i, r2)

            ph = PH["YM"]
            pe.wait_ge(sem("m_lo"), 2 * (OP_ATTN + NJ))
            with pe.Fori(0, ph.iters) as i:
                for hl in range(ph.hn):
                    model_half(ph, hl, i, r1)
            ph = PH["YC"]
            with pe.Fori(0, ph.iters) as i:
                for hl in range(ph.hn):
                    if hl < 8:
                        pe.wait_ge(sem(f"operand_landed{hl // 2}"), 96)
                    model_half(ph, hl, i, r2)
                    if hl in (9, 15):
                        pe.wait_ge(sem("m_ready"), i * 2 + (OP_Y + hl // 15 + 1))
                        channels_first(cols(thz), 0).then_inc(sem("m_tr"), 1)
            ph = PH["OUT"]
            pe.wait_ge(sem("m_lo"), 2 * (OP_Y + NJ))
            for hl in range(ph.hn):
                model_half(ph, hl, 0, r1)


_INS = ["x", "p", "g_pre", "w_in", "b_gate", "w_conv_qkv", "a_log", "dt_bias", "g_dn_out", "w_dw", "b_dw", "ln_g", "ln_b",
        "w_br_a", "w_br_b", "w_out", "g_post", "w_ple_gate", "w_ple_proj", "g_ple", "positions_2", "pre_norm_g_2", "w_in_2",
        "q_a_norm_g_2", "w_q_b_2", "kv_a_norm_g_2", "w_kv_b_2", "conv_w_2", "w_o_mla_2", "w_o_conv_2", "w_out_2", "post_norm_g_2"]


def kernel(**inputs):
    import numpy as np
    import concourse.bacc as bacc
    from concourse.bass_utils import run_bass_kernel_spmd as run

    nc = bacc.Bacc("TRN2", target_bir_lowering=False, num_devices=1)
    arrays = {name: np.ascontiguousarray(inputs[name]) for name in _INS}
    arrays["inv_freq"] = (ROPE_THETA ** (-np.arange(0, ROPE, 2, dtype=np.float32) / ROPE)).astype(np.float32)[None]
    t = {name: nc.dram_tensor(f"in_{name}", a.shape, mybir.dt.from_np(a.dtype), kind="ExternalInput").ap() for name, a in arrays.items()}
    out = nc.dram_tensor("out", (1, TOK, D), F32, kind="ExternalOutput").ap()
    build_layer(nc, t, out)
    r = run(nc, [{f"in_{name}": a for name, a in arrays.items()}], core_ids=[0])
    return r.results[0]["out"]
```

```python
from contextlib import ExitStack

import concourse.bass as bass
from concourse import mybir

ALU = mybir.AluOpType
ACT = mybir.ActivationFunctionType
AX = mybir.AxisListType
F32 = mybir.dt.float32
F32R = mybir.dt.float32r
I32 = mybir.dt.int32

P = 128
TOK = 256
TT = TOK // P
D = 2048
KT = D // P
NB = 512
NJ = D // NB
CT = NB // P
CHUNK_KT = 4
CHUNK = CHUNK_KT * NB
HALF = CHUNK // 2
RAW = 4
HL = 4
LEAD = 3
LO_CREDIT = 2 * RAW
EPS = 1e-6
OWN_BYTES = 50 * 1024

HEADS, DK = 16, 128
SEQ_CHUNK = 64
GH = 4
TAPS = 31
LEVELS = 5
NCH = TOK // SEQ_CHUNK
SCAN = 2 * (NCH - 1)
SHORT = 4
PLE = 256
C_QKV = 0
C_Z = 3 * D
C_BA = C_Z + D
C_GLU = C_BA + 2 * HEADS
C_ZB = C_GLU + 2 * D
C_GATE = C_ZB + D

LORA = 512
NOPE, ROPE, VD = 128, 64, 128
QH = NOPE + ROPE
KVH = NOPE + VD
TAPS2 = 3
SCORES = 3 * P
C2_QA = 0
C2_KV = LORA
C2_KR = 2 * LORA
C2_ZM = C2_KR + ROPE
C2_CIN = C2_ZM + D
C2_BG = C2_CIN + D
C2_CG = C2_BG + D
C2_ZC = C2_CG + D
C2_GM = C2_ZC + D
C2_GC = C2_GM + D
ROPE_THETA = 10000.0
TWO_PI = 6.283185307179586
TWO_PI_1, TWO_PI_2, TWO_PI_3 = 6.28125, 0.001934051513671875, 1.255665914356996e-06
PI_BELOW = 3.1415925
ATT_SCALE = (NOPE + ROPE) ** -0.5

R_DW, R_BDW, R_LNG, R_LNB, R_GPRE, R_GPRE2, R_CW2, R_SC = 0, 31, 32, 33, 34, 35, 36, 39
N_ROWS = R_SC + 3 * SHORT
SQ_X, SQ_LN, SQ_MIX, SQ_PLE, SQ_X2, SQ_OUT = range(1, 7)
RSTD_X, RSTD_LN, RSTD_MIX, RSTD_PLE, RSTD_X2, RSTD_QA, RSTD_KV, RSTD_OUT = range(1, 9)
OP_HT, OP_X1, OP_H2, OP_LAT = 0, NJ, 2 * NJ, 3 * NJ
OP_M, OP_ATTN, OP_Y = 0, NJ, 2 * NJ
ROWS_X = 2 * TT
ROWS_PLE = ROWS_X + TT * NJ
TANH_ZB, TANH_Z, TANH_PLE, TANH_ZC, TANH_ZM = 0, NJ, 2 * NJ, 3 * NJ, 4 * NJ
MASK_IDENT, MASK_TRI, MASK_LVL, MASK_CAUSAL = range(1, 5)
PREP_ANGLE, PREP_PC, PREP_NARROW, PREP_BA, PREP_GLOG, PREP_KEND = range(1, 7)
TABLE_SIN, TABLE_SOFTPLUS, TABLE_EXP = range(1, 4)
R2_QA, R2_KV, R2_DN, N_ROWS2 = 0, 4, 8, 9

OWN = ((8, 9, 10, (11, 14), 15, 16), (16, 18, 19, (20, 22), 23, 24), (24, 25, 26, (27, 29), 30, 31))
OWN_BANKS = (2, 2, 0)
LN_TANH, LN_SILU, LN_HI, LN_LO = (12, 16, 20, 24), (13, 17, 21, 25), (14, 18, 22, 26), (15, 19, 23, 27)


class Phase:

    def __init__(self, k0, h0, b0, iters, halves, blocks):
        self.k0, self.h0, self.b0, self.iters = k0, h0, b0, iters
        self.kn, self.hn, self.bn = len(halves), sum(n for n, _ in halves), blocks


def plan():
    full = (2, HALF)
    order = [
        ("BA", 1, [(1, KT * 2 * HEADS)], 0),
        ("GLU0", 1, [full] * 8, 2),
        ("GLU", 3, [full] * 16, 4),
        ("GT3", 1, [full] * 8, 2),
        ("ZB", 1, [full] * 16, 4),
        ("QKVZ", 4, [full] * 16, 4),
        ("YB", 1, [full] * 16, 4),
        ("YA", 1, [full] * 16, 4),
        ("MIX", 1, [full] * 16, 4),
        ("PLEP", 1, [full] * 2, 4),
        ("PLEG", 1, [full] * 16, 4),
        ("QA", 1, [full] * 4, 1),
        ("KR", 1, [(1, KT * ROPE)], 0),
        ("KVA", 1, [full] * 4, 1),
        ("FC", 4, [full] * 20, 8),
        ("FG", 4, [full] * 8, 2),
        ("FZ", 1, [full] * 16, 4),
        ("YM", 1, [full] * 16, 4),
        ("YC", 1, [full] * 16, 4),
        ("OUT", 1, [full] * 16, 4),
    ]
    phases, halves, k, b = {}, [], 0, 0
    for name, iters, chunks, blocks in order:
        phases[name] = Phase(k, len(halves), b, iters, chunks, blocks)
        for _ in range(iters):
            for n, size in chunks:
                halves += [(k, x, size) for x in range(n)]
                k += 1
            b += blocks
    return phases, halves


def at_block(hl, lag):
    return (hl - lag) // 8 - 1 if hl >= 8 + lag and (hl - lag) % 8 == 0 else None


class Chain:

    def __init__(self, eng, sem):
        self.eng, self.sem, self.n = eng, sem, 0

    def inc(self, ins):
        ins.then_inc(self.sem, 1)
        self.n += 1

    def wait(self, lag=0):
        if self.n > lag:
            self.eng.wait_ge(self.sem, self.n - lag)

    def link(self, ins):
        self.inc(ins)
        self.wait()

    def step(self):
        self.eng.sem_inc(self.sem, 1)
        self.n += 1
        self.wait()

    def restart(self):
        if self.n:
            self.step()
            self.eng.sem_clear(self.sem)
        self.n = 0


def build_layer(nc, t, out):
    PH, HALVES = plan()
    ctx = ExitStack()
    sems = {}

    def sem(name):
        if name not in sems:
            sems[name] = ctx.enter_context(nc.semaphore(name))
        return sems[name]

    def sb(name, shape, dt=F32, stack=ctx):
        return stack.enter_context(nc.sbuf_tensor(name, shape, dt))

    def dram(name, shape, dt=F32):
        return nc.dram_tensor(name, shape, dt, kind="Internal").ap()

    def kp(w):
        return w.rearrange("(kt p) n -> p kt n", p=P)

    w_in, w_in2 = kp(t["w_in"][0]), kp(t["w_in_2"])
    w_br_a, w_br_b, w_out = kp(t["w_br_a"][0]), kp(t["w_br_b"][0]), kp(t["w_out"][0])
    w_ple_gate, w_ple_proj = kp(t["w_ple_gate"][0]), kp(t["w_ple_proj"][0])
    w_q_b, w_kv_b = kp(t["w_q_b_2"]), kp(t["w_kv_b_2"])
    w_o_mla, w_o_conv, w_out2 = kp(t["w_o_mla_2"]), kp(t["w_o_conv_2"]), kp(t["w_out_2"])
    tok = lambda a: a.rearrange("(t p) n -> p t n", p=P)

    gate_dram = dram("gate_spill", (2, NJ, P, TT * NB))
    uT_dram = dram("conv_branch_spill", (2, NJ, P, CT * TOK), F32R)
    oT_dram = dram("delta_branch_spill", (2, NJ, P, CT * TOK), F32R)
    cT_dram = dram("short_conv_spill", (2, NJ, P, CT * TOK), F32R)
    o_dram = dram("attention_spill", (NJ, P, TT * NB))
    x2_dram = dram("residual_spill", (TOK, D))

    with ctx:
        raw = sb("raw", [P, RAW, CHUNK])
        w_hi = sb("w_hi", [P, HL, HALF], F32R)
        w_lo = sb("w_lo", [P, HL, HALF], F32R)
        r1h, r1l = sb("r1h", [P, KT, TOK], F32R), sb("r1l", [P, KT, TOK], F32R)
        ident = sb("ident", [P, P])
        tri_incl = sb("tri_incl", [P, P])
        strict_lo = sb("strict_lo", [P, P])
        same = sb("same", [P, P])
        half_ones = sb("half_ones", [P, 2, P])
        lvl = sb("lvl", [P, 5, P])
        m1u = sb("m1u", [P, P])
        ones_mean = sb("ones_mean", [P, P])
        pc = sb("pc", [P, KT, N_ROWS])
        pc2 = sb("pc2", [P, N_ROWS2])
        lnh = sb("lnh", [P, KT, 2])
        neg_half = sb("neg_half", [P, 1])
        beta = sb("beta", [P, TT, HEADS])
        hbeta = sb("hbeta", [P, TT, HEADS])
        glog = sb("glog", [P, TT, HEADS])
        egc = sb("egc", [P, TT, HEADS])
        kend = sb("kend", [P, TT, HEADS])
        egl = sb("egl", [P, TT, 2, HEADS])
        cos_t, sin_t = sb("cos_t", [P, TT, ROPE // 2]), sb("sin_t", [P, TT, ROPE // 2])
        stat = sb("stat", [P, 64])
        arena_at = nc.sbuf_base

        with ExitStack() as st:
            s1 = lambda n, shape, dt=F32: sb(n, shape, dt, st)
            upad = s1("upad", [P, CT, TAPS - 1 + TOK])
            ycur = s1("ycur", [P, CT, TOK])
            sg = s1("sg", [P, TT, NB])
            u = s1("u", [P, TT, NB])
            gtA, gtB = s1("gtA", [P, TT, NB]), s1("gtB", [P, TT, NB])
            bgt = s1("bgt", [P, 2, NB])
            th0 = s1("th0", [P, TT, NB])
            sz0 = s1("sz0", [P, TT, NB])
            narrow_t = sz0[:, 0, 0:TOK]
            pcw = s1("pcw", [P, CT, TAPS + 1])
            bat = s1("bat", [P, TT, 2 * HEADS])
            ba_tmp = s1("ba_tmp", [P, 6, TT, HEADS])
            ba_const = s1("ba_const", [P, 2, HEADS])
            rope_f = s1("rope_f", [P, 6, TT, ROPE // 2])
            pos_i = s1("pos_i", [P, TT], I32)
            pos_f = s1("pos_f", [P, TT])
            inv_f = s1("inv_f", [P, ROPE // 2])
            own_end = delta_at = arena_at + OWN_BYTES
            s1("pad_to_delta", [P, (own_end - nc.sbuf_base) // 4])
            with ExitStack() as st2:
                xt = sb("xt", [P, TT, D], F32, st2)
                crow = sb("crow", [N_ROWS, D], F32, st2)
                crow2 = sb("crow2", [N_ROWS2, P], F32, st2)
            y = s1("y", [P, KT, TOK])
            szT = s1("szT", [P, KT, TOK])
            lnsq = s1("lnsq", [P, CT, TOK])
            lnt = s1("lnt", [P, CT, TOK])
            luh, lul = s1("luh", [P, CT, TOK], F32R), s1("lul", [P, CT, TOK], F32R)
            var = s1("var", [P, TT])
            rows = s1("rows", [P, TOK])
            rdiag = s1("rdiag", [P, TT, P])

        with ExitStack() as st:
            s1 = lambda n, shape, dt=F32: sb(n, shape, dt, st)
            praw = s1("praw", [P, TT, NB])
            cpad = s1("cpad", [P, GH, SHORT - 1 + TOK])
            cy = s1("cy", [P, GH, TOK])
            cth = s1("cth", [P, TT, NB])
            qtok, qd = s1("qtok", [P, TT, GH, DK]), s1("qd", [P, TT, GH, DK])
            ktok, kb = s1("ktok", [P, TT, GH, DK]), s1("kb", [P, TT, GH, DK])
            kbe, ke = s1("kbe", [P, TT, GH, DK]), s1("ke", [P, TT, GH, DK])
            vb = s1("vb", [P, TT, GH, DK])
            sz = s1("sz", [P, TT, GH, DK])
            wq4 = s1("wq4", [P, 3, GH, SHORT])
            dcol = s1("dcol", [P, 12, TT, GH])
            degl = s1("degl", [P, TT, 2, GH])
            assert nc.sbuf_base <= own_end, (nc.sbuf_base, own_end)
            s1("pad_to_delta2", [P, max(1, (own_end - nc.sbuf_base) // 4)])
            kT, kbT = s1("kT", [P, TT, GH, P]), s1("kbT", [P, TT, GH, P])
            qT, qdT = s1("qT", [P, TT, GH, P]), s1("qdT", [P, TT, GH, P])
            decT = s1("decT", [P, TT, GH, P])
            xs = s1("xs", [P, TT, GH, P])
            bf = s1("bf", [P, TT, GH, P])
            qkT = s1("qkT", [P, TT, GH, P])
            uinv = s1("uinv", [P, TT, GH, P])
            state = s1("state", [P, GH, DK])
            oh, ol = s1("oh", [P, GH, TOK], F32R), s1("ol", [P, GH, TOK], F32R)
            gm, tinv, us, wT, otok = xs, kb, qd, kbT, qT
        with ExitStack() as st:
            gy = sb("gy", [P, TT, D], F32, st)
            assert nc.sbuf_base <= arena_at + 4 * 4 * 1024 + 64

        tail_at = delta_at + 2 * KT * TOK * 4
        with ExitStack() as st:
            s1 = lambda n, shape, dt=F32: sb(n, shape, dt, st)
            mix = s1("mix", [P, TT, D])
            e = s1("e", [P, TT, D])
            xres = s1("xres", [P, 2, TT, NB])
            pth = s1("pth", [P, TT, NB])
            pTh, pTl = s1("pTh", [P, PLE // P, TOK], F32R), s1("pTl", [P, PLE // P, TOK], F32R)
            s1("pad_d", [P, max(1, (own_end - nc.sbuf_base) // 4)])
            r2h, r2l = s1("r2h", [P, KT, TOK], F32R), s1("r2l", [P, KT, TOK], F32R)
            gpost, gple = s1("gpost", [P, D]), s1("gple", [P, D])
        ptok = pth[:, 0].rearrange("p (t n) -> p t n", t=TT)
        with ExitStack() as st:
            s1 = lambda n, shape, dt=F32: sb(n, shape, dt, st)
            qst = s1("qst", [P, TT, GH * QH])
            kvst = s1("kvst", [P, TT, 2, NB])
            qr = s1("qr", [P, TT, GH, ROPE])
            qTn, qrT = s1("qTn", [P, GH, TOK]), s1("qrT", [P, GH // 2, TOK])
            kTn = s1("kTn", [P, GH, TOK])
            sc = s1("sc", [P, GH, SCORES])
            pT = s1("pT", [P, GH, SCORES])
            ost = s1("ost", [P, TT, GH, VD])
            c3 = s1("c3", [P, CT, TOK])
            krT = s1("krT", [P, TOK])
            amask = s1("amask", [P, SCORES])
            mx, nmx, den, rec = [s1(n, [P, TT, GH]) for n in ("mx", "nmx", "den", "rec")]
            assert nc.sbuf_base <= own_end
            s1("pad_f", [P, (tail_at - nc.sbuf_base) // 4])
            cg = s1("cg", [P, TT, NB])
            u2pad = s1("u2pad", [P, CT, TAPS2 - 1 + TOK])
            zs = s1("zs", [P, TT, NB])
            rtmp = s1("rtmp", [P, 2, TT, GH, ROPE // 2])
            wc2 = s1("wc2", [P, CT, TAPS2])
            assert nc.sbuf_base <= tail_at + 2 * D * 4
        qa_t, kva_t = kvst[:, :, 0], kvst[:, :, 1]
        with ExitStack() as st:
            s1 = lambda n, shape, dt=F32: sb(n, shape, dt, st)
            thm, thc = s1("thm", [P, TT, D]), s1("thc", [P, TT, D])
            oin = s1("oin", [P, 2, TT, NB])
            thz = s1("thz", [P, TT, NB])
            assert nc.sbuf_base <= own_end
        outst, x2r, gpost2 = thm, thc, gpost
        gth = [qtok, ktok]
        mtmp = kbe[:].rearrange("p t h d -> p t (h d)")

        acc = ctx.enter_context(nc.psum_tensor("acc", [P, 2, TT, NB], F32))
        X = ctx.enter_context(nc.psum_tensor("aux", [P, 4, NB], F32))

        landed = [sem(f"raw_landed{i}") for i in range(RAW)]
        hi_ready, lo_ready, w_used = sem("hi_ready"), sem("lo_ready"), sem("w_used")
        acc_free = [sem("acc0_free"), sem("acc1_free")]

        def used(ph, hl, i=0):
            return HL + ph.h0 + hl + 1 + i * ph.hn

        def freed(ph, bl, i=0):
            return 2 * ((ph.b0 + bl) // 2) + 2 + i * ph.bn

        block = ctx.enter_context(nc.Block())

        @block.sync
        def _(sp):
            def load(ph, cl, src, i=0, shape=None):
                k = ph.k0 + cl
                if k >= RAW:
                    last = max(h for h, (c, _, _) in enumerate(HALVES) if c == k - RAW)
                    sp.wait_ge(lo_ready, LO_CREDIT + last + 1 + i * ph.hn)
                elif not isinstance(i, int):
                    sp.wait_ge(lo_ready, LO_CREDIT + 2 * (k - RAW) + 1 + i * ph.hn)
                a, b = shape or (CHUNK_KT, NB)
                dst = raw[:, k % RAW, 0:a * b].rearrange("p (a b) -> p a b", a=a)
                sp.dma_start(dst, src).then_inc(landed[k % RAW], 16)

            def load_block(ph, bl, w, col, i=0, cl=None):
                cl = 4 * bl if cl is None else cl
                for c in range(KT // CHUNK_KT):
                    load(ph, cl + c, w[:, CHUNK_KT * c:CHUNK_KT * (c + 1), bass.ds(col, NB)], i)

            sp.dma_start(xt[:], tok(t["x"][0])).then_inc(sem("x_landed"), 16)
            sp.dma_start(crow[R_DW:R_DW + TAPS, :], t["w_dw"][0]).then_inc(sem("rows_landed"), 16)
            for r, name in ((R_BDW, "b_dw"), (R_LNG, "ln_g"), (R_LNB, "ln_b"), (R_GPRE, "g_pre")):
                sp.dma_start(crow[r:r + 1, :], t[name]).then_inc(sem("rows_landed"), 16)
            sp.dma_start(crow[R_GPRE2:R_GPRE2 + 1, :], t["pre_norm_g_2"].rearrange("(a n) -> a n", a=1)).then_inc(sem("rows_landed"), 16)
            sp.dma_start(crow[R_CW2:R_CW2 + TAPS2, :], t["conv_w_2"]).then_inc(sem("rows_landed"), 16)
            for n in range(3):
                sp.dma_start(crow[R_SC + SHORT * n:R_SC + SHORT * (n + 1), :],
                             t["w_conv_qkv"][0][:, n * D:(n + 1) * D]).then_inc(sem("rows_landed"), 16)
            for r, name in ((R2_QA, "q_a_norm_g_2"), (R2_KV, "kv_a_norm_g_2")):
                sp.dma_start(crow2[r:r + 4, :], t[name].rearrange("(a n) -> a n", n=P)).then_inc(sem("rows_landed"), 16)
            sp.dma_start(crow2[R2_DN:R2_DN + 1, :], t["g_dn_out"]).then_inc(sem("rows_landed"), 16)

            load(PH["BA"], 0, w_in[:, :, C_BA:C_BA + 2 * HEADS], shape=(KT, 2 * HEADS))
            load_block(PH["GLU0"], 0, w_in, C_GLU + D)
            load_block(PH["GLU0"], 1, w_in, C_GLU)
            with sp.Fori(0, PH["GLU"].iters) as i:
                ph = PH["GLU"]
                load_block(ph, 0, w_in, i * NB + C_GATE, i)
                load_block(ph, 1, w_in, i * NB + (C_GATE + D), i)
                load_block(ph, 2, w_in, i * NB + (C_GLU + D + NB), i)
                load_block(ph, 3, w_in, i * NB + (C_GLU + NB), i)
            load_block(PH["GT3"], 0, w_in, C_GATE + 3 * NB)
            load_block(PH["GT3"], 1, w_in, C_GATE + D + 3 * NB)
            for j in range(NJ):
                load_block(PH["ZB"], j, w_in, j * NB + C_ZB)
            with sp.Fori(0, NJ) as i:
                for n in range(4):
                    load_block(PH["QKVZ"], n, w_in, i * NB + n * D, i)
            for name, w in (("YB", w_br_b), ("YA", w_br_a), ("MIX", w_out)):
                for j in range(NJ):
                    load_block(PH[name], j, w, j * NB)
            for c in range(2):
                load(PH["PLEP"], c, w_ple_proj[:, :, c * 2 * NB:(c + 1) * 2 * NB], shape=(2, 2 * NB))
            for j in range(NJ):
                load_block(PH["PLEG"], j, w_ple_gate, j * NB)
            load_block(PH["QA"], 0, w_in2, C2_QA)
            load(PH["KR"], 0, w_in2[:, :, C2_KR:C2_KR + ROPE], shape=(KT, ROPE))
            load_block(PH["KVA"], 0, w_in2, C2_KV)
            with sp.Fori(0, NJ) as i:
                ph = PH["FC"]
                load(ph, 0, w_q_b[:, :, bass.ds(i * (GH * QH), NB)], i)
                load(ph, 1, w_q_b[:, :, bass.ds(i * (GH * QH) + (GH * QH - NB), NB)], i)
                load(ph, 2, w_kv_b[:, :, bass.ds(i * (GH * KVH), NB)], i)
                load(ph, 3, w_kv_b[:, :, bass.ds(i * (GH * KVH) + NB, NB)], i)
                for n, col in enumerate((C2_CG, C2_CIN, C2_ZC, C2_BG)):
                    load_block(ph, None, w_in2, i * NB + col, i, cl=4 + 4 * n)
            with sp.Fori(0, NJ) as i:
                load_block(PH["FG"], 0, w_in2, i * NB + C2_GM, i)
                load_block(PH["FG"], 1, w_in2, i * NB + C2_GC, i)
            for j in range(NJ):
                load_block(PH["FZ"], j, w_in2, j * NB + C2_ZM)
            for name, w in (("YM", w_o_mla), ("YC", w_o_conv)):
                for j in range(NJ):
                    load_block(PH[name], j, w, j * NB)
            for j in range(NJ):
                load_block(PH["OUT"], j, w_out2, j * NB)
            for j in range(NJ):
                sp.wait_ge(sem("out_ready"), j + 1)
                sp.dma_start(tok(out[0])[:, :, j * NB:(j + 1) * NB], outst[:, :, j * NB:(j + 1) * NB]).then_inc(sem("out_done"), 16)
            sp.wait_ge(sem("out_done"), 16 * NJ)

        @block.gpsimd
        def _(pool):
            c = Chain(pool, sem("pool_order"))
            g = nc.gpsimd
            c.link(g.memset(ident[:], 0.0))
            c.link(g.affine_select(out=ident[:], in_=ident[:], compare_op=ALU.not_equal, fill=1.0, base=0,
                                   pattern=[[-1, P]], channel_multiplier=1))
            pool.sem_inc(sem("mask_ready"), 1)
            c.link(g.memset(neg_half[:], -0.5))
            pool.dma_start(ba_const[:, 0, :], t["a_log"][0].partition_broadcast(P)).then_inc(sem("small_landed"), 16)
            pool.dma_start(ba_const[:, 1, :], t["dt_bias"][0].partition_broadcast(P)).then_inc(sem("small_landed"), 16)
            pool.dma_start(inv_f[:], t["inv_freq"][0].partition_broadcast(P)).then_inc(sem("small_landed"), 16)
            with nc.allow_non_contiguous_dma(reason="256 positions"):
                pool.dma_start(pos_i[:], t["positions_2"][0].rearrange("(t p) -> p t", p=P)).then_inc(sem("small_landed"), 16)
            for m in (same, tri_incl, strict_lo):
                c.link(g.memset(m[:], 1.0))
                v = m[:].rearrange("p (b s) -> p b s", s=SEQ_CHUNK)
                c.link(g.affine_select(out=v, in_=v, compare_op=ALU.is_ge, fill=0.0, base=0,
                                       pattern=[[-SEQ_CHUNK, P // SEQ_CHUNK], [0, SEQ_CHUNK]], channel_multiplier=1))
                c.link(g.affine_select(out=v, in_=v, compare_op=ALU.is_ge, fill=0.0, base=SEQ_CHUNK - 1,
                                       pattern=[[SEQ_CHUNK, P // SEQ_CHUNK], [0, SEQ_CHUNK]], channel_multiplier=-1))
            c.link(g.affine_select(out=tri_incl[:], in_=tri_incl[:], compare_op=ALU.is_ge, fill=0.0, base=0,
                                   pattern=[[1, P]], channel_multiplier=-1))
            c.link(g.affine_select(out=strict_lo[:], in_=strict_lo[:], compare_op=ALU.is_ge, fill=0.0, base=-1,
                                   pattern=[[-1, P]], channel_multiplier=1))
            c.link(g.memset(half_ones[:], 0.0))
            for n in range(2):
                c.link(g.memset(half_ones[n * SEQ_CHUNK:(n + 1) * SEQ_CHUNK, n, :], 1.0))
            c.link(g.memset(ones_mean[:], 1.0 / D))
            pool.sem_inc(sem("mask_ready"), 1)
            def rsqrt(dst, src, scale, ready, value, post=None, half=None, square=None):
                pool.wait_ge(ready, value)
                n = src.shape[-1]
                c.link(g.tensor_scalar(dst, src, scale, EPS, ALU.mult, ALU.add))
                c.link(g.tensor_tensor(dst, dst, neg_half[:, 0:1].to_broadcast([P, n]), ALU.pow))
                if post is not None:
                    c.link(g.tensor_scalar(dst, dst, post, None, ALU.mult))
                if half is not None:
                    c.inc(g.tensor_scalar(half, dst, 0.5, None, ALU.mult))
                    c.link(g.tensor_tensor(square, dst, dst, ALU.mult))
                pool.sem_inc(sem("rstd_ready"), 1)

            rsqrt(stat[:, 2:4], stat[:, 0:2], 1.0 / D, sem("square_ready"), SQ_X)

            c.link(g.memset(lvl[:], 0.0))
            c.link(g.memset(m1u[:], 0.0))
            for l in range(5):
                s = 4 << l
                v = lvl[:, l, :].rearrange("p (b s) -> p b s", s=s)
                c.link(g.memset(v[:, :, 0:s // 2], 1.0))
                c.link(g.affine_select(out=v, in_=v, compare_op=ALU.is_ge, fill=0.0, base=-s // 2,
                                       pattern=[[-s, P // s], [0, s]], channel_multiplier=1))
                c.link(g.affine_select(out=v, in_=v, compare_op=ALU.is_ge, fill=0.0, base=s - 1,
                                       pattern=[[s, P // s], [0, s]], channel_multiplier=-1))
            v = m1u[:].rearrange("p (b s) -> p b s", s=2)
            c.link(g.affine_select(out=v[:, :, 1], in_=v[:, :, 1], compare_op=ALU.not_equal, fill=1.0, base=0,
                                   pattern=[[-2, P // 2]], channel_multiplier=1))
            pool.sem_inc(sem("mask_ready"), 1)

            def bias(i):
                pool.dma_start(bgt[:, 0, :], t["b_gate"][0, bass.ds(i * NB, NB)].partition_broadcast(P)).then_inc(sem("bias_landed"), 16)
                pool.dma_start(bgt[:, 1, :], t["b_gate"][0, bass.ds(i * NB + D, NB)].partition_broadcast(P)).then_inc(sem("bias_landed"), 16)

            def gates_out(i):
                for kind, tile in ((0, gtA), (1, gtB)):
                    pool.wait_ge(sem(f"gate{kind}_ready"), i + 1)
                    pool.dma_start(gate_dram[kind, bass.ds(i, 1)].rearrange("a p n -> p (a n)"),
                                   tile[:].rearrange("p t n -> p (t n)")).then_inc(sem("gate_out"), 16)

            bias(0)
            c.restart()
            with pool.Fori(0, PH["GLU"].iters) as i:
                gates_out(i)
                pool.wait_ge(sem("gate_out"), 32 * i + 32)
                bias(i + 1)
            gates_out(3)

            q4 = lambda q: y[:, CT * q:CT * (q + 1)]
            row4 = rows[:].unsqueeze(1).to_broadcast([P, CT, TOK])
            pool.wait_ge(sem("rows_ready"), 1)
            pool.wait_ge(sem("conv_done"), NJ + 1)
            for q in range(NJ):
                g.tensor_tensor(q4(q), q4(q), row4, ALU.subtract).then_inc(sem("ln_centered"), 1)
            rsqrt(var[:], var[:], 1.0, sem("square_ready"), SQ_LN)
            def ln_value(q):
                if q:
                    pool.wait_ge(sem("ln_silu"), q)
                for a in range(CT):
                    kt = CT * q + a
                    ins = g.tensor_scalar(lnsq[:, a], y[:, kt], pc[:, kt, R_LNG:R_LNG + 1], pc[:, kt, R_LNB:R_LNB + 1], ALU.mult, ALU.add)
                    if a < CT - 1:
                        c.inc(ins)
                    else:
                        ins.then_inc(sem("ln_value"), 1)

            pool.wait_ge(sem("rows_ready"), 2)
            pool.wait_ge(sem("ln_centered"), NJ)
            for q in range(NJ):
                g.tensor_tensor(q4(q), q4(q), row4, ALU.mult).then_inc(sem("ln_norm"), 1)
                if q == 0:
                    pool.wait_ge(sem("ln_norm"), 1)
                    ln_value(0)
            pool.wait_ge(sem("ln_norm"), NJ)
            for q in range(NJ):
                pool.wait_ge(sem("ln_silu"), q + 1)
                g.tensor_tensor(lnt[:], lnt[:], szT[:, CT * q:CT * (q + 1)], ALU.mult).then_inc(sem("ln_out"), 1)
                if q < NJ - 1:
                    ln_value(q + 1)
                pool.wait_ge(sem("ln_lo"), q + 1)
                for n, tile in ((0, luh), (1, lul)):
                    pool.dma_start(uT_dram[n, q], tile[:].rearrange("p a b -> p (a b)")).then_inc(sem("uT_out"), 16)

            def inverse_norm(i, dst, src, n, post):
                pool.wait_ge(sem("qk_square"), i * 2 + (n + 1))
                c.step()
                c.link(g.tensor_scalar(dcol[:, dst], dcol[:, src], 0.25, EPS, ALU.mult, ALU.add))
                c.link(g.tensor_tensor(dcol[:, dst], dcol[:, dst], neg_half[:, 0:1].to_broadcast([P, TT, GH]), ALU.pow))
                c.link(g.tensor_scalar(dcol[:, dst], dcol[:, dst], post, None, ALU.mult))

            def columns_q(i):
                heads = bass.ds(i * GH, GH)
                inverse_norm(i, 0, 8, 0, 0.5 * DK ** -0.5)
                c.link(g.tensor_copy(dcol[:, 1], egc[:, :, heads]))
                c.link(g.tensor_copy(dcol[:, 3], beta[:, :, heads]))
                c.link(g.tensor_tensor(dcol[:, 4], dcol[:, 3], egc[:, :, heads], ALU.mult))
                c.link(g.tensor_copy(dcol[:, 5], kend[:, :, heads]))
                c.link(g.tensor_copy(dcol[:, 6], hbeta[:, :, heads]))
                c.link(g.tensor_copy(dcol[:, 7], glog[:, :, heads]))

            def columns_k(i, first):
                heads = bass.ds(i * GH, GH)
                inverse_norm(i, 2, 9, 1, 0.5)
                if not first:
                    pool.wait_ge(sem("scan_ready"), i * SCAN)
                    c.step()
                c.link(g.tensor_copy(degl[:], egl[:, :, :, heads]))
                pool.sem_inc(sem("cols_ready"), 1)

            def delta_norm(d):
                pool.wait_ge(sem("o_square"), d + 1)
                c.step()
                c.link(g.tensor_scalar(dcol[:, 10], dcol[:, 11], 1.0 / DK, EPS, ALU.mult, ALU.add))
                c.link(g.tensor_tensor(dcol[:, 10], dcol[:, 10], neg_half[:, 0:1].to_broadcast([P, TT, GH]), ALU.pow))
                pool.sem_inc(sem("o_rstd"), 1)

            def delta_out(d):
                pool.wait_ge(sem("oT_lo"), 2 * (d + 1))
                for n, tile in ((0, oh), (1, ol)):
                    pool.dma_start(oT_dram[n, bass.ds(d, 1)].rearrange("a p n -> p (a n)"),
                                   tile[:].rearrange("p a b -> p (a b)")).then_inc(sem("oT_out"), 16)
                pool.wait_ge(sem("oT_out"), 32 * (d + 1))

            def reload(src, dst, ph, i, q):
                pool.wait_ge(w_used, used(ph, ph.hn - 7 + 2 * q, i))
                for n, r in enumerate(dst):
                    pool.dma_start(r[:, CT * q:CT * (q + 1), :].rearrange("p a b -> p (a b)"), src[n, q]).then_inc(sem(f"operand_landed{q}"), 16)

            columns_q(0)
            columns_k(0, True)
            c.restart()
            with pool.Fori(1, NJ - 1) as i:
                columns_q(i)
                delta_norm(i - 1)
                columns_k(i, False)
                delta_out(i - 1)
                c.restart()
            columns_q(NJ - 1)
            delta_norm(NJ - 2)
            columns_k(NJ - 1, False)
            pool.wait_ge(sem("uT_out"), 32 * NJ)
            for q in range(NJ - 1):
                reload(uT_dram, (r1h, r1l), PH["QKVZ"], NJ - 1, q)
            delta_out(NJ - 2)
            reload(uT_dram, (r1h, r1l), PH["QKVZ"], NJ - 1, NJ - 1)


            def load_gate(kind, j, n):
                src = gate_dram[kind, bass.ds(j, 1)].rearrange("a p n -> p (a n)")
                pool.dma_start(gth[n][:].rearrange("p t h d -> p (t h d)"), src).then_inc(sem(f"tile_landed{n}"), 16)

            pool.wait_ge(sem("gate_out"), 16 * 2 * NJ)
            pool.wait_ge(sem("qT_tr"), 2 * NJ)
            load_gate(1, 0, 0)
            pool.wait_ge(sem("k_scaled"), NJ)
            load_gate(1, 1, 1)
            for j in range(2, NJ):
                pool.wait_ge(sem("gy_ready"), j - 1)
                load_gate(1, j, j % 2)
            pool.wait_ge(sem("gy_ready"), NJ - 1)
            load_gate(0, 0, 0)
            reload(oT_dram, (r1h, r1l), PH["YB"], 0, 0)
            delta_norm(3)
            reload(oT_dram, (r1h, r1l), PH["YB"], 0, 1)
            reload(oT_dram, (r1h, r1l), PH["YB"], 0, 2)
            delta_out(3)
            reload(oT_dram, (r1h, r1l), PH["YB"], 0, 3)
            pool.wait_ge(sem("gy_ready"), NJ)
            load_gate(0, 1, 1)
            for j in range(2, NJ):
                pool.wait_ge(sem("m_ready"), OP_M + j - 1)
                load_gate(0, j, j % 2)
            pool.wait_ge(sem("oT_out"), 32 * NJ)
            pool.dma_start(ptok, tok(t["p"][0, 0])).then_inc(sem("p_landed"), 16)
            pool.dma_start(gpost[:], t["g_post"][0].partition_broadcast(P)).then_inc(sem("gains_landed"), 16)
            pool.dma_start(gple[:], t["g_ple"][0].partition_broadcast(P)).then_inc(sem("gains_landed"), 16)
            pool.wait_ge(sem("m_tr"), NJ)
            for j in range(NJ):
                if j >= 2:
                    pool.wait_ge(sem("op_ready"), j - 1)
                pool.dma_start(xres[:, j % 2], tok(t["x"][0])[:, :, j * NB:(j + 1) * NB]).then_inc(sem(f"tile_landed{j % 2}"), 16)
                if j == 1:
                    rsqrt(stat[:, 6:8], stat[:, 4:6], 1.0 / D, sem("square_ready"), SQ_MIX)
            rsqrt(stat[:, 10:12], stat[:, 8:10], 0.25 / D, sem("square_ready"), SQ_PLE, post=0.5)
            pool.wait_ge(sem("op_ready"), OP_H2 - OP_X1 + NJ)
            pool.dma_start(tok(x2_dram), mix[:]).then_inc(sem("x2_out"), 16)
            rsqrt(stat[:, 14:16], stat[:, 12:14], 1.0 / D, sem("square_ready"), SQ_X2, half=stat[:, 40:42], square=stat[:, 42:44])

            c.link(g.memset(amask[:], 0.0))
            for at in (0, 2 * P):
                m = amask[:, at:at + P]
                c.link(g.affine_select(out=m, in_=m, compare_op=ALU.is_ge, fill=-1e30, base=0, pattern=[[-1, P]], channel_multiplier=1))
            pool.sem_inc(sem("mask_ready"), 1)
            rsqrt(stat[:, 48:50], stat[:, 44:46], 1.0 / LORA, acc_free[0], freed(PH["QA"], 0))
            rsqrt(stat[:, 50:52], stat[:, 46:48], 1.0 / LORA, acc_free[1], freed(PH["KVA"], 0))
            pool.sem_inc(sem("ost_free"), 1)
            pool.sem_inc(sem("ct_free"), 1)
            c.restart()
            with pool.Fori(0, NJ) as i:
                pool.wait_ge(sem("ost_ready"), i + 1)
                c.step()
                pool.dma_start(o_dram[bass.ds(i, 1)].rearrange("a p n -> p (a n)"), ost[:].rearrange("p t h d -> p (t h d)")).then_inc(sem("o_out"), 16)
                pool.wait_ge(sem("o_out"), i * 16 + 16)
                pool.sem_inc(sem("ost_free"), 1)
                pool.wait_ge(sem("c_lo"), i + 1)
                c.step()
                for n, r in enumerate((r1h, r1l)):
                    pool.dma_start(cT_dram[n, bass.ds(i, 1)].rearrange("a p n -> p (a n)"),
                                   r[:, 2 * CT:3 * CT].rearrange("p a b -> p (a b)")).then_inc(sem("cT_out"), 16)
                pool.wait_ge(sem("cT_out"), i * 32 + 32)
                pool.sem_inc(sem("ct_free"), 1)
                c.restart()
            for j in range(NJ):
                if j >= 2:
                    pool.wait_ge(sem("m_tr"), OP_ATTN + j - 1)
                pool.dma_start(oin[:, j % 2].rearrange("p t n -> p (t n)"), o_dram[j]).then_inc(sem(f"tile_landed{j % 2}"), 16)
            pool.dma_start(gpost2[:], t["post_norm_g_2"].partition_broadcast(P)).then_inc(sem("gains_landed"), 16)
            pool.wait_ge(sem("cT_out"), 32 * NJ)
            for q in range(NJ):
                reload(cT_dram, (r2h, r2l), PH["FZ"], 0, q)
            pool.wait_ge(sem("m_ready"), OP_Y + NJ)
            pool.dma_start(x2r[:], tok(x2_dram)).then_inc(sem("x2_landed"), 16)
            rsqrt(stat[:, 62:64], stat[:, 60:62], 1.0 / D, sem("square_ready"), SQ_OUT)

        @block.scalar
        def _(act):
            c = Chain(act, sem("act_order"))
            A = nc.scalar.activation

            def split(h, i=0, hn=0, kn=0):
                if h >= len(HALVES):
                    return
                k, x, n = HALVES[h]
                act.wait_ge(landed[k % RAW], 16 * (k // RAW + 1) + i * (16 * kn // RAW))
                act.wait_ge(w_used, h + 1 + i * hn)
                nc.scalar.copy(w_hi[:, h % HL, 0:n], raw[:, k % RAW, x * HALF:x * HALF + n]).then_inc(hi_ready, 1)

            def ahead(ph, hl, i=0):
                split(ph.h0 + hl + LEAD, i, ph.hn, ph.kn)

            def sig(ins, name, value):
                ins.then_inc(sem(name), 1)
                act.wait_ge(sem(name), value)

            act.wait_ge(sem("x_landed"), 16)
            for n in range(TT):
                sig(A(sz0[:].rearrange("p t n -> p (t n)"), xt[:, n, 0:D // 2], ACT.Square, accum_out=stat[:, 40 + n:41 + n]), "row_sq", 2 * n + 1)
                sig(A(sz0[:].rearrange("p t n -> p (t n)"), xt[:, n, D // 2:D], ACT.Square, accum_out=stat[:, 42 + n:43 + n]), "row_sq", 2 * n + 2)
            for h in range(LEAD - 1):
                split(h)
            act.wait_ge(sem("rstd_ready"), RSTD_X)
            A(xt[:, 0], xt[:, 0], ACT.Copy, scale=stat[:, 2:3]).then_inc(sem("xn_ready"), 1)
            split(LEAD - 1)

            def stationary_hi(dst, kt, bank, scale_col, tr_sem, tr_value, hi_sem, hi_value):
                act.wait_ge(tr_sem, tr_value)
                c.inc(A(dst[:, kt], X[:, bank, 0:TOK], ACT.Copy, scale=scale_col[0]))
                sig(A(dst[:, kt + 1], X[:, bank, TOK:2 * TOK], ACT.Copy, scale=scale_col[1]), hi_sem, hi_value)

            act.wait_ge(sem("prep_ready"), PREP_PC)
            for m in range(KT // 2):
                stationary_hi(r1h, 2 * m, m % 4, [pc[:, 2 * m + q, R_GPRE:R_GPRE + 1] for q in range(2)],
                              sem("xT_tr"), m + 1, "op_hi", 2 * OP_HT + m + 1)

            act.wait_ge(sem("prep_ready"), PREP_ANGLE)
            c.inc(A(sin_t[:], rope_f[:, 2], ACT.Sin))
            c.link(A(rope_f[:, 3], rope_f[:, 2], ACT.Sin, scale=0.5))
            act.sem_inc(sem("table_ready"), 1)

            ahead(PH["BA"], 0)
            act.wait_ge(sem("prep_ready"), PREP_BA)
            c.inc(A(ba_tmp[:, 0], bat[:, :, 0:HEADS], ACT.Tanh, scale=0.5))
            c.link(A(ba_tmp[:, 3], ba_tmp[:, 2], ACT.Exp))
            c.inc(A(ba_const[:, 0, :], ba_const[:, 0, :], ACT.Exp))
            c.link(A(ba_tmp[:, 4], ba_tmp[:, 3], ACT.Ln, bias=1.0))
            act.sem_inc(sem("table_ready"), 1)
            act.wait_ge(sem("gc_done"), 1)
            n16 = TT * HEADS
            c.inc(A(egc[:].rearrange("p t h -> p (t h)"), X[:, 3, 64:64 + n16], ACT.Exp))
            c.link(A(egl[:].rearrange("p t c h -> p (t c h)"), X[:, 3, 128:128 + 2 * n16], ACT.Exp))
            act.sem_inc(sem("table_ready"), 1)
            act.wait_ge(sem("prep_ready"), PREP_KEND)
            c.link(A(kend[:], kend[:], ACT.Exp))
            act.sem_inc(sem("table_ready"), 1)

            def half_tanh(dst, s, done, name=None, half=lambda n: 0.5):
                act.wait_ge(w_used, done)
                for n in range(TT):
                    ins = A(dst[:, n], acc[:, s, n], ACT.Tanh, scale=half(n))
                    if name is None:
                        ins.then_inc(acc_free[s], 1)
                    elif n == TT - 1:
                        ins.then_inc(sem(name), 1)

            def upad_copy(i):
                act.wait_ge(sem("uT_tr"), i + 1)
                c.inc(nc.scalar.copy(upad[:, 0:2, TAPS - 1:], X[:, 0].rearrange("p (a b) -> p a b", a=2)))
                c.link(nc.scalar.copy(upad[:, 2:4, TAPS - 1:], X[:, 1].rearrange("p (a b) -> p a b", a=2)))
                const = lambda a, r: pc[:, bass.ds(i * CT + a, 1), r:r + 1].rearrange("p a n -> p (a n)")
                for a in range(CT):
                    ins = A(ycur[:, a], upad[:, a, 0:TOK], ACT.Identity, scale=const(a, R_DW), bias=const(a, R_BDW))
                    if a < CT - 1:
                        c.inc(ins)
                sig(ins, "upad_ready", i + 1)

            def gate_tanh(kind, tile, ph, bl, i, value):
                act.wait_ge(acc_free[kind], freed(ph, bl, i))
                sig(A(tile[:], tile[:], ACT.Tanh, scale=0.5), f"gate{kind}_ready", value)

            ph = PH["GLU0"]
            for hl in range(ph.hn):
                ahead(ph, hl)
                if hl == 8:
                    half_tanh(sg, 0, used(ph, 7))
            ph = PH["GLU"]
            c.restart()
            with act.Fori(0, ph.iters) as i:
                for hl in range(ph.hn):
                    ahead(ph, hl, i)
                    if hl == 3:
                        act.wait_ge(sem("conv_done"), i + 1)
                        upad_copy(i)
                    if hl == 9:
                        gate_tanh(0, gtA, ph, 0, i, i + 1)
                    if hl == 17:
                        gate_tanh(1, gtB, ph, 1, i, i + 1)
                    if hl == 24:
                        act.wait_ge(acc_free[1], freed(ph, -1, i))
                        half_tanh(sg, 0, used(ph, 23, i))
                c.restart()
            ph = PH["GT3"]
            for hl in range(ph.hn):
                ahead(ph, hl)
                if hl == 3:
                    act.wait_ge(sem("conv_done"), NJ)
                    upad_copy(NJ - 1)
                if hl == 9:
                    gate_tanh(0, gtA, ph, 0, 0, NJ)
            gate_tanh(1, gtB, ph, 1, 0, NJ)

            ph = PH["ZB"]
            c.restart()

            def z_block(j):
                if j:
                    act.wait_ge(acc_free[1 - j % 2], freed(PH["ZB"], j - 1))
                half_tanh(th0, j % 2, used(PH["ZB"], 8 * j + 7), "tanh_ready")

            def szT_copy(j):
                act.wait_ge(sem("zT_tr"), j + 1)
                for q in range(2):
                    sig(A(szT[:, j * CT + 2 * q:j * CT + 2 * q + 2], X[:, 2 + q].rearrange("p (a b) -> p a b", a=2), ACT.Copy, scale=0.25),
                        "szT_ready", 2 * j + q + 1)

            def z_steps(hl):
                if at_block(hl, 0) is not None:
                    z_block(at_block(hl, 0))
                if at_block(hl, 3) is not None:
                    szT_copy(at_block(hl, 3))

            for hl in range(ph.hn):
                ahead(ph, hl)
                z_steps(hl)

            def z_steps_end(hl):
                z_steps(PH["ZB"].hn + hl)

            def own(ph, hl, i, first):
                for n, (evac, _, pad, (_, conv_end), silu, back) in enumerate(OWN):
                    if hl == back + 1 and n < 2:
                        dst = (qtok, ktok)[n]
                        act.wait_ge(sem("tok_tr"), i * 3 + (n + 1))
                        if not first:
                            act.wait_ge(sem(("qT_tr", "kT_tr")[n]), i * 2)
                        c.inc(nc.scalar.copy(dst[:, 0].rearrange("p h d -> p (h d)"), X[:, 2]))
                        sig(nc.scalar.copy(dst[:, 1].rearrange("p h d -> p (h d)"), X[:, 3]), "tok_ready", i * 2 + (n + 1))
                        sig(A(cy[:].rearrange("p h n -> p (h n)"), dst[:].rearrange("p t h d -> p (t h d)"), ACT.Square),
                            "qk_sq", i * 2 + (n + 1))
                for n, (evac, _, pad, (_, conv_end), silu, back) in enumerate(OWN):
                    if hl == evac:
                        if n or not first:
                            act.wait_ge(sem("ch_tr"), i * 3 + n)
                        act.wait_ge(w_used, used(ph, 8 * n + 7, i))
                        for x in range(TT):
                            nc.scalar.copy(praw[:, x], acc[:, n % 2, x]).then_inc(acc_free[n % 2], 1)
                    if hl == pad:
                        act.wait_ge(sem("ch_tr"), i * 3 + (n + 1))
                        act.wait_ge(sem("conv4_done"), i * 3 + (n + 1))
                        b = OWN_BANKS[n]
                        c.inc(nc.scalar.copy(cpad[:, 0:2, SHORT - 1:], X[:, b].rearrange("p (a b) -> p a b", a=2)))
                        sig(nc.scalar.copy(cpad[:, 2:4, SHORT - 1:], X[:, b + 1].rearrange("p (a b) -> p a b", a=2)),
                            "cpad_ready", i * 3 + (n + 1))
                    if hl == silu:
                        act.wait_ge(sem("conv4_done"), i * 3 + (n + 2))
                        if n or not first:
                            act.wait_ge(sem("tok_tr"), i * 3 + n)
                        sig(A(cth[:].rearrange("p t n -> p (t n)"), cy[:].rearrange("p h n -> p (h n)"), ACT.Tanh, scale=0.5),
                            "cth_ready", i * 3 + (n + 1))

            def values(i):
                act.wait_ge(sem("tok_tr"), i * 3 + 3)
                act.wait_ge(sem("cols_ready"), i + 1)
                for x in range(TT):
                    for h in range(GH):
                        ins = A(vb[:, x, h], X[:, 2 + x, h * DK:(h + 1) * DK], ACT.Copy, scale=dcol[:, 6, x, h:h + 1])
                        if (x, h) != (TT - 1, GH - 1):
                            c.inc(ins)
                sig(ins, "vb_ready", i + 1)

            def z_tanh(ph, i):
                half_tanh(cth, 1, used(ph, 31, i), "tanh_ready")

            def bank_copies(dst, banks, tr, dv, name, per=2, at=0):
                for x in range(TT):
                    act.wait_ge(sem(tr), dv(per, at + x + 1))
                    sig(nc.scalar.copy(dst[:, x].rearrange("p h d -> p (h d)"), X[:, banks[x]]), name, dv(per, at + x + 1))

            def delta(hl, dv):
                if hl == 1:
                    bank_copies(kT, (0, 1), "kT_tr", dv, "kT_ready")
                if hl == 2:
                    for x in range(TT):
                        act.wait_ge(sem("decay_done"), dv(2, x + 1))
                        sig(A(decT[:, x].rearrange("p h i -> p (h i)"), X[:, x], ACT.Exp), "decT_ready", dv(2, x + 1))
                if hl == 4:
                    bank_copies(qT, (0, 1), "qT_tr", dv, "qT_ready")
                if hl == 5:
                    bank_copies(tinv, (2, 3), "tinv_tr", dv, "tinv_ready")
                if hl == 16:
                    bank_copies(us, (0, 1), "uw_done", dv, "uw_ready", 4)
                    bank_copies(wT, (2, 3), "uw_done", dv, "uw_ready", 4, 2)
                if hl in (18, 20, 22, 24):
                    n = (hl - 18) // 2
                    x, rows = n // 2, slice(n % 2 * SEQ_CHUNK, (n % 2 + 1) * SEQ_CHUNK)
                    act.wait_ge(sem("o_done"), dv(4, n + 1))
                    sig(nc.scalar.copy(otok[rows, x].rearrange("p h d -> p (h d)"), X[rows, 1]), "o_ready", dv(4, n + 1))
                if hl == 25:
                    sig(A(xs[:].rearrange("p t h d -> p (t h d)"), otok[:].rearrange("p t h d -> p (t h d)"), ACT.Square), "o_sq", dv(2, 1))
                if hl == 27:
                    act.wait_ge(sem("o_rstd"), dv(1, 1))
                    for x in range(TT):
                        for h in range(GH):
                            ins = A(otok[:, x, h], otok[:, x, h], ACT.Copy, scale=dcol[:, 10, x, h:h + 1])
                            if (x, h) != (TT - 1, GH - 1):
                                c.inc(ins)
                    sig(ins, "o_sq", dv(2, 2))
                if hl == 30:
                    act.wait_ge(sem("oT_tr"), dv(1, 1))
                    for q in range(2):
                        sig(A(oh[:, 2 * q:2 * q + 2], X[:, q].rearrange("p (a b) -> p a b", a=2), ACT.Copy, scale=pc2[:, R2_DN:R2_DN + 1]),
                            "oT_hi", dv(2, q + 1))

            ph = PH["QKVZ"]

            def ln_values(q):
                act.wait_ge(sem("ln_norm"), q + 1)
                if q:
                    act.wait_ge(sem("ln_lo"), q)
                for a in range(CT):
                    kt = CT * q + a
                    ins = A(lnt[:, a], y[:, kt], ACT.Tanh, scale=lnh[:, kt, 0:1], bias=lnh[:, kt, 1:2])
                    if a < CT - 1:
                        c.inc(ins)
                    else:
                        ins.then_inc(sem("ln_value"), 1)

            for hl in range(ph.hn):
                ahead(ph, hl)
                if hl < 4:
                    z_steps_end(hl)
                own(ph, hl, 0, True)
                if hl == 2:
                    act.wait_ge(sem("mean_done"), 1)
                    sig(nc.scalar.copy(rows[:], X[:, 0, 0:TOK]), "rows_ready", 1)
                if hl == 11:
                    act.wait_ge(sem("rstd_rows"), 1)
                    act.wait_ge(sem("ln_centered"), NJ)
                    sig(nc.scalar.copy(rows[:], X[:, 1, 0:TOK]), "rows_ready", 2)
                if 4 <= hl < 4 + NJ:
                    q = hl - 4
                    act.wait_ge(sem("ln_centered"), q + 1)
                    if q:
                        act.wait_ge(sem("ln_sq_used"), q)
                    sig(A(lnsq[:].rearrange("p a b -> p (a b)"), y[:, CT * q:CT * (q + 1)].rearrange("p a b -> p (a b)"), ACT.Square), "ln_sq", q + 1)
                if hl in LN_TANH:
                    ln_values(LN_TANH.index(hl))
                if hl in LN_HI:
                    q = LN_HI.index(hl)
                    act.wait_ge(sem("ln_out"), q + 1)
                    if q:
                        act.wait_ge(sem("uT_out"), 32 * q)
                    sig(nc.scalar.copy(luh[:].rearrange("p a b -> p (a b)"), lnt[:].rearrange("p a b -> p (a b)")), "ln_hi", q + 1)
            values(0)
            z_tanh(ph, 0)
            act.wait_ge(sem("uT_out"), 32 * NJ)
            c.restart()
            with act.Fori(1, NJ) as i:
                dv = lambda per, n: i * per + (n - per)
                for hl in range(ph.hn):
                    ahead(ph, hl, i)
                    delta(hl, dv)
                    own(ph, hl, i, False)
                values(i)
                z_tanh(ph, i)
                c.restart()

            dv = lambda per, n: (NJ - 1) * per + n
            ph = PH["YB"]
            for hl in range(ph.hn):
                ahead(ph, hl)
                delta(hl, dv)

            def transposed_hi(banks, dst, tr, tr_value, name, value, scale):
                act.wait_ge(sem(tr), tr_value)
                for q in range(2):
                    sig(A(dst(q), X[:, banks[q]].rearrange("p (a b) -> p a b", a=2), ACT.Copy, scale=scale), name, value - 1 + q)

            def merged_hi(dst, j, base):
                transposed_hi((0, 1), lambda q: dst[:, CT * j + 2 * q:CT * j + 2 * q + 2],
                              "m_tr", base + j + 1, "m_hi", 2 * (base + j) + 2, 0.5)

            ph = PH["YA"]
            for hl in range(ph.hn):
                ahead(ph, hl)
                if at_block(hl, 2) is not None:
                    merged_hi(r2h, at_block(hl, 2), OP_M)

            def evac_square(dst, ssq, scratch, ph, bl, i, scale=lambda x: 1.0):
                s = (ph.b0 + bl) % 2
                act.wait_ge(w_used, used(ph, 8 * bl + 7, i))
                for x in range(TT):
                    c.link(A(dst(x), acc[:, s, x], ACT.Copy, scale=scale(x)))
                for x in range(TT):
                    A(scratch(x), dst(x), ACT.Square, accum_out=ssq(x)).then_inc(acc_free[s], 1)
                act.wait_ge(acc_free[s], freed(ph, bl, i))

            act.wait_ge(sem("p_tr"), 1)
            sig(nc.scalar.copy(pTh[:].rearrange("p a b -> p (a b)"), X[:, 2]), "p_hi", 1)
            ph = PH["MIX"]

            def mix_block(j):
                evac_square(lambda x: mix[:, x, j * NB:(j + 1) * NB], lambda x: stat[:, 16 + NJ * x + j:17 + NJ * x + j],
                            lambda x: e[:, x, 0:NB], ph, j, 0)

            for hl in range(ph.hn):
                ahead(ph, hl)
                if hl == 2:
                    merged_hi(r2h, NJ - 1, OP_M)
                if at_block(hl, 0) is not None:
                    mix_block(at_block(hl, 0))
            mix_block(NJ - 1)

            ph = PH["PLEP"]
            for hl in range(ph.hn):
                ahead(ph, hl)
                if hl % 2:
                    act.wait_ge(w_used, used(ph, hl))
                    for s in range(2):
                        for x in range(TT):
                            nc.scalar.copy(e[:, x, (hl - 1 + s) * NB:(hl + s) * NB], acc[:, s, x]).then_inc(acc_free[s], 1)

            def stationary_block(dst, j, base, scale=lambda kt: 1.0):
                act.wait_ge(sem("op_tr"), base - OP_X1 + j + 1)
                bank0 = 2 * (j % 2)
                for q in range(2):
                    for a in range(2):
                        kt = CT * j + 2 * q + a
                        ins = A(dst[:, kt], X[:, bank0 + q, a * TOK:(a + 1) * TOK], ACT.Copy, scale=scale(kt))
                        if a == 0:
                            c.inc(ins)
                    sig(ins, "op_hi", 2 * (base + j) + q + 1)

            for j in range(NJ):
                stationary_block(r1h, j, OP_X1)
                if j < 2:
                    ahead(PH["PLEG"], j)

            ph = PH["PLEG"]

            def ple_gate(j):
                half_tanh(pth, j % 2, used(ph, 8 * j + 7), "tanh_ready")

            def ple_squares(j):
                act.wait_ge(sem("ple_gated"), j + 1)
                for x in range(TT):
                    sig(A(pth[:, x], e[:, x, j * NB:(j + 1) * NB], ACT.Square, accum_out=stat[:, 24 + NJ * x + j:25 + NJ * x + j]),
                        "row_sq", ROWS_X + 2 * j + x + 1)

            act.wait_ge(sem("p_hi"), 1)
            for hl in range(ph.hn):
                if hl >= 2:
                    ahead(ph, hl)
                if at_block(hl, 0) is not None:
                    ple_gate(at_block(hl, 0))
                if at_block(hl, 1) is not None:
                    ple_squares(at_block(hl, 1))
            ple_gate(NJ - 1)
            ple_squares(NJ - 1)
            for j in range(NJ):
                stationary_block(r2h, j, OP_H2, lambda kt: pc[:, kt, R_GPRE2:R_GPRE2 + 1])
                if j < 2:
                    ahead(PH["QA"], j)
            rstd2 = lambda x: stat[:, 14 + x:15 + x]
            half_rstd2 = lambda x: stat[:, 40 + x:41 + x]

            def latent(ph, tile, at):
                evac_square(lambda x: tile[:, x], lambda x: stat[:, at + x:at + x + 1],
                            lambda x: ost[:, x].rearrange("p h d -> p (h d)"), ph, 0, 0, rstd2)

            for hl in range(PH["QA"].hn):
                if hl >= 2:
                    ahead(PH["QA"], hl)
                if hl < NJ:
                    for x in range(TT):
                        sig(A(pth[:, x], mix[:, x, hl * NB:(hl + 1) * NB], ACT.Square, accum_out=stat[:, 32 + NJ * x + hl:33 + NJ * x + hl]),
                            "row_sq", ROWS_PLE + 2 * hl + x + 1)
            ahead(PH["KR"], 0)
            act.wait_ge(sem("x2_out"), 16)
            act.wait_ge(sem("rstd_ready"), RSTD_X2)
            latent(PH["QA"], qa_t, 44)
            gain = lambda kt: pc2[:, kt:kt + 1]
            for hl in range(PH["KVA"].hn):
                ahead(PH["KVA"], hl)
                if hl == 4:
                    stationary_block(r1h, 0, OP_LAT, gain)
            latent(PH["KVA"], kva_t, 46)
            stationary_block(r1h, 1, OP_LAT, gain)

            ph = PH["FC"]
            c.restart()

            def heads_evac(dst, bl, i, n=NB):
                act.wait_ge(w_used, used(ph, 2 * bl + 1, i))
                for x in range(TT):
                    nc.scalar.copy(dst(x), acc[:, bl % 2, x, 0:n]).then_inc(acc_free[bl % 2], 1)

            def tile_copies(dst, tr, name, i):
                act.wait_ge(sem(tr), i + 1)
                for q in range(2):
                    sig(nc.scalar.copy(dst[:, 2 * q:2 * q + 2].rearrange("p h n -> p (h n)"), X[:, q]), name, i * 2 + (q + 1))

            with act.Fori(0, ph.iters) as i:
                for hl in range(ph.hn):
                    ahead(ph, hl, i)
                    if hl == 2:
                        heads_evac(lambda x: qst[:, x, 0:NB], 0, i)
                    if hl == 4:
                        heads_evac(lambda x: qst[:, x, NB:GH * QH], 1, i, GH * QH - NB)
                    if hl == 6:
                        heads_evac(lambda x: kvst[:, x, 0], 2, i)
                        tile_copies(qTn, "qn_tr", "qTn_ready", i)
                    if hl == 8:
                        heads_evac(lambda x: kvst[:, x, 1], 3, i)
                    if hl == 10:
                        tile_copies(kTn, "kn_tr", "kTn_ready", i)
                    if hl == 14:
                        act.wait_ge(sem("smax_ready"), i + 1)
                        for h in range(GH):
                            for x, at in ((0, slice(0, P)), (1, slice(P, SCORES))):
                                ins = A(sc[:, h, at], sc[:, h, at], ACT.Exp, scale=ATT_SCALE, bias=nmx[:, x, h:h + 1], accum_out=den[:, x, h:h + 1])
                                if (h, x) != (GH - 1, 1):
                                    c.inc(ins)
                        sig(ins, "exp_ready", i + 1)
                    if hl == 16:
                        act.wait_ge(w_used, used(ph, 15, i))
                        for x in range(TT):
                            A(cg[:, x], acc[:, 0, x], ACT.Copy, scale=rstd2(x)).then_inc(acc_free[0], 1)
                    if hl == 17:
                        act.wait_ge(sem("pT_tr"), i + 1)
                        sig(nc.scalar.copy(pT[:, 0:2], X[:, 0:2, 0:SCORES]), "pT_ready0", i + 1)
                    if hl == 26:
                        act.wait_ge(sem("u2_tr"), i + 1)
                        c.inc(nc.scalar.copy(u2pad[:, 0:2, TAPS2 - 1:], X[:, 0].rearrange("p (a b) -> p a b", a=2)))
                        sig(nc.scalar.copy(u2pad[:, 2:4, TAPS2 - 1:], X[:, 1].rearrange("p (a b) -> p a b", a=2)), "u2_ready", i + 1)
                    if hl == 32:
                        half_tanh(zs, 0, used(ph, 31, i), "tanh_ready", half_rstd2)
                act.wait_ge(sem("c_ready"), i + 1)
                act.wait_ge(sem("ct_free"), i + 1)
                sig(nc.scalar.copy(r1h[:, 2 * CT:3 * CT].rearrange("p a b -> p (a b)"), c3[:].rearrange("p a b -> p (a b)")), "c_hi", i + 1)
                c.restart()

            ph = PH["FG"]
            with act.Fori(0, ph.iters) as i:
                for hl in range(ph.hn):
                    ahead(ph, hl, i)
                    if hl == 8:
                        half_tanh(thm[:, :, bass.ds(i * NB, NB)], 0, used(ph, 7, i), half=half_rstd2)
                half_tanh(thc[:, :, bass.ds(i * NB, NB)], 1, used(ph, 15, i), half=half_rstd2)

            def z_tanh2(j):
                if j:
                    act.wait_ge(acc_free[1 - j % 2], freed(PH["FZ"], j - 1))
                act.wait_ge(sem("ct_free"), NJ + 1)
                half_tanh(thz, j % 2, used(PH["FZ"], 8 * j + 7), "tanh_ready", half_rstd2)

            def heads_steps(hl):
                if at_block(hl, 0) is not None:
                    z_tanh2(at_block(hl, 0))
                if at_block(hl, 3) is not None:
                    merged_hi(r1h, at_block(hl, 3), OP_ATTN)

            ph = PH["FZ"]
            for hl in range(ph.hn):
                ahead(ph, hl)
                heads_steps(hl)

            for hl in range(PH["YM"].hn):
                ahead(PH["YM"], hl)
                if hl < 4:
                    heads_steps(ph.hn + hl)
            ph = PH["YC"]
            for hl in range(ph.hn):
                ahead(ph, hl)
                if at_block(hl, 2) is not None:
                    merged_hi(r1h, at_block(hl, 2), OP_Y)

            ph = PH["OUT"]

            def out_block(j):
                evac_square(lambda x: outst[:, x, j * NB:(j + 1) * NB], lambda x: stat[:, 52 + NJ * x + j:53 + NJ * x + j],
                            lambda x: thz[:, x], ph, j, 0)

            for hl in range(ph.hn):
                ahead(ph, hl)
                if hl == 2:
                    merged_hi(r1h, NJ - 1, OP_Y)
                if at_block(hl, 0) is not None:
                    out_block(at_block(hl, 0))
            out_block(NJ - 1)

        @block.vector
        def _(dve):
            c = Chain(dve, sem("dve_order"))
            V = nc.vector
            TC2 = TT * GH

            def sig(ins, name, value):
                ins.then_inc(sem(name), 1)
                dve.wait_ge(sem(name), value)

            def split(h, i=0, hn=0):
                if h >= len(HALVES):
                    return
                k, x, n = HALVES[h]
                dve.wait_ge(hi_ready, h + 1 + i * hn)
                V.tensor_tensor(w_lo[:, h % HL, 0:n], raw[:, k % RAW, x * HALF:x * HALF + n],
                                w_hi[:, h % HL, 0:n].bitcast(F32), ALU.subtract).then_inc(lo_ready, 1)

            def ahead(ph, hl, i=0):
                split(ph.h0 + hl + LEAD, i, ph.hn)

            def over(ap, n):
                return ap.unsqueeze(2).to_broadcast([P, ap.shape[1], n])

            def rep(ap, n):
                return ap.unsqueeze(1).to_broadcast([P, n, ap.shape[1]])

            th = lambda tile: tile[:].rearrange("p t h d -> p (t h) d")
            col = lambda k: dcol[:, k].rearrange("p t h -> p (t h)")
            flat = lambda tile: tile[:].rearrange("p a b -> p (a b)")
            banks = lambda b: X[:, b:b + 2].rearrange("p b (h d) -> p (b h) d", h=GH)

            def gated(dst, tanh, s, done, free):
                dve.wait_ge(w_used, done)
                for x in range(TT):
                    V.scalar_tensor_tensor(dst(x), tanh(x), 1.0, acc[:, s, x], ALU.add, ALU.mult).then_inc(acc_free[s], 1)
                dve.wait_ge(acc_free[s], free)

            dve.sem_inc(lo_ready, LO_CREDIT)
            c.inc(V.memset(upad[:, :, 0:TAPS - 1], 0.0))
            c.wait()
            dve.sem_inc(sem("conv_done"), 1)

            dve.wait_ge(sem("small_landed"), 64)
            c.link(V.tensor_copy(pos_f[:], pos_i[:]))
            f = lambda k: rope_f[:, k].rearrange("p t n -> p (t n)")
            for x in range(TT):
                c.link(V.tensor_scalar(rope_f[:, 0, x], inv_f[:], pos_f[:, x:x + 1], None, ALU.mult))
            MAGIC = 1.5 * 2.0 ** 23
            c.link(V.tensor_scalar(f(1), f(0), 1.0 / TWO_PI, MAGIC, ALU.mult, ALU.add))
            c.link(V.tensor_scalar(f(1), f(1), -MAGIC, None, ALU.add))
            c.link(V.scalar_tensor_tensor(f(2), f(1), -TWO_PI_1, f(0), ALU.mult, ALU.add))
            c.link(V.scalar_tensor_tensor(f(2), f(1), -TWO_PI_2, f(2), ALU.mult, ALU.add))
            c.link(V.scalar_tensor_tensor(f(2), f(1), -TWO_PI_3, f(2), ALU.mult, ALU.add))
            c.link(V.tensor_scalar(f(2), f(2), PI_BELOW, -PI_BELOW, ALU.min, ALU.max))
            dve.sem_inc(sem("prep_ready"), 1)

            dve.wait_ge(sem("rows_tr"), 1)
            for b in range(2):
                c.inc(V.tensor_copy(pc[:, 8 * b:8 * (b + 1), :], X[:, b, 0:8 * N_ROWS].rearrange("p (k r) -> p k r", k=8)))
            c.link(V.tensor_copy(pc2[:], X[:, 2, 0:N_ROWS2]))
            c.inc(V.tensor_scalar(pc[:, :, R_DW:R_DW + TAPS], pc[:, :, R_DW:R_DW + TAPS], 0.5, None, ALU.mult))
            c.inc(V.tensor_scalar(lnh[:], pc[:, :, R_LNG:R_LNG + 2], 0.5, None, ALU.mult))
            c.link(V.tensor_scalar(pc2[:, R2_DN:R2_DN + 1], pc2[:, R2_DN:R2_DN + 1], 0.5, None, ALU.mult))
            dve.sem_inc(sem("prep_ready"), 1)

            dve.wait_ge(sem("row_sq"), ROWS_X)
            sig(V.tensor_tensor(stat[:, 0:2], stat[:, 40:42], stat[:, 42:44], ALU.add), "square_ready", SQ_X)
            for h in range(LEAD - 1):
                split(h)
            dve.wait_ge(sem("rstd_ready"), RSTD_X)
            V.tensor_scalar(xt[:, 1], xt[:, 1], stat[:, 3:4], None, ALU.mult).then_inc(sem("xn_ready"), 1)
            split(LEAD - 1)

            def stationary_lo(hi, lo, kt, src, gain, ready, value):
                dve.wait_ge(sem(ready), value)
                for a in range(2):
                    ins = V.scalar_tensor_tensor(lo[:, kt + a], src[:, a * TOK:(a + 1) * TOK], gain(kt + a),
                                                 hi[:, kt + a].bitcast(F32), ALU.mult, ALU.subtract)
                    if a == 0:
                        c.inc(ins)
                return ins

            for m in range(KT // 2):
                sig(stationary_lo(r1h, r1l, 2 * m, X[:, m % 4], lambda kt: pc[:, kt, R_GPRE:R_GPRE + 1], "op_hi", 2 * OP_HT + m + 1), "op_lo", 2 * OP_HT + m + 1)

            dve.wait_ge(sem("table_ready"), TABLE_SIN)
            ct = cos_t[:].rearrange("p t n -> p (t n)")
            c.link(V.tensor_tensor(ct, f(3), f(3), ALU.mult))
            c.link(V.tensor_scalar(ct, ct, -2.0, 1.0, ALU.mult, ALU.add))

            ph = PH["BA"]
            ahead(ph, 0)
            dve.wait_ge(w_used, used(ph, 0))
            sig(V.tensor_copy(narrow_t[0:2 * HEADS], X[0:2 * HEADS, 3, 0:TOK]), "prep_ready", PREP_NARROW)
            dve.wait_ge(sem("rows_tr"), 2)
            ba = X[:, 3, 0:TT * 2 * HEADS].rearrange("p (t n) -> p t n", t=TT)
            a_in = bat[:, :, HEADS:2 * HEADS]
            c.inc(V.tensor_copy(bat[:, :, 0:HEADS], ba[:, :, 0:HEADS]))
            c.link(V.tensor_tensor(a_in, ba[:, :, HEADS:2 * HEADS], rep(ba_const[:, 1, :], TT), ALU.add))
            c.link(V.tensor_scalar(ba_tmp[:, 1], a_in, -1.0, None, ALU.mult))
            c.inc(V.tensor_tensor(ba_tmp[:, 2], ba_tmp[:, 1], a_in, ALU.min))
            c.link(V.tensor_scalar(ba_tmp[:, 5], a_in, 0.0, None, ALU.max))
            dve.sem_inc(sem("prep_ready"), 1)
            dve.wait_ge(sem("table_ready"), TABLE_SOFTPLUS)
            c.link(V.tensor_scalar(beta[:], ba_tmp[:, 0], 0.5, 0.5, ALU.mult, ALU.add))
            c.inc(V.tensor_scalar(hbeta[:], beta[:], 0.5, None, ALU.mult))
            c.link(V.tensor_tensor(ba_tmp[:, 5], ba_tmp[:, 5], ba_tmp[:, 4], ALU.add))
            c.link(V.scalar_tensor_tensor(glog[:], ba_tmp[:, 5], -1.0, rep(ba_const[:, 0, :], TT), ALU.mult, ALU.mult))
            dve.sem_inc(sem("prep_ready"), 1)
            dve.wait_ge(sem("table_ready"), TABLE_EXP)
            n16 = TT * HEADS
            kf = kend[:].rearrange("p t h -> p (t h)")
            c.link(V.tensor_copy(kf, X[:, 3, 96:96 + n16]))
            c.link(V.tensor_tensor(kf, kf, X[:, 3, 64:64 + n16], ALU.subtract))
            dve.sem_inc(sem("prep_ready"), 1)

            def glu(ph, bl, i, sg_free, value):
                dve.wait_ge(acc_free[0], sg_free)
                if value is not None:
                    dve.wait_ge(sem("uT_tr"), value)
                gated(lambda x: u[:, x], lambda x: sg[:, x], 1, used(ph, 8 * bl + 7, i), freed(ph, bl, i))

            def gate_bias(kind, ph, bl, i, value):
                dve.wait_ge(sem("bias_landed"), 32 * value)
                dve.wait_ge(w_used, used(ph, 8 * bl + 7, i))
                for x in range(TT):
                    V.tensor_tensor((gtA, gtB)[kind][:, x], acc[:, kind, x], bgt[:, kind, :], ALU.add).then_inc(acc_free[kind], 1)

            def tap(k, cur, src, w, out):
                c.wait(tap.apart - 1)
                win = src[..., k:k + TOK]
                c.inc(V.scalar_tensor_tensor(out if k == TAPS - 1 else cur, win, w[:, k:k + 1], cur, ALU.mult, ALU.add))

            def conv_steps(steps, slot, first, last):
                n, m = len(steps), last - first + 1
                if first <= slot <= last:
                    for k, a, i in steps[n * (slot - first) // m:n * (slot - first + 1) // m]:
                        tap(k, ycur[:, a], upad[:, a], pcw[:, a, :], y[:, bass.ds(i * CT + a, 1)].rearrange("p a n -> p (a n)"))

            ph = PH["GLU0"]
            for hl in range(ph.hn):
                ahead(ph, hl)
            glu(ph, 1, 0, freed(ph, 0), None)
            ph = PH["GLU"]
            c.restart()
            with dve.Fori(0, ph.iters) as i:
                steps = [(k, a, i) for k in range(1, TAPS) for a in range(CT)]
                tap.apart = CT
                for hl in range(ph.hn):
                    ahead(ph, hl, i)
                    if hl == 0:
                        c.link(V.tensor_copy(pcw[:], pc[:, bass.ds(i * CT, CT), 0:TAPS + 1]))
                    if hl == 4:
                        dve.wait_ge(sem("upad_ready"), i + 1)
                    if hl == 8:
                        gate_bias(0, ph, 0, i, i + 1)
                    if hl == 16:
                        gate_bias(1, ph, 1, i, i + 1)
                    conv_steps(steps, hl, 4, 31)
                c.wait()
                dve.sem_inc(sem("conv_done"), 1)
                glu(ph, 3, i, freed(ph, 2, i), i + 1)
                c.restart()
            ph = PH["GT3"]
            LAST = NJ - 1
            steps = [(k, a, LAST) for k in range(1, TAPS) for a in range(CT)]
            tap.apart = CT
            for hl in range(ph.hn):
                ahead(ph, hl)
                if hl == 0:
                    c.link(V.tensor_copy(pcw[:], pc[:, LAST * CT:, 0:TAPS + 1]))
                if hl == 4:
                    dve.wait_ge(sem("upad_ready"), NJ)
                if hl == 8:
                    gate_bias(0, ph, 0, 0, NJ)
                conv_steps(steps, hl, 4, 44)
            gate_bias(1, ph, 1, 0, NJ)

            ph = PH["ZB"]

            def z_gate(j):
                dve.wait_ge(sem("tanh_ready"), TANH_ZB + j + 1)
                gated(lambda x: sz0[:, x], lambda x: th0[:, x], j % 2, used(PH["ZB"], 8 * j + 7), freed(PH["ZB"], j))

            for hl in range(ph.hn):
                ahead(ph, hl)
                if at_block(hl, 1) is not None:
                    z_gate(at_block(hl, 1))
                conv_steps(steps, 16 + hl, 4, 44)
                if 16 + hl == 44:
                    c.wait()
                    dve.sem_inc(sem("conv_done"), 1)
            c.restart()

            ph = PH["QKVZ"]

            def own(ph, hl, i):
                if hl == 0:
                    for n in range(3):
                        c.link(V.tensor_copy(wq4[:, n], pc[:, bass.ds(i * GH, GH), R_SC + SHORT * n:R_SC + SHORT * (n + 1)]))
                for n, (_, _, _, (conv, conv_end), silu, back) in enumerate(OWN):
                    if hl == conv:
                        dve.wait_ge(sem("cpad_ready"), i * 3 + (n + 1))
                    if conv <= hl <= conv_end:
                        steps, m = [(k, h) for k in range(SHORT) for h in range(GH)], conv_end - conv + 1
                        for k, h in steps[16 * (hl - conv) // m:16 * (hl - conv + 1) // m]:
                            c.wait(GH - 1)
                            win, w = cpad[:, h, k:k + TOK], wq4[:, n, h, k:k + 1]
                            if k == 0:
                                c.inc(V.tensor_scalar(cy[:, h], win, w, None, ALU.mult))
                            else:
                                c.inc(V.scalar_tensor_tensor(cy[:, h], win, w, cy[:, h], ALU.mult, ALU.add))
                    if hl == conv_end:
                        c.wait()
                        dve.sem_inc(sem("conv4_done"), 1)
                    if hl == silu:
                        dve.wait_ge(sem("cth_ready"), i * 3 + (n + 1))
                        sig(V.scalar_tensor_tensor(flat(cth), flat(cth), 1.0, flat(cy), ALU.add, ALU.mult), "s_ready", i * 3 + (n + 1))
                    if hl == back + 2 and n < 2:
                        dve.wait_ge(sem("qk_sq"), i * 2 + (n + 1))
                        sig(V.tensor_reduce(col(8 + n), cy[:].rearrange("p a n -> p (a n)").rearrange("p (m d) -> p m d", d=DK), AX.X, ALU.add),
                            "qk_square", i * 2 + (n + 1))
                if hl == 31:
                    dve.wait_ge(sem("cols_ready"), i + 1)
                    c.link(V.tensor_tensor(th(ktok), th(ktok), over(col(2), DK), ALU.mult))
                    c.link(V.tensor_tensor(th(kb), th(ktok), over(col(3), DK), ALU.mult))
                    dve.sem_inc(sem("kb_ready"), 1)

            def z_silu(ph, i):
                dve.wait_ge(sem("tanh_ready"), i + (TANH_Z + 1))
                gated(lambda x: sz[:, x].rearrange("p h d -> p (h d)"), lambda x: cth[:, x], 1, used(ph, 31, i), freed(ph, 3, i))

            def delta(hl, dv):
                if hl == 0:
                    sig(V.tensor_tensor(th(gm), rep(tri_incl[:], TC2), over(col(7), P), ALU.mult), "gm_ready", dv(1, 1))
                if hl == 2:
                    c.link(V.tensor_tensor(th(qtok), th(qtok), over(col(0), DK), ALU.mult))
                    sig(V.tensor_tensor(th(qd), th(qtok), over(col(1), DK), ALU.mult), "q_scaled", dv(1, 1))
                if hl == 8:
                    c.inc(V.tensor_tensor(th(kbe), th(ktok), over(col(4), DK), ALU.mult))
                if hl == 10:
                    sig(V.tensor_tensor(th(ke), th(ktok), over(col(5), DK), ALU.mult), "k_scaled", dv(1, 1))
                    c.wait()
                if hl == 1:
                    dve.wait_ge(sem("kbT_tr"), dv(1, 1))
                    sig(V.tensor_copy(th(kbT), banks(2)), "kbT_ready", dv(1, 1))
                if hl == 3:
                    dve.wait_ge(sem("B_done"), dv(1, 1))
                    dve.wait_ge(sem("decT_ready"), dv(2, 2))
                    sig(V.tensor_tensor(th(bf), banks(2), th(decT), ALU.mult), "bf_ready", dv(1, 1))
                    c.inc(V.tensor_tensor(th(decT), th(decT), rep(tri_incl[:], TC2), ALU.mult))
                    c.link(V.tensor_tensor(th(xs), th(bf), rep(m1u[:], TC2), ALU.mult))
                    sig(V.tensor_tensor(th(uinv), rep(ident[:], TC2), th(xs), ALU.subtract), "uinv_ready", dv(1, 1))
                if hl == 4:
                    dve.wait_ge(sem("qdT_tr"), dv(1, 1))
                    sig(V.tensor_copy(th(qdT), banks(2)), "qdT_ready", dv(1, 1))
                if hl == 5:
                    dve.wait_ge(sem("qk_done"), dv(1, 1))
                    sig(V.tensor_tensor(th(qkT), banks(0), th(decT), ALU.mult), "qkT_ready", dv(1, 1))
                for l in range(LEVELS):
                    if hl == 6 + 2 * l:
                        dve.wait_ge(sem("lx_done"), dv(LEVELS, l + 1))
                        sig(V.tensor_tensor(th(xs), banks(0), rep(lvl[:, l, :], TC2), ALU.mult), "xs_ready", dv(LEVELS, l + 1))
                    if hl == 7 + 2 * l:
                        dve.wait_ge(sem("ly_done"), dv(LEVELS, l + 1))
                        s = 4 << l
                        late = lambda ap: ap.rearrange("p t h (b s) -> p (t h b) s", s=s)[:, :, s // 2:]
                        early = lambda ap: ap.rearrange("p t h (b s) -> p (t h b) s", s=s)[:, :, 0:s // 2]
                        bank4 = lambda b: X[:, b:b + 2].rearrange("p t (h d) -> p t h d", h=GH)
                        ins = V.tensor_tensor(late(uinv[:]), late(uinv[:]), late(bank4(0)), ALU.subtract)
                        if l < LEVELS - 1:
                            c.inc(ins)
                            ins = V.tensor_tensor(early(tinv[:]), early(tinv[:]), early(bank4(2)), ALU.subtract)
                        sig(ins, "inv_ready", dv(LEVELS, l + 1))
                        c.wait()
                for n in range(NCH):
                    x, rows = n // 2, slice(n % 2 * SEQ_CHUNK, (n % 2 + 1) * SEQ_CHUNK)
                    if hl == 17 + 2 * n and n:
                        dve.wait_ge(sem("scan_done"), dv(SCAN, 2 * n))
                        v = us[rows, x].rearrange("p h d -> p (h d)")
                        sig(V.tensor_tensor(v, v, X[rows, 0], ALU.subtract), "scan_ready", dv(SCAN, 2 * n))
                    if hl == 18 + 2 * n and n < NCH - 1:
                        dve.wait_ge(sem("scan_done"), dv(SCAN, 2 * n + 1))
                        if n == 0:
                            sig(V.tensor_copy(state[:].rearrange("p h d -> p (h d)"), X[:, 0]), "scan_ready", dv(SCAN, 1))
                        else:
                            for h in range(GH):
                                ins = V.scalar_tensor_tensor(state[:, h], state[:, h], degl[:, x, n % 2, h:h + 1],
                                                             X[:, 0, h * DK:(h + 1) * DK], ALU.mult, ALU.add)
                                if h < GH - 1:
                                    c.inc(ins)
                            sig(ins, "scan_ready", dv(SCAN, 2 * n + 1))
                            c.wait()
                if hl == 25:
                    dve.wait_ge(sem("o_sq"), dv(2, 1))
                    sig(V.tensor_reduce(col(11), th(xs), AX.X, ALU.add), "o_square", dv(1, 1))
                if hl == 28:
                    dve.wait_ge(sem("o_sq"), dv(2, 2))
                    sig(V.tensor_tensor(th(otok), th(otok), th(sz), ALU.mult), "o_gated", dv(1, 1))
                if hl == 31:
                    for q in range(2):
                        dve.wait_ge(sem("oT_hi"), dv(2, q + 1))
                        sig(V.scalar_tensor_tensor(ol[:, 2 * q:2 * q + 2], X[:, q].rearrange("p (a b) -> p a b", a=2), pc2[:, R2_DN:R2_DN + 1],
                                                   oh[:, 2 * q:2 * q + 2].bitcast(F32), ALU.mult, ALU.subtract), "oT_lo", dv(2, q + 1))

            dve.wait_ge(sem("gate_out"), 32 * NJ)
            dve.wait_ge(sem("mask_ready"), MASK_LVL)
            c.link(V.memset(cpad[:, :, 0:SHORT - 1], 0.0))
            dve.sem_inc(sem("conv4_done"), 1)
            q4 = lambda tile, q: tile[:, CT * q:CT * (q + 1)]
            for hl in range(ph.hn):
                ahead(ph, hl)
                if hl == 1:
                    z_gate(NJ - 1)
                own(ph, hl, 0)
                if hl == 8:
                    dve.wait_ge(sem("ln_sq_used"), NJ)
                    sig(V.tensor_copy(var[:], X[:, 0:TT, 0]), "square_ready", SQ_LN)
                if hl == 9:
                    dve.wait_ge(sem("rstd_ready"), RSTD_LN)
                    for x in range(TT):
                        c.inc(V.tensor_scalar(rdiag[:, x], ident[:], var[:, x:x + 1], float(D), ALU.mult, ALU.mult))
                    c.wait()
                    dve.sem_inc(sem("rdiag_ready"), 1)
                if hl in LN_SILU:
                    q = LN_SILU.index(hl)
                    dve.wait_ge(sem("ln_value"), 2 * (q + 1))
                    sig(V.scalar_tensor_tensor(lnt[:], lnt[:], 1.0, lnsq[:], ALU.add, ALU.mult), "ln_silu", q + 1)
                if hl in LN_LO:
                    q = LN_LO.index(hl)
                    dve.wait_ge(sem("ln_hi"), q + 1)
                    sig(V.tensor_tensor(lul[:], lnt[:], luh[:].bitcast(F32), ALU.subtract), "ln_lo", q + 1)
            z_silu(ph, 0)
            c.restart()
            with dve.Fori(1, NJ) as i:
                dv = lambda per, n: i * per + (n - per)
                for hl in range(ph.hn):
                    ahead(ph, hl, i)
                    delta(hl, dv)
                    own(ph, hl, i)
                z_silu(ph, i)
                c.restart()

            ph = PH["YB"]
            dv = lambda per, n: (NJ - 1) * per + n

            def branch_b(j):
                dve.wait_ge(sem(f"tile_landed{j % 2}"), 16 * (j // 2 + 1))
                gated(lambda x: gy[:, x, j * NB:(j + 1) * NB], lambda x: gth[j % 2][:, x].rearrange("p h d -> p (h d)"),
                      j % 2, used(ph, 8 * j + 7), freed(ph, j))
                dve.sem_inc(sem("gy_ready"), 1)

            for hl in range(ph.hn):
                ahead(ph, hl)
                delta(hl, dv)
                if hl and hl % 8 == 0:
                    branch_b(hl // 8 - 1)
            branch_b(NJ - 1)

            def merge(j):
                dve.wait_ge(sem(f"tile_landed{j % 2}"), 16 * (j // 2) + 48)
                gated(lambda x: mtmp[:, x], lambda x: gth[j % 2][:, x].rearrange("p h d -> p (h d)"), j % 2,
                      used(PH["YA"], 8 * j + 7), freed(PH["YA"], j))
                sig(V.tensor_tensor(mtmp, mtmp, gy[:, :, j * NB:(j + 1) * NB], ALU.add), "m_ready", OP_M + j + 1)

            def merged_lo(hi, lo, j, base):
                for q in range(2):
                    dve.wait_ge(sem("m_hi"), 2 * (base + j) + q + 1)
                    kt = slice(CT * j + 2 * q, CT * j + 2 * q + 2)
                    sig(V.scalar_tensor_tensor(lo[:, kt], X[:, q].rearrange("p (a b) -> p a b", a=2), 0.5,
                                               hi[:, kt].bitcast(F32), ALU.mult, ALU.subtract), "m_lo", 2 * (base + j) + q + 1)

            ph = PH["YA"]
            for hl in range(ph.hn):
                ahead(ph, hl)
                if at_block(hl, 0) is not None:
                    merge(at_block(hl, 0))
                if at_block(hl, 2) is not None:
                    merged_lo(r2h, r2l, at_block(hl, 2), OP_M)

            dve.wait_ge(sem("p_hi"), 1)
            sig(V.tensor_tensor(flat(pTl), X[:, 2], flat(pTh).bitcast(F32), ALU.subtract), "p_lo", 1)
            ph = PH["MIX"]

            def mix_gain(j):
                js = slice(j * NB, (j + 1) * NB)
                dve.wait_ge(acc_free[j % 2], freed(PH["MIX"], j))
                c.link(V.tensor_tensor(mix[:, :, js], mix[:, :, js], rep(gpost[:, js], TT), ALU.mult))

            dve.wait_ge(sem("gains_landed"), 32)
            for hl in range(ph.hn):
                ahead(ph, hl)
                if hl == 0:
                    merge(NJ - 1)
                if hl == 2:
                    merged_lo(r2h, r2l, NJ - 1, OP_M)
                if at_block(hl, 1) is not None:
                    mix_gain(at_block(hl, 1))
            squares = lambda k: stat[:, k:k + TT * NJ].rearrange("p (t j) -> p t j", t=TT)
            dve.wait_ge(acc_free[1], freed(ph, NJ - 1))
            sig(V.tensor_reduce(stat[:, 4:6], squares(16), AX.X, ALU.add), "square_ready", SQ_MIX)
            mix_gain(NJ - 1)

            ph = PH["PLEP"]
            for hl in range(ph.hn):
                ahead(ph, hl)
            dve.wait_ge(sem("rstd_ready"), RSTD_MIX)

            def lo_block(hi, lo, j, gain, base):
                for q in range(2):
                    sig(stationary_lo(hi, lo, CT * j + 2 * q, X[:, 2 * (j % 2) + q], gain, "op_hi", 2 * (base + j) + q + 1),
                        "op_lo", 2 * (base + j) + q + 1)

            for j in range(NJ):
                js = slice(j * NB, (j + 1) * NB)
                dve.wait_ge(sem(f"tile_landed{j % 2}"), 64 + 16 * (j // 2 + 1))
                c.inc(V.scalar_tensor_tensor(mix[:, 0, js], mix[:, 0, js], stat[:, 6:7], xres[:, j % 2, 0], ALU.mult, ALU.add))
                sig(V.scalar_tensor_tensor(mix[:, 1, js], mix[:, 1, js], stat[:, 7:8], xres[:, j % 2, 1], ALU.mult, ALU.add), "op_ready", j + 1)
                if j:
                    lo_block(r1h, r1l, j - 1, lambda kt: 1.0, OP_X1)
                if j in (1, 2):
                    ahead(PH["PLEG"], j - 1)
            lo_block(r1h, r1l, NJ - 1, lambda kt: 1.0, OP_X1)

            ph = PH["PLEG"]

            def ple(j):
                js = slice(j * NB, (j + 1) * NB)
                dve.wait_ge(sem("tanh_ready"), TANH_PLE + j + 1)
                for x in range(TT):
                    V.scalar_tensor_tensor(e[:, x, js], pth[:, x], 1.0, e[:, x, js], ALU.add, ALU.mult).then_inc(acc_free[j % 2], 1)
                dve.wait_ge(acc_free[j % 2], freed(ph, j))
                dve.sem_inc(sem("ple_gated"), 1)

            gained = lambda j: e[:, :, j * NB:(j + 1) * NB] if j < NJ - 1 else xres[:, 0]

            def ple_gain(j):
                js = slice(j * NB, (j + 1) * NB)
                c.link(V.tensor_tensor(gained(j), e[:, :, js], rep(gple[:, js], TT), ALU.mult))

            for hl in range(ph.hn):
                if hl >= 2:
                    ahead(ph, hl)
                if at_block(hl, 1) is not None:
                    ple(at_block(hl, 1))
                if at_block(hl, 2) is not None:
                    dve.wait_ge(sem("row_sq"), ROWS_X + 2 * at_block(hl, 2) + 2)
                    ple_gain(at_block(hl, 2))
            ple(NJ - 1)
            ple_gain(NJ - 1)
            dve.wait_ge(sem("row_sq"), ROWS_PLE)
            sig(V.tensor_reduce(stat[:, 8:10], squares(24), AX.X, ALU.add), "square_ready", SQ_PLE)
            dve.wait_ge(sem("rstd_ready"), RSTD_PLE)
            for j in range(NJ):
                js = slice(j * NB, (j + 1) * NB)
                c.inc(V.scalar_tensor_tensor(mix[:, 0, js], gained(j)[:, 0], stat[:, 10:11], mix[:, 0, js], ALU.mult, ALU.add))
                sig(V.scalar_tensor_tensor(mix[:, 1, js], gained(j)[:, 1], stat[:, 11:12], mix[:, 1, js], ALU.mult, ALU.add),
                    "op_ready", OP_H2 - OP_X1 + j + 1)
                if j:
                    lo_block(r2h, r2l, j - 1, lambda kt: pc[:, kt, R_GPRE2:R_GPRE2 + 1], OP_H2)
                if j in (1, 2):
                    ahead(PH["QA"], j - 1)
            lo_block(r2h, r2l, NJ - 1, lambda kt: pc[:, kt, R_GPRE2:R_GPRE2 + 1], OP_H2)
            rstd2 = lambda x: stat[:, 14 + x:15 + x]
            rstd2_squared = lambda x: stat[:, 42 + x:43 + x]

            def rope(x1, x2, dst, cos, sin, t1, t2):
                c.inc(V.tensor_tensor(t1, x1, cos, ALU.mult))
                c.link(V.tensor_tensor(t2, x2, sin, ALU.mult))
                c.link(V.tensor_tensor(dst[..., 0:ROPE // 2], t1, t2, ALU.subtract))
                c.inc(V.tensor_tensor(t1, x1, sin, ALU.mult))
                c.link(V.tensor_tensor(t2, x2, cos, ALU.mult))
                c.link(V.tensor_tensor(dst[..., ROPE // 2:], t1, t2, ALU.add))

            def scaled(tile, at, rstd_value, value):
                dve.wait_ge(sem("rstd_ready"), rstd_value)
                c.inc(V.tensor_scalar(tile[:, 0], tile[:, 0], stat[:, at:at + 1], None, ALU.mult))
                sig(V.tensor_scalar(tile[:, 1], tile[:, 1], stat[:, at + 1:at + 2], None, ALU.mult), "op_ready", OP_LAT - OP_X1 + value)

            gain = lambda kt: pc2[:, kt:kt + 1]
            for hl in range(PH["QA"].hn):
                if hl >= 2:
                    ahead(PH["QA"], hl)
                if hl == 5:
                    dve.wait_ge(sem("row_sq"), ROWS_PLE + TT * NJ)
                    sig(V.tensor_reduce(stat[:, 12:14], squares(32), AX.X, ALU.add), "square_ready", SQ_X2)
            ahead(PH["KR"], 0)
            dve.wait_ge(sem("x2_out"), 16)
            dve.wait_ge(w_used, used(PH["KR"], 0))
            sig(V.tensor_copy(krT[0:ROPE], X[0:ROPE, 3, 0:TOK]), "kr_ready", 1)
            for hl in range(PH["KVA"].hn):
                ahead(PH["KVA"], hl)
                if hl == 1:
                    dve.wait_ge(sem("kr_tr"), 1)
                    dve.wait_ge(sem("rstd_ready"), RSTD_X2)
                    k = X[:, 3, 0:TT * ROPE].rearrange("p (t n) -> p t n", t=TT)
                    rope(k[:, :, 0:ROPE // 2], k[:, :, ROPE // 2:], qr[:, :, 0], cos_t[:], sin_t[:], rtmp[:, 0, :, 0], rtmp[:, 1, :, 0])
                    for x in range(TT):
                        c.link(V.tensor_scalar(qr[:, x, 1], qr[:, x, 0], rstd2(x), None, ALU.mult))
                    sig(V.tensor_copy(qr[:, :, 0], qr[:, :, 1]), "kr_ready", 2)
                if hl == 2:
                    scaled(qa_t, 48, RSTD_QA, 1)
                if hl == 3:
                    dve.wait_ge(sem("kr_tr"), 2)
                    sig(V.tensor_copy(krT[:], X[:, 3, 0:TOK]), "krT_ready", 1)
                if hl == 4:
                    lo_block(r1h, r1l, 0, gain, OP_LAT)
            scaled(kva_t, 50, RSTD_KV, 2)
            lo_block(r1h, r1l, 1, gain, OP_LAT)
            c.link(V.memset(u2pad[:, :, 0:TAPS2 - 1], 0.0))
            dve.wait_ge(sem("mask_ready"), MASK_CAUSAL)

            ph = PH["FC"]
            c.restart()
            with dve.Fori(0, ph.iters) as i:
                for hl in range(ph.hn):
                    ahead(ph, hl, i)
                    if hl == 0:
                        c.link(V.tensor_copy(wc2[:], pc[:, bass.ds(i * CT, CT), R_CW2:R_CW2 + TAPS2]))
                    if hl == 5:
                        dve.wait_ge(acc_free[1], freed(ph, 1, i))
                        for x in range(TT):
                            q = qst[:, x].rearrange("p (h d) -> p h d", h=GH)
                            rope(q[:, :, NOPE:NOPE + ROPE // 2], q[:, :, NOPE + ROPE // 2:], qr[:, x], rep(cos_t[:, x], GH), rep(sin_t[:, x], GH),
                                 rtmp[:, 0, x], rtmp[:, 1, x])
                        dve.sem_inc(sem("qr_ready"), 1)
                    if hl == 8:
                        dve.wait_ge(sem("qr_tr"), i + 1)
                        sig(V.tensor_copy(qrT[:].rearrange("p a n -> p (a n)"), X[:, 2]), "qrT_ready", i + 1)
                    if hl == 12:
                        dve.wait_ge(sem("sc_done"), i + 1)
                        c.link(V.tensor_tensor(sc[:], X[:, 0:GH, 0:SCORES], rep(amask[:], GH), ALU.add))
                    if hl == 13:
                        c.inc(V.tensor_reduce(mx[:, 0], sc[:, :, 0:P], AX.X, ALU.max))
                        c.link(V.tensor_reduce(mx[:, 1], sc[:, :, P:SCORES], AX.X, ALU.max))
                        sig(V.tensor_scalar(nmx[:], mx[:], -ATT_SCALE, None, ALU.mult), "smax_ready", i + 1)
                    if hl == 17:
                        dve.wait_ge(sem("pT_tr"), i + 1)
                        c.link(V.reciprocal(rec[:], den[:]))
                        sig(V.tensor_copy(pT[:, 2:4], X[:, 2:4, 0:SCORES]), "pT_ready1", i + 1)
                    if hl == 19:
                        dve.wait_ge(sem("pv_done"), i + 1)
                        dve.wait_ge(sem("ost_free"), i + 1)
                        sig(V.tensor_tensor(th(ost), banks(0), over(rec[:].rearrange("p t h -> p (t h)"), VD), ALU.mult), "ost_ready", i + 1)
                    if hl == 24:
                        dve.wait_ge(acc_free[0], freed(ph, 4, i))
                        dve.wait_ge(w_used, used(ph, 23, i))
                        for x in range(TT):
                            V.scalar_tensor_tensor(cg[:, x], acc[:, 1, x], rstd2(x), cg[:, x], ALU.mult, ALU.mult).then_inc(acc_free[1], 1)
                    if hl in (27, 28):
                        dve.wait_ge(sem("u2_ready"), i + 1)
                        steps = [(k, a) for k in range(TAPS2) for a in range(CT)]
                        for k, a in steps[6 * (hl - 27):6 * (hl - 26)]:
                            c.wait(CT - 1)
                            win, w = u2pad[:, a, k:k + TOK], wc2[:, a, k:k + 1]
                            if k == 0:
                                c.inc(V.tensor_scalar(c3[:, a], win, w, None, ALU.mult))
                            else:
                                c.inc(V.scalar_tensor_tensor(c3[:, a], win, w, c3[:, a], ALU.mult, ALU.add))
                    if hl == 33:
                        dve.wait_ge(sem("tanh_ready"), i + (TANH_ZC + 1))
                        gated(lambda x: zs[:, x], lambda x: zs[:, x], 0, used(ph, 31, i), freed(ph, 6, i))
                dve.wait_ge(w_used, used(ph, 39, i))
                for x in range(TT):
                    V.scalar_tensor_tensor(zs[:, x], acc[:, 1, x], rstd2_squared(x), zs[:, x], ALU.mult, ALU.mult).then_inc(acc_free[1], 1)
                dve.wait_ge(sem("bz_tr"), i + 1)
                c.wait()
                for q in range(2):
                    cq = c3[:, 2 * q:2 * q + 2].rearrange("p a b -> p (a b)")
                    c.link(V.scalar_tensor_tensor(cq, X[:, 2 + q], 0.5, cq, ALU.mult, ALU.mult))
                dve.sem_inc(sem("c_ready"), 1)
                dve.wait_ge(sem("c_hi"), i + 1)
                sig(V.tensor_tensor(r1l[:, 2 * CT:3 * CT], c3[:], r1h[:, 2 * CT:3 * CT].bitcast(F32), ALU.subtract), "c_lo", i + 1)
                c.restart()

            ph = PH["FG"]
            with dve.Fori(0, ph.iters) as i:
                for hl in range(ph.hn):
                    ahead(ph, hl, i)

            def attn_gate(j):
                dve.wait_ge(sem("tanh_ready"), TANH_ZM + j + 1)
                dve.wait_ge(sem(f"tile_landed{j % 2}"), 16 * (j // 2) + 112)
                gated(lambda x: thz[:, x], lambda x: thz[:, x], j % 2, used(PH["FZ"], 8 * j + 7), freed(PH["FZ"], j))
                c.inc(V.scalar_tensor_tensor(oin[:, j % 2, 0], thz[:, 0], rstd2(0), oin[:, j % 2, 0], ALU.mult, ALU.mult))
                sig(V.scalar_tensor_tensor(oin[:, j % 2, 1], thz[:, 1], rstd2(1), oin[:, j % 2, 1], ALU.mult, ALU.mult), "m_ready", OP_ATTN + j + 1)

            def heads_steps(hl):
                if at_block(hl, 1) is not None:
                    attn_gate(at_block(hl, 1))
                if at_block(hl, 3) is not None:
                    merged_lo(r1h, r1l, at_block(hl, 3), OP_ATTN)

            for hl in range(PH["FZ"].hn):
                ahead(PH["FZ"], hl)
                heads_steps(hl)

            def gated_attn(j):
                js = slice(j * NB, (j + 1) * NB)
                gated(lambda x: thm[:, x, js], lambda x: thm[:, x, js], j % 2, used(PH["YM"], 8 * j + 7), freed(PH["YM"], j))

            def merge2(j):
                js = slice(j * NB, (j + 1) * NB)
                gated(lambda x: thz[:, x], lambda x: thc[:, x, js], j % 2, used(PH["YC"], 8 * j + 7), freed(PH["YC"], j))
                sig(V.tensor_tensor(thz[:], thz[:], thm[:, :, js], ALU.add), "m_ready", OP_Y + j + 1)

            for hl in range(PH["YM"].hn):
                ahead(PH["YM"], hl)
                if hl < 4:
                    heads_steps(PH["FZ"].hn + hl)
                if at_block(hl, 0) is not None:
                    gated_attn(at_block(hl, 0))
            for hl in range(PH["YC"].hn):
                ahead(PH["YC"], hl)
                if hl == 0:
                    gated_attn(NJ - 1)
                if at_block(hl, 0) is not None:
                    merge2(at_block(hl, 0))
                if at_block(hl, 2) is not None:
                    merged_lo(r1h, r1l, at_block(hl, 2), OP_Y)

            ph = PH["OUT"]

            def out_gain(j):
                js = slice(j * NB, (j + 1) * NB)
                dve.wait_ge(acc_free[j % 2], freed(PH["OUT"], j))
                c.link(V.tensor_tensor(outst[:, :, js], outst[:, :, js], rep(gpost2[:, js], TT), ALU.mult))

            dve.wait_ge(sem("gains_landed"), 48)
            for hl in range(ph.hn):
                ahead(ph, hl)
                if at_block(hl, 1) is not None:
                    out_gain(at_block(hl, 1))
                if hl == 0:
                    merge2(NJ - 1)
                if hl == 2:
                    merged_lo(r1h, r1l, NJ - 1, OP_Y)
            dve.wait_ge(acc_free[1], freed(ph, NJ - 1))
            sig(V.tensor_reduce(stat[:, 60:62], squares(52), AX.X, ALU.add), "square_ready", SQ_OUT)
            out_gain(NJ - 1)
            dve.wait_ge(sem("rstd_ready"), RSTD_OUT)
            dve.wait_ge(sem("x2_landed"), 16)
            for j in range(NJ):
                js = slice(j * NB, (j + 1) * NB)
                c.inc(V.scalar_tensor_tensor(outst[:, 0, js], outst[:, 0, js], stat[:, 62:63], x2r[:, 0, js], ALU.mult, ALU.add))
                sig(V.scalar_tensor_tensor(outst[:, 1, js], outst[:, 1, js], stat[:, 63:64], x2r[:, 1, js], ALU.mult, ALU.add), "out_ready", j + 1)

        @block.tensor
        def _(pe):
            T = nc.tensor
            r1, r2 = (r1h, r1l), (r2h, r2l)

            def gemm(ph, hl, i, ops, kt0, bl, start, stop, n=NB, off=0, kts=2):
                h, b = ph.h0 + hl, ph.b0 + bl
                s = b % 2
                pe.wait_ge(lo_ready, LO_CREDIT + h + 1 + i * ph.hn)
                if start and b >= 2:
                    pe.wait_ge(acc_free[s], 2 * (b // 2) + i * ph.bn)
                for k in range(kts):
                    at = slice(k * NB + off, k * NB + off + n)
                    for x in range(TT):
                        xs_ = slice(x * P, (x + 1) * P)
                        for m, (a, w) in enumerate(((ops[0], w_hi), (ops[0], w_lo), (ops[1], w_hi))):
                            ins = T.matmul(acc[:, s, x, 0:n], a[:, kt0 + k, xs_], w[:, h % HL, at],
                                           start=start and k == 0 and m == 0, stop=stop and k == kts - 1 and m == 2)
                ins.then_inc(w_used, 1)

            def model_half(ph, hl, i, ops, hl0=0, bl0=0):
                bl, q = divmod(hl - hl0, 8)
                gemm(ph, hl, i, ops, 2 * q, bl0 + bl, q == 0, q == 7)

            def narrow(ph, ops, n, bank):
                pe.wait_ge(lo_ready, LO_CREDIT + ph.h0 + 1)
                for kt in range(KT):
                    cols_ = slice(kt * n, (kt + 1) * n)
                    for m, (a, w) in enumerate(((ops[0], w_hi), (ops[0], w_lo), (ops[1], w_hi))):
                        ins = T.matmul(X[0:n, bank, 0:TOK], w[:, ph.h0 % HL, cols_], a[:, kt, :],
                                       start=kt == 0 and m == 0, stop=kt == KT - 1 and m == 2)
                ins.then_inc(w_used, 1)

            def narrow_tr(src, n, bank):
                for x in range(TT):
                    ins = T.transpose(X[:, bank, x * n:(x + 1) * n], src[0:n, x * P:(x + 1) * P], ident[0:n, 0:n])
                return ins

            def channels_first(src, bank):
                for a in range(CT):
                    for x in range(TT):
                        ins = T.transpose(X[:, bank + a // 2, (a % 2) * TOK + x * P:(a % 2) * TOK + (x + 1) * P],
                                          src(x, a), ident[:])
                return ins

            def cols(tile):
                return lambda x, a: tile[:, x, a * P:(a + 1) * P]

            pe.sem_inc(w_used, HL)
            pe.wait_ge(sem("mask_ready"), MASK_IDENT)
            pe.wait_ge(sem("rows_landed"), 16 * 13)
            for kt in range(KT):
                T.transpose(X[:, kt // 8, kt % 8 * N_ROWS:(kt % 8 + 1) * N_ROWS], crow[:, kt * P:(kt + 1) * P], ident[0:N_ROWS, 0:N_ROWS])
            T.transpose(X[:, 2, 0:N_ROWS2], crow2[:], ident[0:N_ROWS2, 0:N_ROWS2]).then_inc(sem("rows_tr"), 1)

            pe.wait_ge(sem("xn_ready"), TT)
            pe.wait_ge(sem("prep_ready"), PREP_PC)
            for m in range(KT // 2):
                if m >= 4:
                    pe.wait_ge(sem("op_lo"), 2 * OP_HT + m - 3)
                for a in range(2):
                    for x in range(TT):
                        ins = T.transpose(X[:, m % 4, a * TOK + x * P:a * TOK + (x + 1) * P], xt[:, x, (2 * m + a) * P:(2 * m + a + 1) * P], ident[:])
                ins.then_inc(sem("xT_tr"), 1)
            pe.wait_ge(sem("op_lo"), 2 * (OP_HT + NJ))

            narrow(PH["BA"], r1, 2 * HEADS, 3)
            pe.wait_ge(sem("prep_ready"), PREP_NARROW)
            narrow_tr(narrow_t, 2 * HEADS, 3).then_inc(sem("rows_tr"), 1)

            def log_decays():
                pe.wait_ge(sem("mask_ready"), MASK_TRI)
                pe.wait_ge(sem("prep_ready"), PREP_GLOG)
                for x in range(TT):
                    T.matmul(X[:, 3, 64 + x * HEADS:64 + (x + 1) * HEADS], tri_incl[:], glog[:, x], start=True, stop=True)
                    T.matmul(X[:, 3, 96 + x * HEADS:96 + (x + 1) * HEADS], same[:], glog[:, x], start=True, stop=True)
                    for n in range(2):
                        at = 128 + (2 * x + n) * HEADS
                        ins = T.matmul(X[:, 3, at:at + HEADS], half_ones[:, n, :], glog[:, x], start=True, stop=True)
                ins.then_inc(sem("gc_done"), 1)

            def u_transposed(ph, i):
                pe.wait_ge(acc_free[1], freed(ph, -1, i))
                channels_first(cols(u), 0).then_inc(sem("uT_tr"), 1)

            ph = PH["GLU0"]
            for hl in range(ph.hn):
                model_half(ph, hl, 0, r1)
                if hl == 1:
                    log_decays()
            ph = PH["GLU"]
            with pe.Fori(0, ph.iters) as i:
                for hl in range(ph.hn):
                    model_half(ph, hl, i, r1)
                    if hl == 2:
                        u_transposed(ph, i)
            ph = PH["GT3"]
            for hl in range(ph.hn):
                model_half(ph, hl, 0, r1)
                if hl == 2:
                    u_transposed(ph, 0)

            ph = PH["ZB"]

            def z_transposed(j):
                pe.wait_ge(acc_free[j % 2], freed(PH["ZB"], j))
                channels_first(cols(sz0), 2).then_inc(sem("zT_tr"), 1)

            for hl in range(ph.hn):
                model_half(ph, hl, 0, r1)
                if at_block(hl, 2) is not None:
                    z_transposed(at_block(hl, 2))

            ph = PH["QKVZ"]

            def own(ph, hl, i):
                for n, (_, to_channels, _, _, _, back) in enumerate(OWN):
                    if hl == to_channels:
                        pe.wait_ge(acc_free[n % 2], freed(ph, n, i))
                        if n == 1:
                            pe.wait_ge(sem("tok_ready"), i * 2 + 1)
                        channels_first(cols(praw), OWN_BANKS[n]).then_inc(sem("ch_tr"), 1)
                    if hl == back:
                        pe.wait_ge(sem("s_ready"), i * 3 + (n + 1))
                        pf = cth[:].rearrange("p a b -> p (a b)")
                        for x in range(TT):
                            for h in range(GH):
                                ins = T.transpose(X[:, 2 + x, h * DK:(h + 1) * DK], pf[:, h * TOK + x * P:h * TOK + (x + 1) * P], ident[:])
                        ins.then_inc(sem("tok_tr"), 1)

            PAIRS = [(x, h) for x in range(TT) for h in range(GH)]

            def per_head(bank, lhsT, rhs):
                for x, h in PAIRS:
                    ins = T.matmul(X[:, bank + x, h * P:(h + 1) * P], lhsT[:, x, h], rhs[:, x, h], start=True, stop=True)
                return ins

            def per_head_tr(bank, src, name=None):
                for x, h in PAIRS:
                    ins = T.transpose(X[:, bank + x, h * P:(h + 1) * P], src[:, x, h], ident[:])
                    if name is not None and h == GH - 1:
                        ins.then_inc(sem(name), 1)
                return ins

            def delta(hl, dv, i=None):
                if hl == 0:
                    pe.wait_ge(sem("kb_ready"), dv(1, 1))
                    per_head_tr(0, ktok, "kT_tr")
                    pe.wait_ge(sem("vb_ready"), dv(1, 1))
                    per_head_tr(2, kb).then_inc(sem("kbT_tr"), 1)
                if hl == 1:
                    pe.wait_ge(sem("kT_ready"), dv(2, 2))
                    pe.wait_ge(sem("gm_ready"), dv(1, 1))
                    for x in range(TT):
                        T.matmul(X[:, x], strict_lo[:], gm[:, x].rearrange("p h i -> p (h i)"), start=True, stop=True).then_inc(sem("decay_done"), 1)
                if hl == 2:
                    pe.wait_ge(sem("kbT_ready"), dv(1, 1))
                    per_head(2, kT, kbT).then_inc(sem("B_done"), 1)
                if hl == 3:
                    pe.wait_ge(sem("decT_ready"), dv(2, 2))
                    pe.wait_ge(sem("q_scaled"), dv(1, 1))
                    per_head_tr(0, qtok, "qT_tr")
                    pe.wait_ge(sem("bf_ready"), dv(1, 1))
                    per_head_tr(2, qd).then_inc(sem("qdT_tr"), 1)
                if hl == 4:
                    pe.wait_ge(sem("qT_ready"), dv(2, 2))
                    per_head(0, kT, qT).then_inc(sem("qk_done"), 1)
                    pe.wait_ge(sem("uinv_ready"), dv(1, 1))
                    pe.wait_ge(sem("qdT_ready"), dv(1, 1))
                    per_head_tr(2, uinv, "tinv_tr")
                for l in range(LEVELS):
                    if hl == 5 + 2 * l:
                        if l == 0:
                            pe.wait_ge(sem("qkT_ready"), dv(1, 1))
                            pe.wait_ge(sem("tinv_ready"), dv(2, 2))
                        else:
                            pe.wait_ge(sem("inv_ready"), dv(LEVELS, l))
                        per_head(0, bf, tinv).then_inc(sem("lx_done"), 1)
                    if hl == 6 + 2 * l:
                        pe.wait_ge(sem("xs_ready"), dv(LEVELS, l + 1))
                        ins = per_head(0, xs, uinv)
                        if l < LEVELS - 1:
                            if hl == 10 and i is not None:
                                pe.wait_ge(sem("cpad_ready"), i * 3 + 1)
                            ins = per_head(2, uinv, xs)
                        ins.then_inc(sem("ly_done"), 1)
                if hl == 15:
                    pe.wait_ge(sem("inv_ready"), dv(LEVELS, LEVELS))
                    pe.wait_ge(sem("k_scaled"), dv(1, 1))
                    for x, h in PAIRS:
                        ins = T.matmul(X[:, x, h * P:(h + 1) * P], uinv[:, x, h], vb[:, x, h], start=True, stop=True)
                        if h == GH - 1:
                            ins.then_inc(sem("uw_done"), 1)
                    for x, h in PAIRS:
                        ins = T.matmul(X[:, 2 + x, h * P:(h + 1) * P], kbe[:, x, h], uinv[:, x, h], start=True, stop=True)
                        if h == GH - 1:
                            ins.then_inc(sem("uw_done"), 1)
                for n in range(NCH):
                    x, rows = n // 2, slice(n % 2 * SEQ_CHUNK, (n % 2 + 1) * SEQ_CHUNK)
                    hs = [slice(h * DK, (h + 1) * DK) for h in range(GH)]
                    if hl == 16 + 2 * n and n:
                        pe.wait_ge(sem("scan_ready"), dv(SCAN, 2 * n - 1))
                        for h in range(GH):
                            ins = T.matmul(X[:, 0, hs[h]], wT[:, x, h], state[:, h], start=True, stop=True)
                        ins.then_inc(sem("scan_done"), 1)
                    if hl == 17 + 2 * n:
                        if n == 0:
                            pe.wait_ge(sem("uw_ready"), dv(4, 4))
                        else:
                            pe.wait_ge(sem("scan_ready"), dv(SCAN, 2 * n))
                            pe.wait_ge(sem("o_ready"), dv(NCH, n))
                        for h in range(GH):
                            if n:
                                T.matmul(X[:, 1, hs[h]], qdT[:, x, h], state[:, h], start=True, stop=False)
                            ins = T.matmul(X[:, 1, hs[h]], qkT[:, x, h], us[:, x, h], start=n == 0, stop=True)
                        ins.then_inc(sem("o_done"), 1)
                        if n < NCH - 1:
                            for h in range(GH):
                                ins = T.matmul(X[:, 0, hs[h]], ke[rows, x, h], us[rows, x, h], start=True, stop=True)
                            ins.then_inc(sem("scan_done"), 1)
                if hl == 29:
                    pe.wait_ge(sem("o_gated"), dv(1, 1))
                    channels_first(lambda x, a: otok[:, x, a], 0).then_inc(sem("oT_tr"), 1)

            for hl in range(ph.hn):
                model_half(ph, hl, 0, r1)
                if hl == 2:
                    z_transposed(NJ - 1)
                if hl == 1:
                    pe.wait_ge(sem("conv_done"), NJ + 1)
                    for kt in range(KT):
                        ins = T.matmul(X[:, 0, 0:TOK], ones_mean[:], y[:, kt], start=kt == 0, stop=kt == KT - 1)
                    ins.then_inc(sem("mean_done"), 1)
                if 4 <= hl < 4 + NJ:
                    q = hl - 4
                    pe.wait_ge(sem("ln_sq"), q + 1)
                    for x in range(TT):
                        for a in range(CT):
                            ins = T.matmul(X[:, x, 0:1], lnsq[:, a, x * P:(x + 1) * P], ones_mean[:, 0:1],
                                           start=q == 0 and a == 0, stop=q == NJ - 1 and a == CT - 1)
                    ins.then_inc(sem("ln_sq_used"), 1)
                if hl == 10:
                    pe.wait_ge(sem("rdiag_ready"), 1)
                    for x in range(TT):
                        ins = T.matmul(X[:, 1, x * P:(x + 1) * P], ones_mean[:], rdiag[:, x], start=True, stop=True)
                    ins.then_inc(sem("rstd_rows"), 1)
                own(ph, hl, 0)
            with pe.Fori(1, NJ) as i:
                dv = lambda per, n: i * per + (n - per)
                for hl in range(ph.hn):
                    model_half(ph, hl, i, r1)
                    if hl == 9:
                        pe.wait_ge(sem("inv_ready"), dv(LEVELS, 2))
                    if hl == 16:
                        pe.wait_ge(sem("uw_ready"), dv(4, 4))
                    if hl == 25:
                        pe.wait_ge(sem("o_ready"), dv(NCH, NCH))
                    own(ph, hl, i)
                    delta(hl, dv, i)

            ph = PH["YB"]
            dv = lambda per, n: (NJ - 1) * per + n
            for hl in range(ph.hn):
                if hl < 8:
                    pe.wait_ge(sem(f"operand_landed{hl // 2}"), 32)
                model_half(ph, hl, 0, r1)
                delta(hl, dv)
            def merged_tr(tile, j, base):
                pe.wait_ge(sem("m_ready"), base + j + 1)
                channels_first(cols(tile), 0).then_inc(sem("m_tr"), 1)

            ph = PH["YA"]
            for hl in range(ph.hn):
                if hl < 8:
                    pe.wait_ge(sem(f"operand_landed{hl // 2}"), 64)
                model_half(ph, hl, 0, r1)
                if at_block(hl, 1) is not None:
                    merged_tr(mtmp, at_block(hl, 1), OP_M)

            pe.wait_ge(sem("p_landed"), 16)
            for a in range(PLE // P):
                for x in range(TT):
                    ins = T.transpose(X[:, 2, a * TOK + x * P:a * TOK + (x + 1) * P], ptok[:, x, a * P:(a + 1) * P], ident[:])
            ins.then_inc(sem("p_tr"), 1)
            ph = PH["MIX"]
            for hl in range(ph.hn):
                if hl < 8:
                    pe.wait_ge(sem("m_lo"), 2 * OP_M + hl + 1)
                model_half(ph, hl, 0, r2)
                if hl == 1:
                    merged_tr(mtmp, NJ - 1, OP_M)
            ph = PH["PLEP"]
            pe.wait_ge(sem("p_lo"), 1)
            for hl in range(ph.hn):
                n, kt = divmod(hl, 2)
                pe.wait_ge(lo_ready, LO_CREDIT + ph.h0 + hl + 1)
                for s in range(2):
                    if kt == 0:
                        pe.wait_ge(acc_free[s], 2 * ((ph.b0 + 2 * n + s) // 2))
                    for x in range(TT):
                        for m, (a, w) in enumerate(((pTh, w_hi), (pTh, w_lo), (pTl, w_hi))):
                            ins = T.matmul(acc[:, s, x], a[:, kt, x * P:(x + 1) * P], w[:, (ph.h0 + hl) % HL, s * NB:(s + 1) * NB],
                                           start=kt == 0 and m == 0, stop=kt == 1 and m == 2)
                ins.then_inc(w_used, 1)

            def operand_tr(tile, base, j):
                pe.wait_ge(sem("op_ready"), base - OP_X1 + j + 1)
                if j >= 2:
                    pe.wait_ge(sem("op_lo"), 2 * (base + j - 1))
                channels_first(lambda x, a: tile[:, x, j * NB + a * P:j * NB + (a + 1) * P], 2 * (j % 2)).then_inc(sem("op_tr"), 1)

            def operand_half(ph, hl, tile, base, ops):
                pe.wait_ge(sem("op_lo"), 2 * base + hl + 1)
                model_half(ph, hl, 0, ops)
                if hl in (1, 2):
                    operand_tr(tile, base, hl + 1)

            for j in range(2):
                operand_tr(mix, OP_X1, j)
            ph = PH["PLEG"]
            for hl in range(ph.hn):
                if hl < 8:
                    operand_half(ph, hl, mix, OP_X1, r1)
                else:
                    model_half(ph, hl, 0, r1)
            for j in range(2):
                operand_tr(mix, OP_H2, j)

            ph = PH["QA"]
            for hl in range(ph.hn):
                operand_half(ph, hl, mix, OP_H2, r2)
            narrow(PH["KR"], r2, ROPE, 3)
            ph = PH["KVA"]
            for hl in range(ph.hn):
                model_half(ph, hl, 0, r2)
                if hl == 0:
                    pe.wait_ge(sem("kr_ready"), 1)
                    narrow_tr(krT, ROPE, 3).then_inc(sem("kr_tr"), 1)
                if hl == 2:
                    pe.wait_ge(sem("kr_ready"), 2)
                    for x in range(TT):
                        ins = T.transpose(X[:, 3, x * P:(x + 1) * P], qr[:, x, 0:2].rearrange("p a n -> p (a n)"), ident[:])
                    ins.then_inc(sem("kr_tr"), 1)
                if hl == 3:
                    pe.wait_ge(sem("op_ready"), OP_LAT - OP_X1 + 1)
                    channels_first(cols(qa_t), 0).then_inc(sem("op_tr"), 1)
            pe.wait_ge(sem("op_ready"), OP_LAT - OP_X1 + 2)
            pe.wait_ge(sem("krT_ready"), 1)
            channels_first(cols(kva_t), 2).then_inc(sem("op_tr"), 1)
            pe.wait_ge(sem("op_lo"), 2 * OP_LAT + 4)

            ph = PH["FC"]
            V0 = [slice(h % 2 * KVH + NOPE, (h % 2 + 1) * KVH) for h in range(GH)]
            with pe.Fori(0, ph.iters) as i:
                for hl in range(ph.hn):
                    if hl < 8:
                        bl, q = divmod(hl, 2)
                        wide = bl != 1
                        gemm(ph, hl, i, r1, (0 if bl < 2 else CT) + 2 * q, bl, q == 0, q == 1,
                             n=NB if wide else GH * QH - NB, off=0 if wide else 2 * NB - GH * QH)
                    else:
                        model_half(ph, hl, i, r2, 8, 4)
                    if hl == 5:
                        pe.wait_ge(acc_free[0], freed(ph, 0, i))
                        pe.wait_ge(acc_free[1], freed(ph, 1, i))
                        for h in range(GH):
                            for x in range(TT):
                                ins = T.transpose(X[:, h // 2, h % 2 * TOK + x * P:h % 2 * TOK + (x + 1) * P], qst[:, x, h * QH:h * QH + NOPE], ident[:])
                        ins.then_inc(sem("qn_tr"), 1)
                    if hl == 7:
                        pe.wait_ge(sem("qr_ready"), i + 1)
                        for a in range(GH // 2):
                            for x in range(TT):
                                ins = T.transpose(X[:, 2, a * TOK + x * P:a * TOK + (x + 1) * P], qr[:, x, 2 * a:2 * a + 2].rearrange("p a n -> p (a n)"), ident[:])
                        ins.then_inc(sem("qr_tr"), 1)
                    if hl == 9:
                        pe.wait_ge(acc_free[0], freed(ph, 2, i))
                        pe.wait_ge(acc_free[1], freed(ph, 3, i))
                        pe.wait_ge(sem("qTn_ready"), i * 2 + 2)
                        for h in range(GH):
                            for x in range(TT):
                                ins = T.transpose(X[:, h // 2, h % 2 * TOK + x * P:h % 2 * TOK + (x + 1) * P],
                                                  kvst[:, x, h // 2, h % 2 * KVH:h % 2 * KVH + NOPE], ident[:])
                        ins.then_inc(sem("kn_tr"), 1)
                    if hl == 11:
                        pe.wait_ge(sem("kTn_ready"), i * 2 + 2)
                        pe.wait_ge(sem("qrT_ready"), i + 1)
                        for h in range(GH):
                            half = slice(h % 2 * ROPE, (h % 2 + 1) * ROPE)
                            for x, keys, at in ((0, P, slice(0, P)), (1, TOK, slice(P, SCORES))):
                                T.matmul(X[:, h, at], qTn[:, h, x * P:(x + 1) * P], kTn[:, h, 0:keys], start=True, stop=False)
                                ins = T.matmul(X[:, h, at], qrT[half, h // 2, x * P:(x + 1) * P], krT[half, 0:keys], start=False, stop=True)
                        ins.then_inc(sem("sc_done"), 1)
                    if hl == 16:
                        pe.wait_ge(sem("exp_ready"), i + 1)
                        for h in range(GH):
                            for n in range(3):
                                ins = T.transpose(X[:, h, n * P:(n + 1) * P], sc[:, h, n * P:(n + 1) * P], ident[:])
                        ins.then_inc(sem("pT_tr"), 1)
                    if hl == 18:
                        pe.wait_ge(sem("pT_ready0"), i + 1)
                        pe.wait_ge(sem("pT_ready1"), i + 1)
                        for h in range(GH):
                            o = slice(h * VD, (h + 1) * VD)
                            T.matmul(X[:, 0, o], pT[:, h, 0:P], kvst[:, 0, h // 2, V0[h]], start=True, stop=True)
                            T.matmul(X[:, 1, o], pT[:, h, P:2 * P], kvst[:, 0, h // 2, V0[h]], start=True, stop=False)
                            ins = T.matmul(X[:, 1, o], pT[:, h, 2 * P:3 * P], kvst[:, 1, h // 2, V0[h]], start=False, stop=True)
                        ins.then_inc(sem("pv_done"), 1)
                    if hl == 25:
                        pe.wait_ge(acc_free[1], freed(ph, 5, i))
                        channels_first(cols(cg), 0).then_inc(sem("u2_tr"), 1)
                    if hl == 39:
                        pe.wait_ge(acc_free[1], freed(ph, 7, i))
                        channels_first(cols(zs), 2).then_inc(sem("bz_tr"), 1)

            ph = PH["FG"]
            with pe.Fori(0, ph.iters) as i:
                for hl in range(ph.hn):
                    model_half(ph, hl, i, r2)

            def heads_tr(hl):
                j = at_block(hl, 2)
                if j is not None:
                    merged_tr(oin[:, j % 2], j, OP_ATTN)

            ph = PH["FZ"]
            for hl in range(ph.hn):
                model_half(ph, hl, 0, r2)
                heads_tr(hl)

            ph = PH["YM"]
            for hl in range(ph.hn):
                if hl < 8:
                    pe.wait_ge(sem("m_lo"), 2 * OP_ATTN + hl + 1)
                model_half(ph, hl, 0, r1)
                if hl < 4:
                    heads_tr(PH["FZ"].hn + hl)
            ph = PH["YC"]
            for hl in range(ph.hn):
                if hl < 8:
                    pe.wait_ge(sem(f"operand_landed{hl // 2}"), 96)
                model_half(ph, hl, 0, r2)
                if at_block(hl, 1) is not None:
                    merged_tr(thz, at_block(hl, 1), OP_Y)
            ph = PH["OUT"]
            for hl in range(ph.hn):
                if hl < 8:
                    pe.wait_ge(sem("m_lo"), 2 * OP_Y + hl + 1)
                model_half(ph, hl, 0, r1)
                if hl == 1:
                    merged_tr(thz, NJ - 1, OP_Y)


_INS = ["x", "p", "g_pre", "w_in", "b_gate", "w_conv_qkv", "a_log", "dt_bias", "g_dn_out", "w_dw", "b_dw", "ln_g", "ln_b",
        "w_br_a", "w_br_b", "w_out", "g_post", "w_ple_gate", "w_ple_proj", "g_ple", "positions_2", "pre_norm_g_2", "w_in_2",
        "q_a_norm_g_2", "w_q_b_2", "kv_a_norm_g_2", "w_kv_b_2", "conv_w_2", "w_o_mla_2", "w_o_conv_2", "w_out_2", "post_norm_g_2"]


def kernel(**inputs):
    import numpy as np
    import concourse.bacc as bacc
    from concourse.bass_utils import run_bass_kernel_spmd as run

    nc = bacc.Bacc("TRN2", target_bir_lowering=False, num_devices=1)
    arrays = {name: np.ascontiguousarray(inputs[name]) for name in _INS}
    arrays["inv_freq"] = (ROPE_THETA ** (-np.arange(0, ROPE, 2, dtype=np.float32) / ROPE)).astype(np.float32)[None]
    t = {name: nc.dram_tensor(f"in_{name}", a.shape, mybir.dt.from_np(a.dtype), kind="ExternalInput").ap() for name, a in arrays.items()}
    out = nc.dram_tensor("out", (1, TOK, D), F32, kind="ExternalOutput").ap()
    build_layer(nc, t, out)
    r = run(nc, [{f"in_{name}": a for name, a in arrays.items()}], core_ids=[0])
    return r.results[0]["out"]
```
